# Optimizing a Trainium2 kernel written in Bass

```python
import jax, jax.numpy as jnp
from jax import lax
import numpy as np

D_MODEL = 2048
BATCH = 1
SEQ = 512
DEPTH = 1

HEAD_DIM = 64
D_RWKV = 1024
D_FOX = D_MODEL - D_RWKV
H_RWKV = D_RWKV // HEAD_DIM
H_FOX = D_FOX // HEAD_DIM
D_DECAY_LORA = 64
D_AAA_LORA = 64
D_GATE_LORA = 160
D_FF = 4 * D_MODEL
D_PLE = 256
Q_BLOCK = 128
NORM_EPS = 1e-6
GN_EPS = 64e-5

N_SHIFT = 3 * D_RWKV + D_DECAY_LORA + D_AAA_LORA + D_GATE_LORA
D_IN = N_SHIFT + 3 * D_FOX + H_FOX
RWKV_SPLITS = [D_RWKV, 2 * D_RWKV, 3 * D_RWKV, 3 * D_RWKV + D_DECAY_LORA, 3 * D_RWKV + D_DECAY_LORA + D_AAA_LORA]
FOX_SPLITS = [D_FOX, 2 * D_FOX, 3 * D_FOX]

kernel_name = "hybrid_rwkv7_fox_parallel_heads"

def rmsnorm(x, g):
    xf = x.astype(jnp.float32)
    y = xf * lax.rsqrt(jnp.mean(xf * xf, axis=-1, keepdims=True) + NORM_EPS)
    return (y * g.astype(jnp.float32)).astype(x.dtype)

def rwkv7_mixer(z, w0, w2, a0, a2, g2, k_k, k_a, r_k, gn_w, gn_b):
    B, S, _ = z.shape
    f32 = jnp.float32
    r, k, v, xw, xa, xg = jnp.split(z, RWKV_SPLITS, axis=-1)
    w_log = -jax.nn.softplus(-(w0 + jnp.tanh(xw) @ w2)) - 0.5
    decay = jnp.exp(-jnp.exp(w_log.astype(f32)))
    a = jax.nn.sigmoid(a0 + xa @ a2)
    g = jax.nn.sigmoid(xg) @ g2

    def heads(t):
        return t.reshape(B, S, H_RWKV, HEAD_DIM).astype(f32)

    kk = heads(k * k_k)
    kk = kk / jnp.maximum(jnp.sqrt(jnp.sum(kk * kk, axis=-1, keepdims=True)), 1e-12)
    k = k * (1.0 + (a - 1.0) * k_a)
    r_h, k_h, v_h, w_h, a_h = heads(r), heads(k), heads(v), heads(decay), heads(a)

    def step(state, inp):
        r_t, w_t, k_t, v_t, kk_t, a_t = inp
        sa = jnp.einsum('bhvk,bhk->bhv', state, -kk_t)
        state = (state * w_t[:, :, None, :]
                 + sa[..., None] * (kk_t * a_t)[:, :, None, :]
                 + v_t[..., None] * k_t[:, :, None, :])
        y_t = jnp.einsum('bhvk,bhk->bhv', state, r_t)
        return state, y_t

    xs = tuple(jnp.moveaxis(t, 1, 0) for t in (r_h, w_h, k_h, v_h, kk, a_h))
    state0 = jnp.zeros((B, H_RWKV, HEAD_DIM, HEAD_DIM), f32)
    _, y = lax.scan(step, state0, xs)
    y = jnp.moveaxis(y, 0, 1)
    mu = jnp.mean(y, axis=-1, keepdims=True)
    var = jnp.mean(jnp.square(y - mu), axis=-1, keepdims=True)
    y = ((y - mu) * lax.rsqrt(var + GN_EPS)).reshape(B, S, D_RWKV)
    y = y * gn_w.astype(f32) + gn_b.astype(f32)
    bonus = jnp.sum(r_h * k_h * r_k.astype(f32), axis=-1, keepdims=True) * v_h
    y = y + bonus.reshape(B, S, D_RWKV)
    return (y * g.astype(f32)).astype(z.dtype)

def fox_mixer(q, k, v, f_logit, q_norm, k_norm):
    B, S, _ = q.shape
    nb = S // Q_BLOCK
    f32 = jnp.float32

    def heads(t):
        return t.reshape(B, S, H_FOX, HEAD_DIM).transpose(0, 2, 1, 3)

    qh = rmsnorm(heads(q), q_norm)
    kh = rmsnorm(heads(k), k_norm)
    vh = heads(v)
    log_f = jax.nn.log_sigmoid(f_logit.astype(f32))
    c = jnp.cumsum(log_f, axis=1).transpose(0, 2, 1)
    scale = HEAD_DIM ** -0.5
    qb = qh.reshape(B, H_FOX, nb, Q_BLOCK, HEAD_DIM).transpose(2, 0, 1, 3, 4)
    cb = c.reshape(B, H_FOX, nb, Q_BLOCK).transpose(2, 0, 1, 3)
    pos_q = jnp.arange(S, dtype=jnp.int32).reshape(nb, Q_BLOCK)
    pos_k = jnp.arange(S, dtype=jnp.int32)

    def block(args):
        q_blk, c_blk, pq = args
        logits = jnp.einsum('bhqd,bhkd->bhqk', q_blk, kh).astype(f32) * scale
        logits = logits + (c_blk[..., None] - c[:, :, None, :])
        logits = jnp.where(pq[:, None] >= pos_k[None, :], logits, -jnp.inf)
        probs = jax.nn.softmax(logits, axis=-1)
        return jnp.einsum('bhqk,bhkd->bhqd', probs.astype(vh.dtype), vh)

    o = lax.map(block, (qb, cb, pos_q))
    return o.transpose(1, 0, 3, 2, 4).reshape(B, S, D_FOX)

def setup_inputs(seed: int = 0) -> dict:
    key = jax.random.key(seed)
    ks = jax.random.split(key, 32)
    f32 = jnp.float32

    def nrm(k, shape, scale):
        return jax.random.normal(k, shape, f32) * scale

    L = DEPTH
    return {
        "x": nrm(ks[0], (BATCH, SEQ, D_MODEL), 1.0),
        "p": nrm(ks[1], (DEPTH, BATCH, SEQ, D_PLE), 1.0),
        "norm_mix": 1.0 + nrm(ks[2], (L, D_MODEL), 0.02),
        "w_in": nrm(ks[3], (L, D_MODEL, D_IN), D_MODEL ** -0.5),
        "mu_shift": 0.5 + nrm(ks[4], (L, N_SHIFT), 0.1),
        "w0": nrm(ks[5], (L, D_RWKV), 0.5),
        "w2": nrm(ks[6], (L, D_DECAY_LORA, D_RWKV), D_DECAY_LORA ** -0.5),
        "a0": nrm(ks[7], (L, D_RWKV), 0.1),
        "a2": nrm(ks[8], (L, D_AAA_LORA, D_RWKV), D_AAA_LORA ** -0.5),
        "g2": nrm(ks[9], (L, D_GATE_LORA, D_RWKV), D_GATE_LORA ** -0.5),
        "k_k": 0.85 + nrm(ks[10], (L, D_RWKV), 0.02),
        "k_a": 1.0 + nrm(ks[11], (L, D_RWKV), 0.02),
        "r_k": nrm(ks[12], (L, H_RWKV, HEAD_DIM), 0.1),
        "gn_w": 1.0 + nrm(ks[13], (L, D_RWKV), 0.02),
        "gn_b": nrm(ks[14], (L, D_RWKV), 0.02),
        "b_f": 3.0 + nrm(ks[15], (L, H_FOX), 1.0),
        "q_norm": 1.0 + nrm(ks[16], (L, HEAD_DIM), 0.02),
        "k_norm": 1.0 + nrm(ks[17], (L, HEAD_DIM), 0.02),
        "w_out": nrm(ks[18], (L, D_MODEL, D_MODEL), D_MODEL ** -0.5),
        "norm_mlp": 1.0 + nrm(ks[19], (L, D_MODEL), 0.02),
        "w_ff1": nrm(ks[20], (L, D_MODEL, D_FF), D_MODEL ** -0.5),
        "w_ff2": nrm(ks[21], (L, D_FF, D_MODEL), D_FF ** -0.5),
        "norm_ple": 1.0 + nrm(ks[22], (L, D_MODEL), 0.02),
        "w_ple_gate": nrm(ks[23], (L, D_MODEL, D_MODEL), D_MODEL ** -0.5),
        "w_ple_proj": nrm(ks[24], (L, D_PLE, D_MODEL), D_PLE ** -0.5),
        "norm_final": 1.0 + nrm(ks[25], (D_MODEL,), 0.02),
    }

def reference(x, p, norm_mix, w_in, mu_shift, w0, w2, a0, a2, g2, k_k, k_a, r_k, gn_w, gn_b,
              b_f, q_norm, k_norm, w_out, norm_mlp, w_ff1, w_ff2, norm_ple, w_ple_gate,
              w_ple_proj, norm_final):
    h = x
    for i in range(DEPTH):
        u = rmsnorm(h, norm_mix[i])
        z = u @ w_in[i]
        z_rw, z_fox = z[..., :N_SHIFT], z[..., N_SHIFT:]
        z_prev = jnp.pad(z_rw, ((0, 0), (1, 0), (0, 0)))[:, :-1]
        z_rw = z_rw + (z_prev - z_rw) * mu_shift[i]
        y_rw = rwkv7_mixer(z_rw, w0[i], w2[i], a0[i], a2[i], g2[i], k_k[i], k_a[i], r_k[i],
                           gn_w[i], gn_b[i])
        fq, fk, fv, ff = jnp.split(z_fox, FOX_SPLITS, axis=-1)
        y_fox = fox_mixer(fq, fk, fv, ff + b_f[i], q_norm[i], k_norm[i])
        h = h + jnp.concatenate([y_rw, y_fox], axis=-1) @ w_out[i]
        u = rmsnorm(h, norm_mlp[i])
        h = h + jnp.square(jax.nn.relu(u @ w_ff1[i])) @ w_ff2[i]
        gate = jax.nn.sigmoid(rmsnorm(h, norm_ple[i]) @ w_ple_gate[i])
        h = h + gate * (p[i] @ w_ple_proj[i])
    return rmsnorm(h, norm_final)


_drawn_inputs = setup_inputs


def setup_inputs(seed=0):
    import zlib

    import numpy as np

    out = dict(_drawn_inputs(seed))
    spreads = {}
    factors = {'norm_mix': 3.358,
     'a0': 2.994,
     'k_k': 200.0,
     'k_a': 5.58,
     'gn_w': 58.112,
     'gn_b': 62.768,
     'q_norm': 32.492,
     'k_norm': 37.654,
     'norm_mlp': 11.604,
     'norm_ple': 200.0,
     'norm_final': 20.369,
     'p': 8.0,
     'w_ple_gate': 8.0,
     'w_ple_proj': 8.0}
    for name, (base, spread) in spreads.items():
        noise = np.random.default_rng([zlib.crc32(name.encode()), seed]).standard_normal(out[name].shape)
        drawn = base * np.exp(spread * noise) if base else spread * noise
        out[name] = __import__('jax').numpy.asarray(drawn.astype(out[name].dtype))
    for name, factor in factors.items():
        out[name] = (out[name] * factor).astype(out[name].dtype)
    return out
```

```python
import numpy as np
from contextlib import ExitStack

import concourse.bass as bass
from concourse import mybir

F32 = mybir.dt.float32
F32R = mybir.dt.float32r
ALU = mybir.AluOpType
ACT = mybir.ActivationFunctionType
AX = mybir.AxisListType

P = 128
D = 2048
T = 512
KT = D // P
HD = 64
DR = 1024
NPAIR = DR // P
FF = 4 * D
FG = FF // D
DPLE = 256
C = 64
NC = T // C
N_SHIFT = 3 * DR + 64 + 64 + 160
EPS = 1e-6
GN_EPS = 64e-5
UK = KT // 2
NEG = -1e30

Z_LORA, Z_K, Z_R, Z_V, Z_FQ, Z_FK, Z_FV = 0, 2, 10, 18, 26, 34, 42
Z_TILES = 50

C_ID, C_ONE, C_MASK, C_LVL = 0, 128, 256, 384
C_BLK, C_HEAD, C_HEADT, C_CAUS = 768, 896, 898, 1026
C_EYE2, C_RESET = 1154, 1218
C_COLS = C_RESET + T


def constants():
    c = np.zeros((P, C_COLS), np.float32)
    p = np.arange(P)
    j = p % C
    t = np.arange(C)
    c[:, C_ID:C_ID + P] = np.eye(P)
    c[:, C_ONE:C_ONE + P] = 1.0
    c[:, C_MASK:C_MASK + C] = t[None, :] > j[:, None]
    c[:, C_MASK + C:C_MASK + 2 * C] = t[None, :] >= j[:, None]
    for n in range(6):
        b = 1 << n
        c[:, C_LVL + n * C:C_LVL + (n + 1) * C] = (
            (j[:, None] // (2 * b) == t[None, :] // (2 * b)) & (j[:, None] % (2 * b) < b) & (t[None, :] % (2 * b) >= b))
    c[:, C_BLK:C_BLK + P] = (p[:, None] // HD == p[None, :] // HD) / HD
    c[:, C_HEAD:C_HEAD + 2] = p[:, None] // HD == np.arange(2)[None, :]
    c[0:2, C_HEADT:C_HEADT + P] = np.arange(2)[:, None] == p[None, :] // HD
    c[:, C_EYE2:C_EYE2 + C] = t[None, :] == j[:, None]
    c[:, C_CAUS:C_CAUS + P] = np.where(p[:, None] >= p[None, :], 0.0, NEG)
    c[:, C_RESET:C_RESET + T] = np.arange(T)[None, :] % C != 0
    return c




def build(nc, x, p, norm_mix, w_in, mu_shift, w0, w2, a0, a2, g2, k_k, k_a, r_k, gn_w, gn_b, b_f, q_norm,
          k_norm, w_out, norm_mlp, w_ff1, w_ff2, norm_ple, w_ple_gate, w_ple_proj, norm_final, consts, out):
    ctx = ExitStack()
    sems = {}

    def sg(name):
        if name not in sems:
            sems[name] = ctx.enter_context(nc.semaphore(name))
        return sems[name]

    def sb(name, shape, where, dt=F32):
        n = 4
        for s in shape[1:]:
            n *= s
        t = nc.alloc_sbuf_tensor_at(name, shape, dt, offset=where[0])
        where[0] += (n + 63) // 64 * 64
        return t

    top = [(nc.sbuf_base + 63) // 64 * 64]
    a_hi = sb("a_hi", [P, KT, T], top, F32R)
    a_lo = sb("a_lo", [P, KT, T], top, F32R)
    arena = top[0]
    b_hi = sb("b_hi", [P, KT, T], top, F32R)
    b_lo = sb("b_lo", [P, KT, T], top, F32R)
    arena_h = top[0]
    h = sb("h", [P, KT, T], top)
    h_end = top[0]
    w_raw = sb("w_raw", [P, 2, UK, P], top)
    w_hi = sb("w_hi", [P, 2, UK, P], top, F32R)
    w_lo = sb("w_lo", [P, 2, UK, P], top, F32R)
    rstd = sb("rstd", [P, T], top)
    sumsq = sb("sumsq", [P, T], top)
    sq = sb("sq", [P, 2, T], top)
    ev = sb("ev", [P, 2, T], top)
    tmp = sb("tmp", [P, T], top)
    par = sb("par", [P, 160], top)
    cst = sb("cst", [P, C_RESET], top)
    assert top[0] <= nc.sbuf_usable_end, (top[0], nc.sbuf_usable_end)

    def const(c, n, parts=slice(0, P)):
        return cst[parts, c:c + n]

    ident, ones, eye2 = const(C_ID, P), const(C_ONE, P), const(C_EYE2, C)
    head_of, of_head = const(C_HEAD, 2), const(C_HEADT, P, slice(0, 2))

    acc = [nc.alloc_psum_tensor(f"acc{i}", [P, T], F32) for i in range(2)]
    bank = [nc.alloc_psum_tensor(f"bank{i}", [P, T], F32) for i in range(6)]

    def dram(name, shape):
        return nc.dram_tensor(name, shape, F32, kind="Internal").ap()

    z_d = dram("z_d", (Z_TILES, P, T))
    zo_d = dram("zo_d", (48, T))
    h_d = dram("h_d", (KT, P, T))
    ab_d = dram("ab_d", (NC, P, NPAIR, 4, C))
    v_d = dram("v_d", (NC, P, NPAIR, C))
    bonus_d = dram("bonus_d", (NPAIR, P, T))
    y_d = dram("y_d", (NC, P, NPAIR, C))
    c_d = dram("c_d", (2 * NPAIR, T))
    h_v = h_d.rearrange("k p t -> p k t")

    rows = [("norm_mix", norm_mix, 16), ("norm_mlp", norm_mlp, 16), ("norm_ple", norm_ple, 16),
            ("norm_final", norm_final, 16), ("w0", w0, 8), ("a0", a0, 8), ("k_k", k_k, 8), ("k_a", k_a, 8),
            ("r_k", r_k, 8), ("gn_w", gn_w, 8), ("gn_b", gn_b, 8)]
    col = {"q_norm": 120, "k_norm": 121, "mu": P}
    for n, row in enumerate(rows):
        col[row[0]] = sum(r[2] for r in rows[:n])
    N_PAR = len(rows) + 4 + 2

    def pc(name, i=0):
        return par[:, bass.ds(col[name] + i, 1)]

    def flat(a):
        if len(a.shape) == 3:
            a = a.rearrange("a h d -> a (h d)")
        return a.rearrange("(a n) -> a n", a=1) if len(a.shape) == 1 else a

    def w_view(w):
        return w.rearrange("a (k p) n -> p (a k) n", p=P)

    w_in_v, w_out_v, ff1_v, ff2_v, gate_v = (w_view(w) for w in (w_in, w_out, w_ff1, w_ff2, w_ple_gate))
    ple_v = w_view(w_ple_proj)

    at = [arena]
    xin = sb("xin", [P, 2, T // P, P], at)
    prow = sb("prow", [P, 2, P], at)
    at = [arena]
    kin = sb("kin", [P, T + 1], at)
    rin = sb("rin", [P, T + 1], at)
    vin = sb("vin", [P, T + 1], at)
    xin_l = sb("xin_l", [P, T + 1], at)
    xin_g = sb("xin_g", [32, T + 1], at)
    reset = sb("reset", [P, T], at)
    wa_in = sb("wa_in", [P, P], at)
    dif = sb("dif", [P, T], at)
    ks = sb("ks", [P, T], at)
    rs = sb("rs", [P, T], at)
    vs = sb("vs", [P, T], at)
    lw = sb("lw", [P, T], at)
    cum = sb("cum", [P, T], at)
    cex = sb("cex", [P, T], at)
    av = sb("av", [P, T], at)
    e_in = sb("e_in", [P, T], at)
    e_ex = sb("e_ex", [P, T], at)
    e_no = sb("e_no", [P, T], at)
    kkr = sb("kkr", [P, T], at)
    kk = sb("kk", [P, T], at)
    km = sb("km", [P, T], at)
    t1 = sb("t1", [P, T], at)
    t2 = sb("t2", [P, T], at)
    ab = sb("ab", [P, NC, 4, C], at)
    bon = sb("bon", [P, T], at)
    assert at[0] <= h_end
    at = [arena]
    abd = sb("abd", [P, NPAIR, 2, C], at)
    bbd = sb("bbd", [P, NPAIR, 2, C], at)
    kbd = sb("kbd", [P, NPAIR, 2, C], at)
    vbd = sb("vbd", [P, NPAIR, 2, C], at)
    ars = sb("ars", [P, NPAIR, 2, C], at)
    gb = sb("gb", [P, NPAIR, 2, C], at)
    gk = sb("gk", [P, NPAIR, 2, C], at)
    mbd = sb("mbd", [P, NPAIR, 2, C], at)
    nbd = sb("nbd", [P, 2, NPAIR, 2, C], at)
    xs = sb("xs", [P, NPAIR, C], at)
    xt = sb("xt", [P, NPAIR, C], at)
    xbd = sb("xbd", [P, NPAIR, 2, C], at)
    pt = sb("pt", [P, NPAIR, C], at)
    ptbd = sb("ptbd", [P, NPAIR, 2, C], at)
    bt = sb("bt", [P, NPAIR, P], at)
    ktm = sb("ktm", [P, NPAIR, P], at)
    vt = sb("vt", [P, NPAIR, P], at)
    vst = sb("vst", [P, NPAIR, C], at)
    rr = sb("rr", [P, NPAIR, C], at)
    sa = sb("sa", [P, NPAIR, C], at)
    sabd = sb("sabd", [P, NPAIR, 2, C], at)
    st = sb("st", [P, NPAIR, C], at)
    stbd = sb("stbd", [P, NPAIR, 2, C], at)
    sn = sb("sn", [P, NPAIR, C], at)
    yo = sb("yo", [P, NPAIR, C], at)
    assert at[0] <= h_end, at[0] - h_end
    diagonals = [t[:, :, :, :] for t in (abd, bbd, kbd, vbd, mbd, xbd, ptbd, sabd, stbd)] + [nbd[:, 0, :, :, :], nbd[:, 1, :, :, :], st[:, :, :]]
    N_CLEAR = len(diagonals)
    keep = [h_end - 3 * 2048 - 256 - 2048]
    tx = sb("tx", [P, T], keep)
    sga = sb("sga", [P, T], keep)
    sgb = sb("sgb", [32, T], keep)
    ec = sb("ec", [P, NPAIR, NC], keep)
    assert keep[0] <= h_end and at[0] <= h_end - 3 * 2048 - 256 - 2048, (at[0], h_end)
    at = [arena]
    yt = sb("yt", [P, T], at)
    yb = sb("yb", [P, T], at)
    g2a = sb("g2a", [P, P], at)
    g2b = sb("g2b", [32, P], at)
    yc = sb("yc", [P, T], at)
    yn = sb("yn", [P, T], at)
    fin = sb("fin", [16, T], at)
    f1 = sb("f1", [16, T], at)
    f2 = sb("f2", [16, T], at)
    f3 = sb("f3", [16, T], at)
    bf = sb("bf", [16, 1], at)
    cq = sb("cq", [P, T // P, 16], at)
    qin = sb("qin", [P, T], at)
    k_in = sb("k_in", [P, T], at)
    v_in = sb("v_in", [P, T], at)
    qh = sb("qh", [P, T], at)
    kh = sb("kh", [P, T], at)
    vtm = sb("vtm", [P, T // P, P], at)
    ncb = sb("ncb", [P, 2, T], at)
    lg = sb("lg", [P, T // P, T], at)
    pr = sb("pr", [P, T // P, T], at)
    prt = sb("prt", [P, T // P, T], at)
    mx = sb("mx", [P, 4], at)
    nmx = sb("nmx", [P, 4], at)
    rsum = sb("rsum", [P, 4], at)
    rinv = sb("rinv", [P, 4], at)
    og = sb("og", [P, T], at)
    assert at[0] <= arena_h
    at = [(nc.sbuf_base + 63) // 64 * 64]
    p_in = sb("p_in", [P, T // P, DPLE], at)
    p_hi = sb("p_hi", [P, 2, T], at, F32R)
    p_lo = sb("p_lo", [P, 2, T], at, F32R)
    pw = sb("pw", [P, 2, 2, P], at)
    pw_hi = sb("pw_hi", [P, 2, 2, P], at, F32R)
    pw_lo = sb("pw_lo", [P, 2, 2, P], at, F32R)
    p_t = sb("p_t", [P, 2, T], at)
    gt = sb("gt", [P, 2, T], at)
    hn = sb("hn", [P, 2, T], at)
    ot = sb("ot", [P, 2, T // P, P], at)
    hs = sb("hs", [P, 8], top)
    hr = sb("hr", [P, 8], top)
    hrt = sb("hrt", [2, T], top)
    qs = sb("qs", [P, 1], top)
    assert top[0] <= nc.sbuf_usable_end, (top[0], nc.sbuf_usable_end)

    ZT = [(3 * DR, 2), (DR, 8), (0, 8), (2 * DR, 8), (N_SHIFT, 24)]
    Z_ODD = 2
    M_OUT = Z_TILES
    M_FF = M_OUT + KT
    M_GATE = M_FF + FG * 2 * KT
    M_END = M_GATE + KT


    with nc.Block() as block:

        @block.sync
        def _(sp):
            def unit(slot, src, n):
                sp.wait_ge(sg("w_split"), n + 1)
                sp.dma_start(w_raw[:, slot, :, :], src).then_inc(sg(f"w_landed{slot}"), 16)

            def stream(view, row, column, m, tiles, outer=0):
                with sp.Fori(0, tiles // 2) as i:
                    for b in range(2):
                        for s in range(2):
                            unit(s, view[:, row + s * UK:row + (s + 1) * UK, bass.ds(i * (2 * P) + (column + b * P), P)],
                                 i * 4 + outer + Z_ODD + 2 * m + 2 * b + s)

            sp.dma_start(cst[:, :], consts[:, 0:C_RESET]).then_inc(sg("constants_landed"), 16)
            sp.wait_ge(sg("rows_cleared"), 1)
            for name, a, n in rows:
                sp.dma_start(prow[col[name]:col[name] + n, 0, :],
                             flat(a).rearrange("a (n q) -> (a n) q", q=P)).then_inc(sg("parameters_landed"), 16)
            for k, a in enumerate((q_norm, k_norm)):
                for half in range(2):
                    sp.dma_start(prow[120 + k:121 + k, 0, half * HD:(half + 1) * HD], a).then_inc(sg("parameters_landed"), 16)
            sp.dma_start(prow[0:26, 1, :], mu_shift[0, 0:26 * P].rearrange("(n q) -> n q", q=P)).then_inc(sg("parameters_landed"), 16)
            sp.dma_start(prow[26:27, 1, 0:32], mu_shift[0:1, 26 * P:N_SHIFT]).then_inc(sg("parameters_landed"), 16)
            x_v = x.rearrange("a (b q) n -> q (a b) n", q=P)
            with sp.Fori(0, KT // 2) as i:
                for b in range(2):
                    sp.wait_ge(sg("x_transposed"), 2 * i + b + 1)
                    sp.dma_start(xin[:, b, :, :], x_v[:, :, bass.ds(i * (2 * P) + b * P, P)]).then_inc(sg(f"x_landed{b}"), 16)
            for s in range(2):
                r = slice(s * UK, (s + 1) * UK)
                sp.wait_ge(sg("w_split"), s + 1)
                sp.dma_start(w_raw[:, s, :, 0:32], w_in_v[:, r, N_SHIFT - 32:N_SHIFT]).then_inc(sg(f"w_landed{s}"), 16)
                sp.dma_start(w_raw[:, s, :, 32:48], w_in_v[:, r, N_SHIFT + 3 * DR:N_SHIFT + 3 * DR + 16]).then_inc(sg(f"w_landed{s}"), 16)
            m = 0
            for c0, n in ZT:
                stream(w_in_v, 0, c0, m, n)
                m += n
            for s in range(2):
                unit(s, w_out_v[:, s * UK:(s + 1) * UK, 0:P], Z_ODD + 2 * M_OUT + s)

            for b in range(2):
                sp.wait_ge(sg(f"ev_free{b}"), 16 * (Z_TILES // 2) + 16 * (b == 0))
            sp.wait_ge(sg("operand_split"), KT)
            sp.wait_ge(sg("h_stored"), 64)
            for dst, src in ((xin_l[:, 1:], z_d[0]), (rin[:, 1:], z_d[1]), (xin_g[:, 1:], zo_d[0:32, :]),
                             (reset[:, :], consts[:, C_RESET:C_RESET + T])):
                sp.dma_start(dst, src).then_inc(sg("lora_in_landed"), 16)
            sp.wait_ge(sg("lora_features_ready"), 3)
            with sp.Fori(0, NPAIR) as i:
                sp.wait_ge(sg("features_made"), i + 1)
                for dst, src in ((kin, Z_K), (rin, Z_R), (vin, Z_V)):
                    sp.dma_start(dst[:, 1:], z_d[bass.ds(i + src, 1), :, :].rearrange("a p t -> (a p) t")).then_inc(sg("features_landed"), 16)
                sp.dma_start(wa_in[0:64, :], w2[0, :, bass.ds(i * P, P)]).then_inc(sg("features_landed"), 16)
                sp.dma_start(wa_in[64:128, :], a2[0, :, bass.ds(i * P, P)]).then_inc(sg("features_landed"), 16)

            sp.wait_ge(sg("features_stored"), 48 * NPAIR)
            sp.wait_ge(sg("diagonals_cleared"), N_CLEAR)
            with sp.Fori(0, NC) as c:
                sp.wait_ge(sg("y_multiplied"), c + 1)
                for half in range(2):
                    ph = slice(half * HD, (half + 1) * HD)
                    for dst, kind in ((abd, 0), (bbd, 2), (kbd, 3)):
                        sp.dma_start(dst[ph, :, half, :], ab_d[bass.ds(c, 1), ph, :, kind, :].rearrange("a p n t -> (a p) n t")).then_inc(sg("chunk_landed"), 16)
                    sp.dma_start(vbd[ph, :, half, :], v_d[bass.ds(c, 1), ph, :, :].rearrange("a p n t -> (a p) n t")).then_inc(sg("chunk_landed"), 16)
                sp.dma_start(ars[:, :, :, :], ab_d[bass.ds(c, 1), :, :, 0:2, :].rearrange("a p n k t -> (a p) n k t")).then_inc(sg("chunk_landed"), 16)

            sp.wait_ge(sg("y_stored"), 16 * NC)
            sp.wait_ge(sg("state_ready"), NC)
            with sp.Fori(0, NPAIR) as i:
                sp.wait_ge(sg("mixed"), i + 1)
                sp.dma_start(yt[:, :].rearrange("p (c t) -> p c t", c=NC),
                             y_d[:, :, bass.ds(i, 1), :].rearrange("c p a t -> p c (a t)")).then_inc(sg("y_landed"), 16)
                sp.dma_start(yb[:, :], bonus_d[bass.ds(i, 1), :, :].rearrange("a p t -> (a p) t")).then_inc(sg("y_landed"), 16)
                sp.dma_start(g2a[:, :], g2[0, 0:P, bass.ds(i * P, P)]).then_inc(sg("y_landed"), 16)
                sp.dma_start(g2b[:, :], g2[0, P:P + 32, bass.ds(i * P, P)]).then_inc(sg("y_landed"), 16)

            sp.dma_start(fin[:, :], zo_d[32:48, :]).then_inc(sg("f_landed"), 16)
            sp.dma_start(bf[:, :], b_f.rearrange("a n -> n a")).then_inc(sg("f_landed"), 16)
            sp.wait_ge(sg("c_stored"), 16)
            with sp.Fori(0, NPAIR) as i:
                sp.wait_ge(sg("fox_made"), i + 1)
                for dst, src in ((qin, Z_FQ), (k_in, Z_FK), (v_in, Z_FV)):
                    sp.dma_start(dst[:, :], z_d[bass.ds(i + src, 1), :, :].rearrange("a p t -> (a p) t")).then_inc(sg("fox_landed"), 16)
                for k in range(2):
                    sp.dma_start(ncb[:, k, :], c_d[bass.ds(2 * i + k, 1), :].broadcast_to([P, T])).then_inc(sg("fox_landed"), 16)

            sp.wait_ge(sg("mixed"), NPAIR + 1)
            sp.wait_ge(sg("h_stored"), 16 * 4)
            for k in range(4):
                sp.dma_start(h[:, 4 * k:4 * k + 4, :], h_v[:, 4 * k:4 * k + 4, :]).then_inc(sg("h_landed"), 16)
            for s in range(2):
                unit(s, w_out_v[:, s * UK:(s + 1) * UK, P:2 * P], Z_ODD + 2 * M_OUT + 2 + s)
            stream(w_out_v, 0, 2 * P, M_OUT + 2, KT - 2)
            with sp.Fori(0, FG) as g:
                for view, m0, row, cc in ((ff1_v, 0, 0, D), (ff2_v, KT, KT, 0)):
                    with sp.Fori(0, KT // 2) as i:
                        for b in range(2):
                            for s in range(2):
                                r0 = s * UK
                                src = (view[:, r0:r0 + UK, bass.ds(g * D + i * (2 * P) + b * P, P)] if cc else
                                       view[:, bass.ds(g * KT + r0, UK), bass.ds(i * (2 * P) + b * P, P)])
                                unit(s, src, g * (4 * KT) + i * 4 + (Z_ODD + 2 * (M_FF + m0) + 2 * b + s))
            def gate_units(n, i=0):
                for s in range(2):
                    unit(s, gate_v[:, s * UK:(s + 1) * UK, bass.ds(i * (2 * P) + n * P, P)], i * 4 + (Z_ODD + 2 * (M_GATE + n) + s))

            gate_units(0)
            sp.wait_ge(sg("unit_done"), 2 + Z_ODD + 2 * M_GATE)
            sp.dma_start(p_in[:, :, :], p.rearrange("l a (b q) n -> q (l a b) n", q=P)).then_inc(sg("p_landed"), 16)

            def ple_weights(b, c0, n):
                sp.wait_ge(sg("ple_split"), n + 1)
                sp.dma_start(pw[:, b, :, :], ple_v[:, :, bass.ds(c0, P)]).then_inc(sg(f"ple_landed{b}"), 16)

            ple_weights(0, 0, 0)
            ple_weights(1, P, 1)
            gate_units(1)
            with sp.Fori(0, KT // 2 - 1) as i:
                for b in range(2):
                    ple_weights(b, i * (2 * P) + (b + 2) * P, 2 * i + (b + 2))
                    gate_units(b + 2, i)
            o_v = out.rearrange("a (b q) n -> q (a b) n", q=P)
            with sp.Fori(0, KT // 2) as i:
                for b in range(2):
                    sp.wait_ge(sg("out_ready"), 2 * i + b + 3)
                    sp.dma_start(o_v[:, :, bass.ds(i * (2 * P) + b * P, P)], ot[:, b, :, :]).then_inc(sg(f"out_stored{b}"), 16)
            for b in range(2):
                sp.wait_ge(sg(f"out_stored{b}"), 16 * (KT // 2))

        @block.tensor
        def _(pe):
            pe.sem_inc(sg("unit_done"), 2)
            pe.sem_inc(sg("x_transposed"), 2)
            pe.sem_inc(sg("ple_done"), 2)
            pe.sem_inc(sg("final_transposed"), 2)
            pe.sem_inc(sg("y_multiplied"), 1)

            mm = nc.tensor.matmul

            def gemm(dst, hi, lo, n, width=P, ready=None):
                for s in range(2):
                    pe.wait_ge(sg("w_split"), n + s + 3)
                    for k in range(UK):
                        kt = s * UK + k
                        if ready is not None and k == 0:
                            pe.wait_ge(sg("operand_split"), ready + (UK if s == 0 else KT))
                        wh, wl = w_hi[:, s, k, 0:width], w_lo[:, s, k, 0:width]
                        mm(dst, wh, hi[:, kt, :], start=kt == 0, stop=False)
                        mm(dst, wh, lo[:, kt, :], start=False, stop=False)
                        last = mm(dst, wl, hi[:, kt, :], start=False, stop=kt == KT - 1)
                    last.then_inc(sg("unit_done"), 1)

            def tiles(m, count, hi, lo, ready=None, outer=0, after=None):
                with pe.Fori(0, count // 2) as i:
                    for b in range(2):
                        pe.wait_ge(sg("acc_taken"), i * 2 + outer + (m + b + 1))
                        gemm(acc[b][:, :], hi, lo, i * 4 + outer * 2 + (Z_ODD + 2 * m + 2 * b), ready=ready)
                        if after:
                            after(i, b)

            def spread_sumsq(n):
                pe.wait_ge(sg("squares_summed"), 2 + KT * (n + 1))
                mm(bank[3][:, :], ones, sumsq[:, :], start=True, stop=True).then_inc(sg("sumsq_spread"), 1)

            def head_stat(c, src):
                pe.wait_ge(sg("head_squares_ready"), c + 1)
                for q in range(T // P):
                    last = mm(bank[5][:, 2 * q:2 * q + 2], src[:, q * P:(q + 1) * P], head_of, start=True, stop=True)
                last.then_inc(sg("head_sums_done"), 1)
                pe.wait_ge(sg("head_inverse_ready"), c + 1)
                for q in range(T // P):
                    last = mm(bank[5][0:2, q * P:(q + 1) * P], hr[:, 2 * q:2 * q + 2], ident, start=True, stop=True)
                last.then_inc(sg("head_rows_done"), 1)
                pe.wait_ge(sg("head_rows_ready"), c + 1)
                mm(bank[4][:, :], of_head, hrt[:, :], start=True, stop=True).then_inc(sg("head_spread"), 1)

            pe.wait_ge(sg("constants_landed"), 16)
            pe.wait_ge(sg("parameters_landed"), 16 * N_PAR)
            for k in range(2):
                last = nc.tensor.transpose(bank[0][:, k * P:(k + 1) * P], prow[:, k, :], ident)
            last.then_inc(sg("parameters_transposed"), 1)
            with pe.Fori(0, KT // 2) as i:
                for b in range(2):
                    pe.wait_ge(sg(f"x_landed{b}"), 16 * i + 16)
                    if b == 0:
                        pe.wait_ge(sg("parameters_ready"), 1)
                    pe.wait_ge(sg("xt_taken"), 2 * i + b + 1)
                    for q in range(T // P):
                        last = nc.tensor.transpose(bank[1 + b][:, q * P:(q + 1) * P], xin[:, b, q, :], ident)
                    last.then_inc(sg("x_transposed"), 1)
            gemm(bank[0][0:48, :], a_hi, a_lo, 0, width=48, ready=0)
            spread_sumsq(0)
            tiles(0, Z_TILES, a_hi, a_lo)

            pe.wait_ge(sg("lora_features_ready"), 3)
            with pe.Fori(0, NPAIR) as i:
                pe.wait_ge(sg("features_landed"), 80 * i + 80)
                mm(bank[0][:, :], wa_in[0:64, :], tx[0:64, :], start=True, stop=True)
                mm(bank[1][:, :], wa_in[64:128, :], tx[64:128, :], start=True, stop=True).then_inc(sg("lora_multiplied"), 1)
                head_stat(i, t1)
                pe.wait_ge(sg("rk_ready"), i + 1)
                mm(bank[2][:, :], const(C_BLK, P), t2[:, :], start=True, stop=True).then_inc(sg("bonus_summed"), 1)

            pe.wait_ge(sg("diagonals_cleared"), N_CLEAR)
            with pe.Fori(0, NC) as c:
                pe.wait_ge(sg("chunk_landed"), 144 * c + 144)
                pe.wait_ge(sg("y_taken"), 1 * c)
                pe.wait_ge(sg("state_ready"), 1 * c)
                for k, src in enumerate((bbd, kbd)):
                    for n in range(NPAIR):
                        last = mm(bank[2 * k + n // 4][:, (n % 4) * P:(n % 4 + 1) * P], src[:, n, :, :].rearrange("p a t -> p (a t)"),
                                  ars[:, n, :, :].rearrange("p a t -> p (a t)"), start=True, stop=True)
                        if n % 4 == 3:
                            last.then_inc(sg("products_done"), 1)
                for k, src in enumerate((bbd, kbd, vbd)):
                    for half in range(2):
                        pe.wait_ge(sg("transposes_taken"), 6 * c + 2 * k + half + 1)
                        for n in range(4):
                            last = nc.tensor.transpose(bank[4 + half][:, n * P:(n + 1) * P],
                                                       src[:, 4 * half + n, :, :].rearrange("p a t -> p (a t)"), ident)
                        last.then_inc(sg("transposes_done"), 1)
                pe.wait_ge(sg("x_bd_ready"), 6 * c + 1)
                for n in range(NPAIR):
                    last = mm(bank[0][:, n * C:(n + 1) * C], xbd[:, n, :, :].rearrange("p a t -> p (a t)"), eye2, start=True, stop=True)
                last.then_inc(sg("xt0_done"), 1)
                for lv in range(1, 6):
                    pe.wait_ge(sg("n_ready"), 5 * c + lv)
                    pe.wait_ge(sg("xt_ready"), 5 * c + lv)
                    for n in range(NPAIR):
                        last = mm(bank[1][:, n * C:(n + 1) * C], nbd[:, lv % 2, n, :, :].rearrange("p a t -> p (a t)"), xt[:, n, :], start=True, stop=True)
                    last.then_inc(sg("pt_done"), 1)
                    pe.wait_ge(sg("pt_ready_a"), 5 * c + lv)
                    pe.wait_ge(sg("pt_ready_b"), 5 * c + lv)
                    for n in range(NPAIR):
                        last = mm(bank[2][:, n * C:(n + 1) * C], ptbd[:, n, :, :].rearrange("p a t -> p (a t)"), xs[:, n, :], start=True, stop=True)
                    last.then_inc(sg("dx_done"), 1)
                    if lv < 5:
                        pe.wait_ge(sg("x_bd_ready"), 6 * c + lv)
                        for n in range(NPAIR):
                            last = mm(bank[3][:, n * C:(n + 1) * C], xbd[:, n, :, :].rearrange("p a t -> p (a t)"), pt[:, n, :], start=True, stop=True)
                        last.then_inc(sg("dxt_done"), 1)
                pe.wait_ge(sg("m_ready"), c + 1)
                pe.wait_ge(sg("v_stacked"), c + 1)
                pe.wait_ge(sg("state_ready"), 1 * c)
                for n in range(NPAIR):
                    mm(bank[0][:, n * C:(n + 1) * C], abd[:, n, :, :].rearrange("p a t -> p (a t)"), st[:, n, :], start=True, stop=False)
                    last = mm(bank[0][:, n * C:(n + 1) * C], mbd[:, n, :, :].rearrange("p a t -> p (a t)"), vst[:, n, :], start=False, stop=True)
                last.then_inc(sg("r_done"), 1)
                pe.wait_ge(sg("r_ready"), c + 1)
                pe.wait_ge(sg("x_bd_ready"), 6 * c + 6)
                for n in range(NPAIR):
                    last = mm(bank[1][:, n * C:(n + 1) * C], xbd[:, n, :, :].rearrange("p a t -> p (a t)"), rr[:, n, :], start=True, stop=True)
                last.then_inc(sg("sa_done"), 1)
                pe.wait_ge(sg("sa_ready_a"), c + 1)
                pe.wait_ge(sg("sa_ready_b"), c + 1)
                pe.wait_ge(sg("transposes_taken"), 6 * c + 8)
                for n in range(NPAIR):
                    mm(bank[5][:, n * C:(n + 1) * C], bt[:, n, :], sa[:, n, :], start=True, stop=False)
                    last = mm(bank[5][:, n * C:(n + 1) * C], ktm[:, n, :], vst[:, n, :], start=False, stop=True)
                last.then_inc(sg("s_done"), 1)
                pe.wait_ge(sg("state_bd_ready_a"), 1 * c)
                pe.wait_ge(sg("state_bd_ready_b"), 1 * c)
                for n in range(NPAIR):
                    o = bank[4][:, n * C:(n + 1) * C]
                    mm(o, stbd[:, n, :, :].rearrange("p a t -> p (a t)"), ars[:, n, 1, :], start=True, stop=False)
                    mm(o, sabd[:, n, :, :].rearrange("p a t -> p (a t)"), gb[:, n, 1, :], start=False, stop=False)
                    last = mm(o, vt[:, n, :], gk[:, n, 1, :], start=False, stop=True)
                last.then_inc(sg("y_multiplied"), 1)

            with pe.Fori(0, NPAIR) as i:
                pe.wait_ge(sg("y_landed"), 64 * i + 64)
                mm(bank[0][:, :], const(C_BLK, P), yt[:, :], start=True, stop=True).then_inc(sg("mean_done"), 1)
                mm(bank[1][:, :], g2a[:, :], sga[:, :], start=True, stop=False)
                mm(bank[1][:, :], g2b[:, :], sgb[:, :], start=False, stop=True).then_inc(sg("gate_done"), 1)
                head_stat(i + NPAIR, sq[:, 0, :])

            pe.wait_ge(sg("f_cumulated"), 1)
            for q in range(T // P):
                last = mm(bank[0][:, q * 16:(q + 1) * 16], f1[:, q * P:(q + 1) * P], ident[0:16, 0:16], start=True, stop=True)
            last.then_inc(sg("c_transposed"), 1)
            pe.wait_ge(sg("cq_ready"), 1)
            with pe.Fori(0, NPAIR) as i:
                pe.wait_ge(sg("fox_landed"), 80 * i + 80)
                for q in range(T // P):
                    last = nc.tensor.transpose(bank[0][:, q * P:(q + 1) * P], v_in[:, q * P:(q + 1) * P], ident)
                last.then_inc(sg("fv_done"), 1)
                for k in range(2):
                    head_stat(i * 2 + 2 * NPAIR + k, sq[:, k, :])
                for k in range(2):
                    ph = slice(k * HD, (k + 1) * HD)
                    pe.wait_ge(sg("qk_ready"), 2 * i + 2)
                    for q in range(T // P):
                        pe.wait_ge(sg("logits_taken"), i * 8 + 4 * k + q + 1)
                        mm(bank[2 + q % 2][:, 0:(q + 1) * P], qh[ph, q * P:(q + 1) * P], kh[ph, 0:(q + 1) * P],
                           start=True, stop=True).then_inc(sg("logits_done"), 1)
                    for j in range(T // P):
                        pe.wait_ge(sg("probs_ready"), i * 8 + 4 * k + 4)
                        pe.wait_ge(sg("probs_t_taken"), i * 8 + 4 * k + j + 1)
                        for q in range(j, T // P):
                            last = nc.tensor.transpose(bank[4 + j % 2][:, q * P:(q + 1) * P], pr[:, q, j * P:(j + 1) * P], ident)
                        last.then_inc(sg("probs_t_done"), 1)
                    for j in range(T // P):
                        pe.wait_ge(sg("probs_t_taken"), i * 8 + 4 * k + j + 3)
                        if j == 0:
                            pe.wait_ge(sg("fv_ready"), i + 1)
                            pe.wait_ge(sg("fox_taken"), 1 * i)
                        last = mm(bank[1][ph, j * P:], vtm[:, j, ph], prt[:, j, j * P:], start=j == 0, stop=j == T // P - 1)
                    last.then_inc(sg("heads_done"), 1)

            tiles(M_OUT, KT, a_hi, a_lo, ready=KT)
            spread_sumsq(1)
            with pe.Fori(0, FG) as g:
                tiles(M_FF, KT, b_hi, b_lo, ready=2 * KT, outer=g * (2 * KT))
                tiles(M_FF + KT, KT, a_hi, a_lo, ready=g * KT + 3 * KT, outer=g * (2 * KT))
            spread_sumsq(2)

            pe.wait_ge(sg("p_landed"), 16)
            for k in range(2):
                for q in range(T // P):
                    last = nc.tensor.transpose(bank[k][:, q * P:(q + 1) * P], p_in[:, q, k * P:(k + 1) * P], ident)
            last.then_inc(sg("p_transposed"), 1)
            pe.wait_ge(sg("p_split"), 1)

            def embed(i, b):
                pe.wait_ge(sg("ple_split"), 2 * i + b + 3)
                pe.wait_ge(sg("ple_taken"), 2 * i + b + 1)
                for k in range(2):
                    mm(bank[b][:, :], pw_hi[:, b, k, :], p_hi[:, k, :], start=k == 0, stop=False)
                    mm(bank[b][:, :], pw_hi[:, b, k, :], p_lo[:, k, :], start=False, stop=False)
                    last = mm(bank[b][:, :], pw_lo[:, b, k, :], p_hi[:, k, :], start=False, stop=k == 1)
                last.then_inc(sg("ple_done"), 1)

            tiles(M_GATE, KT, b_hi, b_lo, ready=(3 + FG) * KT, after=embed)
            spread_sumsq(3)
            with pe.Fori(0, KT // 2) as i:
                for b in range(2):
                    pe.wait_ge(sg("final_ready"), 2 * i + b + 1)
                    pe.wait_ge(sg("out_ready"), 2 * i + b + 1)
                    for q in range(T // P):
                        last = nc.tensor.transpose(bank[4 + b][:, q * P:(q + 1) * P], hn[:, b, q * P:(q + 1) * P], ident)
                    last.then_inc(sg("final_transposed"), 1)

        @block.scalar
        def _(act):
            act.sem_inc(sg("xt_taken"), 2)
            act.sem_inc(sg("transposes_taken"), 2)
            act.sem_inc(sg("probs_t_taken"), 2)
            act.sem_inc(sg("out_ready"), 2)
            A = nc.scalar.activation

            def settled():
                act.sem_inc(sg("act_waits_taken"), 1)

            def next_units(i, m, outer=0):
                for s in range(2):
                    act.wait_ge(sg(f"w_landed{s}"), i * 32 + outer * 16 + 16 * (m + 4))
                    act.wait_ge(sg("unit_done"), i * 4 + outer * 2 + (Z_ODD + 2 * (m + 1) + s + 1))
                    A(w_hi[:, s, :, :], w_raw[:, s, :, :], ACT.Copy).then_inc(sg("w_hi_ready"), 1)

            def fold(hi, gain, f, n, b, gains=True):
                act.wait_ge(sg("h_ready"), n + 1)
                if gains:
                    A(hi[:, bass.ds(f, 1), :], h[:, bass.ds(f, 1), :], ACT.Copy, scale=pc(gain, f)).then_inc(sg("operand_hi_ready"), 1)
                act.wait_ge(sg("squares_summed"), n + 1)
                settled()
                A(sq[:, b:b + 1, :], h[:, bass.ds(f, 1), :], ACT.Square).then_inc(sg("squares_ready"), 1)

            def root(n):
                act.wait_ge(sg("mean_square_ready"), n + 1)
                A(tmp[:, :], tmp[:, :], ACT.Sqrt).then_inc(sg("rms_ready"), 1)

            def head_stat(c):
                act.wait_ge(sg("head_means_ready"), c + 1)
                A(hr[:, :], hs[:, :], ACT.Sqrt).then_inc(sg("head_roots_ready"), 1)
                act.wait_ge(sg("head_rows_done"), c + 1)
                A(hrt[:, :], bank[5][0:2, :], ACT.Copy).then_inc(sg("head_rows_ready"), 1)

            act.wait_ge(sg("parameters_transposed"), 1)
            A(par[:, :], bank[0][:, 0:160], ACT.Copy).then_inc(sg("parameters_ready"), 1)
            act.wait_ge(sg("parameters_ready"), 1)
            with act.Fori(0, KT // 2) as i:
                for b in range(2):
                    act.wait_ge(sg("x_transposed"), 2 * i + b + 3)
                    settled()
                    A(h[:, bass.ds(2 * i + b, 1), :], bank[1 + b][:, :].rearrange("p (a t) -> p a t", a=1), ACT.Copy).then_inc(sg("h_ready"), 1)
                    act.wait_ge(sg("h_ready"), 2 * i + b + 1)
                    act.sem_inc(sg("xt_taken"), 1)
                    fold(a_hi, "norm_mix", 2 * i + b, 2 * i + b, b)
            for s in range(2):
                act.wait_ge(sg(f"w_landed{s}"), 32)
                act.wait_ge(sg("unit_done"), s + 1)
                A(w_hi[:, s, :, 0:48], w_raw[:, s, :, 0:48], ACT.Copy).then_inc(sg("w_hi_ready"), 1)
            next_units(0, -1)
            root(0)

            def stage(m, count, outer=0, body=None, peel=False):
                with act.Fori(0, count // 2) as i:
                    for b in range(2):
                        next_units(i, m + b, outer)
                        if body:
                            body(i, b)

            stage(0, Z_TILES)

            act.wait_ge(sg("lora_shifted"), 1)
            A(tx[0:64, :], t1[0:64, :], ACT.Tanh)
            A(tx[64:128, :], t1[64:128, :], ACT.Copy).then_inc(sg("lora_features_ready"), 1)
            act.wait_ge(sg("lora_shifted"), 2)
            A(sga[:, :], t2[:, :], ACT.Sigmoid).then_inc(sg("lora_features_ready"), 1)
            act.wait_ge(sg("lora_shifted"), 3)
            A(sgb[:, :], ks[0:32, :], ACT.Sigmoid).then_inc(sg("lora_features_ready"), 1)
            with act.Fori(0, NPAIR) as i:
                act.wait_ge(sg("lora_multiplied"), i + 1)
                settled()
                A(lw[:, :], bank[0][:, :], ACT.Sigmoid, bias=pc("w0", i)).then_inc(sg("sigmoids_ready"), 1)
                A(av[:, :], bank[1][:, :], ACT.Sigmoid, bias=pc("a0", i)).then_inc(sg("sigmoids_ready"), 1)
                head_stat(i)
                act.wait_ge(sg("cum_ready"), i + 1)
                A(e_in[:, :], cum[:, :], ACT.Exp).then_inc(sg("exps_ready"), 1)
                A(e_no[:, :], cum[:, :], ACT.Exp, scale=-1.0).then_inc(sg("exps_ready"), 1)
                A(e_ex[:, :], cex[:, :], ACT.Exp).then_inc(sg("exps_ready"), 1)
                act.wait_ge(sg("exps_ready"), 3 * i + 1)
                settled()
                A(ec[:, bass.ds(i, 1), :], e_in[:, :].rearrange("p (a c t) -> p a c t", a=1, c=NC)[:, :, :, C - 1], ACT.Copy).then_inc(sg("ends_ready"), 1)

            with act.Fori(0, NC) as c:
                for n in range(6):
                    dst = (bt, ktm, vt)[n // 2]
                    act.wait_ge(sg("transposes_done"), 6 * c + n + 1)
                    A(dst[:, (n % 2) * 4:(n % 2) * 4 + 4, :], bank[4 + n % 2][:, :].rearrange("p (n t) -> p n t", n=4), ACT.Copy).then_inc(sg("transposes_taken"), 1)
                    if n == 1:
                        act.wait_ge(sg("x_ready"), 6 * c + 1)
                        A(xbd[0:64, :, 0, :], xs[0:64, :, :], ACT.Copy)
                        A(xbd[64:128, :, 1, :], xs[64:128, :, :], ACT.Copy).then_inc(sg("x_bd_ready"), 1)
                for lv in range(1, 6):
                    act.wait_ge(sg("pt_done"), 5 * c + lv)
                    A(ptbd[0:64, :, 0, :], bank[1][0:64, :].rearrange("p (n t) -> p n t", n=NPAIR), ACT.Copy)
                    A(pt[0:64, :, :], bank[1][0:64, :].rearrange("p (n t) -> p n t", n=NPAIR), ACT.Copy).then_inc(sg("pt_ready_a"), 1)
                    act.wait_ge(sg("x_ready"), 6 * c + lv + 1)
                    if lv < 5:
                        act.wait_ge(sg("dxt_done"), 4 * c + lv)
                    A(xbd[0:64, :, 0, :], xs[0:64, :, :], ACT.Copy)
                    A(xbd[64:128, :, 1, :], xs[64:128, :, :], ACT.Copy).then_inc(sg("x_bd_ready"), 1)
                act.wait_ge(sg("sa_done"), c + 1)
                act.wait_ge(sg("y_multiplied"), 1 * c + 1)
                A(sabd[0:64, :, 0, :], bank[1][0:64, :].rearrange("p (n t) -> p n t", n=NPAIR), ACT.Copy)
                A(sa[0:64, :, :], bank[1][0:64, :].rearrange("p (n t) -> p n t", n=NPAIR), ACT.Copy).then_inc(sg("sa_ready_a"), 1)
                act.wait_ge(sg("y_multiplied"), c + 2)
                act.wait_ge(sg("y_stored"), 16 * c)
                A(yo[:, :, :], bank[4][:, :].rearrange("p (n t) -> p n t", n=NPAIR), ACT.Copy).then_inc(sg("y_taken"), 1)
                act.wait_ge(sg("state_ready"), c + 1)
                A(stbd[0:64, :, 0, :], st[0:64, :, :], ACT.Copy).then_inc(sg("state_bd_ready_a"), 1)

            with act.Fori(0, NPAIR) as i:
                act.wait_ge(sg("y_centred"), i + 1)
                A(sq[:, 0, :], yc[:, :], ACT.Square).then_inc(sg("head_squares_ready"), 1)
                head_stat(i + NPAIR)
                act.wait_ge(sg("y_finished"), i + 1)
                settled()
                A(a_hi[:, bass.ds(i, 1), :], yn[:, :].rearrange("p (a t) -> p a t", a=1), ACT.Copy).then_inc(sg("operand_hi_ready"), 1)

            act.wait_ge(sg("f_prepared"), 1)
            A(f2[:, :], f2[:, :], ACT.Exp, scale=-1.0).then_inc(sg("f_exp"), 1)
            act.wait_ge(sg("f_exp"), 1)
            A(f2[:, :], f2[:, :], ACT.Ln, bias=cst[0:16, C_ONE:C_ONE + 1]).then_inc(sg("f_log"), 1)
            act.wait_ge(sg("c_transposed"), 1)
            A(cq[:, :, :], bank[0][:, 0:64].rearrange("p (q n) -> p q n", q=4), ACT.Copy).then_inc(sg("cq_ready"), 1)
            with act.Fori(0, NPAIR) as i:
                act.wait_ge(sg("fv_done"), i + 1)
                A(vtm[:, :, :], bank[0][:, :].rearrange("p (q n) -> p q n", q=4), ACT.Copy).then_inc(sg("fv_ready"), 1)
                for k, src in enumerate((qin, k_in)):
                    act.wait_ge(sg("fox_landed"), 80 * i + 80)
                    A(sq[:, k, :], src[:, :], ACT.Square).then_inc(sg("head_squares_ready"), 1)
                    head_stat(i * 2 + 2 * NPAIR + k)
                    if k == 0:
                        act.wait_ge(sg("qk_ready"), 2 * i + 1)
                for k in range(2):
                    for q in range(T // P):
                        act.wait_ge(sg("logits_max_ready"), i * 8 + 4 * k + q + 1)
                        A(pr[:, q, 0:(q + 1) * P], lg[:, q, 0:(q + 1) * P], ACT.Exp, bias=nmx[:, q:q + 1],
                          accum_out=rsum[:, q:q + 1]).then_inc(sg("exp_ready"), 1)
                    for j in range(T // P):
                        act.wait_ge(sg("probs_t_done"), i * 8 + 4 * k + j + 1)
                        if j == 0 and k == 1:
                            act.wait_ge(sg("heads_done"), 2 * i + 1)
                        A(prt[:, j, j * P:], bank[4 + j % 2][:, j * P:], ACT.Copy).then_inc(sg("probs_t_taken"), 1)
                act.wait_ge(sg("heads_done"), 2 * i + 2)
                A(og[:, :], bank[1][:, :], ACT.Copy).then_inc(sg("fox_taken"), 1)
                act.wait_ge(sg("fox_taken"), i + 1)
                settled()
                A(a_hi[:, bass.ds(i + NPAIR, 1), :], og[:, :].rearrange("p (a t) -> p a t", a=1), ACT.Copy).then_inc(sg("operand_hi_ready"), 1)

            stage(M_OUT, KT, body=lambda i, b: fold(b_hi, "norm_mlp", 2 * i + b, 2 * i + (b + KT), b))
            root(1)

            def hidden(g):
                def body(i, b):
                    act.wait_ge(sg("relu_squared"), 2 * i + g * KT + (b + 1))
                    settled()
                    A(a_hi[:, bass.ds(2 * i + b, 1), :], sq[:, b:b + 1, :], ACT.Copy).then_inc(sg("operand_hi_ready"), 1)
                return body

            with act.Fori(0, FG - 1) as g:
                stage(M_FF, KT, outer=g * (2 * KT), body=hidden(g))
                stage(M_FF + KT, KT, outer=g * (2 * KT))
            stage(M_GATE - 2 * KT, KT, body=hidden(FG - 1))
            stage(M_GATE - KT, KT, body=lambda i, b: fold(b_hi, "norm_ple", 2 * i + b, 2 * i + (b + 2 * KT), b))
            root(2)

            act.wait_ge(sg("p_transposed"), 1)
            for k in range(2):
                A(p_t[:, k, :], bank[k][:, :], ACT.Copy).then_inc(sg("p_taken"), 1)
            act.wait_ge(sg("p_taken"), 2)
            A(p_hi[:, :, :], p_t[:, :, :], ACT.Copy).then_inc(sg("p_hi_ready"), 1)

            def gated(i, b):
                act.wait_ge(sg("gate_scaled"), 2 * i + (b + 1))
                A(gt[:, b, :], ev[:, b, :], ACT.Sigmoid).then_inc(sg("gate_ready"), 1)
                fold(None, None, 2 * i + b, 2 * i + (b + 3 * KT), b, gains=False)

            def ple_units(i, b):
                act.wait_ge(sg(f"ple_landed{b}"), i * 16 + 16)
                act.wait_ge(sg("ple_done"), i * 2 + b + 1)
                A(pw_hi[:, b, :, :], pw[:, b, :, :], ACT.Copy).then_inc(sg("ple_hi_ready"), 1)

            with act.Fori(0, KT // 2 - 1) as i:
                for b in range(2):
                    ple_units(i, b)
                    next_units(i, M_GATE + b)
                    gated(i, b)
            i = KT // 2 - 1
            ple_units(i, 0)
            next_units(i, M_GATE)
            gated(i, 0)
            ple_units(i, 1)
            gated(i, 1)
            root(3)
            with act.Fori(0, KT // 2) as i:
                for b in range(2):
                    act.wait_ge(sg("final_transposed"), 2 * i + b + 3)
                    act.wait_ge(sg(f"out_stored{b}"), 16 * i)
                    A(ot[:, b, :, :], bank[4 + b][:, :].rearrange("p (q n) -> p q n", q=4), ACT.Copy).then_inc(sg("out_ready"), 1)

        @block.vector
        def _(dve):
            V = nc.vector
            for name, n in (("w_split", 2), ("acc_taken", 2), ("features_made", 1), ("mixed", 1), ("fox_made", 1),
                            ("logits_taken", 2), ("ple_split", 2), ("ple_taken", 2)):
                dve.sem_inc(sg(name), n)
            chain = [0, 0, 0]

            def then(ins):
                ins.then_inc(sg("dve_chain"), 1)
                chain[0] += 1
                dve.wait_ge(sg("dve_chain"), chain[0] + (chain[1] * chain[2] if chain[2] else 0))

            def chained(i, steps):
                chain[1], chain[2] = i, steps
                return chain[0] + steps

            def unchained(turns, end):
                assert end == chain[0], f"steps a turn: {chain[0] - end + chain[2]}"
                chain[0] += chain[2] * (turns - 1)
                chain[1], chain[2] = 0, 0

            def lo_unit(s, n, width=P):
                dve.wait_ge(sg("w_hi_ready"), n + 1)
                V.tensor_tensor(w_lo[:, s, :, 0:width], w_raw[:, s, :, 0:width], w_hi[:, s, :, 0:width].bitcast(F32),
                                ALU.subtract).then_inc(sg("w_split"), 1)

            def next_units(i, m, outer=0):
                for s in range(2):
                    lo_unit(s, i * 4 + outer * 2 + (Z_ODD + 2 * (m + 1) + s))

            def fold(hi, lo, gain, f, n):
                dve.wait_ge(sg("operand_hi_ready"), n + 1)
                V.scalar_tensor_tensor(lo[:, bass.ds(f, 1), :], h[:, bass.ds(f, 1), :], pc(gain, f), hi[:, bass.ds(f, 1), :].bitcast(F32),
                                       ALU.mult, ALU.subtract).then_inc(sg("operand_split"), 1)

            def invert_rms(n):
                dve.wait_ge(sg("sumsq_spread"), n + 1)
                V.tensor_scalar(tmp[:, :], bank[3][:, :], 1.0 / D, EPS, ALU.mult, ALU.add).then_inc(sg("mean_square_ready"), 1)
                dve.wait_ge(sg("rms_ready"), n + 1)
                then(V.reciprocal(rstd[:, :], tmp[:, :]))

            def head_stat(c, kind):
                dve.wait_ge(sg("head_sums_done"), c + 1)
                a = {"kk": (1e-24, None, ALU.max, ALU.bypass), "rms": (1.0 / HD, EPS, ALU.mult, ALU.add),
                     "gn": (1.0 / HD, GN_EPS, ALU.mult, ALU.add)}[kind]
                V.tensor_scalar(hs[:, :], bank[5][:, 0:8], a[0], a[1], a[2], a[3]).then_inc(sg("head_means_ready"), 1)
                dve.wait_ge(sg("head_roots_ready"), c + 1)
                V.reciprocal(hr[:, :], hr[:, :]).then_inc(sg("head_inverse_ready"), 1)
                dve.wait_ge(sg("head_spread"), c + 1)

            def stage(m, count, outer=0, body=None):
                with dve.Fori(0, count // 2) as i:
                    for b in range(2):
                        next_units(i, m + b, outer)
                        dve.wait_ge(sg("unit_done"), i * 4 + outer * 2 + (2 + Z_ODD + 2 * (m + b + 1)))
                        body(i, b)

            dve.wait_ge(sg("parameters_ready"), 1)
            with dve.Fori(0, KT) as i:
                fold(a_hi, a_lo, "norm_mix", i, 1 * i)
            dve.wait_ge(sg("operand_split"), KT)
            lo_unit(0, 0, 48)
            lo_unit(1, 1, 48)
            next_units(0, -1)
            invert_rms(0)
            dve.wait_ge(sg("unit_done"), 2 + Z_ODD)
            V.tensor_tensor(ev[0:48, 0, :], bank[0][0:48, :], rstd[0:48, :], ALU.mult).then_inc(sg("odd_ready"), 1)

            def project(i, b):
                dve.wait_ge(sg(f"ev_free{b}"), 16 * i + 16 * (b == 0))
                V.tensor_tensor(ev[:, b, :], acc[b][:, :], rstd[:, :], ALU.mult).then_inc(sg("acc_taken"), 1)

            stage(0, Z_TILES, body=project)

            def shift(dst, src, mu, parts=P):
                then(V.tensor_tensor(dif[0:parts, :], src[0:parts, 0:T], src[0:parts, 1:], ALU.subtract))
                return V.scalar_tensor_tensor(dst, dif[0:parts, :], mu[0:parts, :], src[0:parts, 1:], ALU.mult, ALU.add)

            dve.wait_ge(sg("lora_in_landed"), 64)
            dve.wait_ge(sg("first_columns_zero"), 5)
            shift(t1[:, :], xin_l, pc("mu", 24)).then_inc(sg("lora_shifted"), 1)
            dve.wait_ge(sg("lora_shifted"), 1)
            shift(t2[:, :], rin, pc("mu", 25)).then_inc(sg("lora_shifted"), 1)
            dve.wait_ge(sg("lora_shifted"), 2)
            shift(ks[0:32, :], xin_g, pc("mu", 26), 32).then_inc(sg("lora_shifted"), 1)
            dve.wait_ge(sg("lora_features_ready"), 3)
            dve.wait_ge(sg("lora_shifted"), 3)
            with dve.Fori(0, NPAIR) as i:
                end = chained(i, 17)
                dve.wait_ge(sg("features_landed"), 80 * i + 80)
                then(shift(ks[:, :], kin, pc("mu", i + 8)))
                then(V.tensor_scalar(kkr[:, :], ks[:, :], pc("k_k", i), None, ALU.mult))
                V.tensor_tensor(t1[:, :], kkr[:, :], kkr[:, :], ALU.mult).then_inc(sg("head_squares_ready"), 1)
                then(shift(rs[:, :], rin, pc("mu", i)))
                dve.wait_ge(sg("sigmoids_ready"), 2 * i + 2)
                then(V.tensor_scalar(lw[:, :], lw[:, :], -float(np.exp(-0.5)), None, ALU.mult))
                then(V.tensor_tensor_scan(cum[:, :], reset[:, :], lw[:, :], 0.0, ALU.mult, ALU.add))
                V.tensor_tensor(cex[:, :], cum[:, :], lw[:, :], ALU.subtract).then_inc(sg("cum_ready"), 1)
                head_stat(i, "kk")
                then(V.tensor_tensor(kk[:, :], kkr[:, :], bank[4][:, :], ALU.mult))
                dve.wait_ge(sg("exps_ready"), 3 * i + 3)
                dve.wait_ge(sg("features_stored"), 48 * i)

                def by_chunk(t):
                    return t[:, :].rearrange("p (c t) -> p c t", c=NC)

                V.scalar_tensor_tensor(ab[:, :, 0, :], by_chunk(kk), -1.0, by_chunk(e_ex), ALU.mult, ALU.mult)
                V.tensor_tensor(ab[:, :, 1, :], by_chunk(rs), by_chunk(e_in), ALU.mult)
                then(V.tensor_tensor(t2[:, :], kk[:, :], av[:, :], ALU.mult))
                then(V.tensor_tensor(ab[:, :, 2, :], by_chunk(t2), by_chunk(e_no), ALU.mult))
                then(V.tensor_scalar(t1[:, :], av[:, :], -1.0, pc("k_a", i), ALU.add, ALU.mult))
                then(V.scalar_tensor_tensor(km[:, :], t1[:, :], 1.0, ks[:, :], ALU.add, ALU.mult))
                then(V.tensor_tensor(ab[:, :, 3, :], by_chunk(km), by_chunk(e_no), ALU.mult))
                then(shift(vs[:, :], vin, pc("mu", i + 16)))
                then(V.tensor_tensor(t1[:, :], rs[:, :], km[:, :], ALU.mult))
                V.tensor_scalar(t2[:, :], t1[:, :], pc("r_k", i), None, ALU.mult).then_inc(sg("rk_ready"), 1)
                dve.wait_ge(sg("bonus_summed"), i + 1)
                dve.wait_ge(sg("ends_ready"), i + 1)
                then(V.scalar_tensor_tensor(bon[:, :], bank[2][:, :], float(HD), vs[:, :], ALU.mult, ALU.mult))
                dve.sem_inc(sg("features_made"), 1)
            unchained(NPAIR, end)

            def m3(b, n=NPAIR):
                return b.rearrange("p (n t) -> p n t", n=n)

            dve.wait_ge(sg("diagonals_cleared"), N_CLEAR)
            with dve.Fori(0, NC) as c:
                end = chained(c, 2)
                for k in range(4):
                    dve.wait_ge(sg("products_done"), 4 * c + k + 1)
                    V.tensor_tensor((gb, gk)[k // 2][:, 4 * (k % 2):4 * (k % 2) + 4, :, :].rearrange("p n a t -> p n (a t)"), m3(bank[k][:, :], 4),
                                    const(C_MASK, P)[:, None, :].broadcast_to([P, 4, P]), ALU.mult).then_inc(sg("products_ready"), 1)
                    if k == 1:
                        dve.wait_ge(sg("products_ready"), 4 * c + 2)
                        then(V.tensor_tensor(xs[:, :, :], gb[:, :, 0, :], const(C_LVL, C)[:, None, :].broadcast_to([P, NPAIR, C]), ALU.mult))
                        V.tensor_tensor(xs[:, :, :], xs[:, :, :], eye2[:, None, :].broadcast_to([P, NPAIR, C]), ALU.add).then_inc(sg("x_ready"), 1)
                dve.wait_ge(sg("xt0_done"), c + 1)
                V.tensor_copy(xt[:, :, :], m3(bank[0][:, :])).then_inc(sg("xt_ready"), 1)
                for lv in range(1, 6):
                    dve.wait_ge(sg("pt_done"), 5 * c + lv)
                    V.tensor_copy(ptbd[64:128, :, 1, :], m3(bank[1][64:128, :]))
                    V.tensor_copy(pt[64:128, :, :], m3(bank[1][64:128, :])).then_inc(sg("pt_ready_b"), 1)
                    dve.wait_ge(sg("dx_done"), 5 * c + lv)
                    dve.wait_ge(sg("x_bd_ready"), 6 * c + lv)
                    dve.wait_ge(sg("x_ready"), 6 * c + lv)
                    V.tensor_tensor(xs[:, :, :], xs[:, :, :], m3(bank[2][:, :]), ALU.add).then_inc(sg("x_ready"), 1)
                    if lv < 5:
                        dve.wait_ge(sg("dxt_done"), 4 * c + lv)
                        dve.wait_ge(sg("xt_ready"), 5 * c + lv)
                        V.tensor_tensor(xt[:, :, :], xt[:, :, :], m3(bank[3][:, :]), ALU.add).then_inc(sg("xt_ready"), 1)
                dve.wait_ge(sg("r_done"), c + 1)
                V.tensor_copy(rr[:, :, :], m3(bank[0][:, :])).then_inc(sg("r_ready"), 1)
                dve.wait_ge(sg("sa_done"), c + 1)
                V.tensor_copy(sabd[64:128, :, 1, :], m3(bank[1][64:128, :]))
                V.tensor_copy(sa[64:128, :, :], m3(bank[1][64:128, :])).then_inc(sg("sa_ready_b"), 1)
                dve.wait_ge(sg("s_done"), c + 1)
                then(V.tensor_tensor(sn[:, :, :], st[:, :, :], m3(bank[5][:, :]), ALU.add))
                dve.wait_ge(sg("state_bd_ready_a"), 1 * c)
                V.tensor_tensor(st[:, :, :], sn[:, :, :], ec[:, :, bass.ds(c, 1)].broadcast_to([P, NPAIR, C]), ALU.mult).then_inc(sg("state_ready"), 1)
                dve.wait_ge(sg("y_multiplied"), c + 2)
                dve.wait_ge(sg("state_ready"), c + 1)
                V.tensor_copy(stbd[64:128, :, 1, :], st[64:128, :, :]).then_inc(sg("state_bd_ready_b"), 1)
            unchained(NC, end)
            dve.wait_ge(sg("state_bd_ready_b"), NC)

            with dve.Fori(0, NPAIR) as i:
                end = chained(i, 3)
                dve.wait_ge(sg("mean_done"), i + 1)
                V.tensor_tensor(yc[:, :], yt[:, :], bank[0][:, :], ALU.subtract).then_inc(sg("y_centred"), 1)
                dve.wait_ge(sg("y_centred"), i + 1)
                head_stat(i + NPAIR, "gn")
                then(V.tensor_tensor(yn[:, :], yc[:, :], bank[4][:, :], ALU.mult))
                then(V.tensor_scalar(yn[:, :], yn[:, :], pc("gn_w", i), pc("gn_b", i), ALU.mult, ALU.add))
                then(V.tensor_tensor(yn[:, :], yn[:, :], yb[:, :], ALU.add))
                dve.wait_ge(sg("gate_done"), i + 1)
                V.tensor_tensor(yn[:, :], yn[:, :], bank[1][:, :], ALU.mult).then_inc(sg("y_finished"), 1)
                dve.wait_ge(sg("y_finished"), i + 1)
                dve.wait_ge(sg("operand_hi_ready"), i + (KT + 1))
                V.tensor_tensor(a_lo[:, bass.ds(i, 1), :], yn[:, :].rearrange("p (a t) -> p a t", a=1), a_hi[:, bass.ds(i, 1), :].bitcast(F32), ALU.subtract).then_inc(sg("operand_split"), 1)
                dve.wait_ge(sg("operand_split"), i + (KT + 1))
                dve.sem_inc(sg("mixed"), 1)
            unchained(NPAIR, end)

            dve.wait_ge(sg("f_landed"), 32)
            then(V.tensor_scalar(fin[:, :], fin[:, :], bf[:, :], None, ALU.add))
            then(V.tensor_scalar(f1[:, :], fin[:, :], -1.0, None, ALU.mult))
            V.tensor_tensor(f2[:, :], fin[:, :], f1[:, :], ALU.max).then_inc(sg("f_prepared"), 1)
            then(V.tensor_scalar(f3[:, :], fin[:, :], 0.0, None, ALU.min))
            dve.wait_ge(sg("f_log"), 1)
            then(V.tensor_tensor(f3[:, :], f3[:, :], f2[:, :], ALU.subtract))
            then(V.memset(f2[:, :], 1.0))
            V.tensor_tensor_scan(f1[:, :], f2[:, :], f3[:, :], 0.0, ALU.mult, ALU.add).then_inc(sg("f_cumulated"), 1)
            dve.wait_ge(sg("f_cumulated"), 1)
            V.tensor_scalar(f3[:, :], f1[:, :], -1.0, None, ALU.mult).then_inc(sg("c_ready"), 1)
            then(V.tensor_scalar(qs[:, :], par[:, 120:121], HD ** -0.5, None, ALU.mult))
            dve.wait_ge(sg("cq_ready"), 1)
            with dve.Fori(0, NPAIR) as i:
                end = chained(i, 24)
                dve.wait_ge(sg("fox_landed"), 80 * i + 80)
                for k, (dst, src, gain) in enumerate(((qh, qin, qs[:, :]), (kh, k_in, par[:, 121:122]))):
                    head_stat(i * 2 + 2 * NPAIR + k, "rms")
                    V.scalar_tensor_tensor(dst[:, :], src[:, :], gain, bank[4][:, :], ALU.mult, ALU.mult).then_inc(sg("qk_ready"), 1)
                for k in range(2):
                    for q in range(T // P):
                        w = (q + 1) * P
                        dve.wait_ge(sg("logits_done"), i * 8 + 4 * k + q + 1)
                        V.scalar_tensor_tensor(lg[:, q, 0:w], bank[2 + q % 2][:, 0:w], cq[:, q, bass.ds(2 * i + k, 1)], ncb[:, k, 0:w], ALU.add, ALU.add).then_inc(sg("logits_taken"), 1)
                        dve.wait_ge(sg("logits_taken"), i * 8 + 4 * k + q + 3)
                        then(V.tensor_tensor(lg[:, q, q * P:w], lg[:, q, q * P:w], const(C_CAUS, P), ALU.add))
                        then(V.reduce_max(mx[:, q:q + 1], lg[:, q, 0:w], AX.X))
                        V.tensor_scalar(nmx[:, q:q + 1], mx[:, q:q + 1], -1.0, None, ALU.mult).then_inc(sg("logits_max_ready"), 1)
                    for q in range(T // P):
                        w = (q + 1) * P
                        dve.wait_ge(sg("exp_ready"), i * 8 + 4 * k + q + 1)
                        then(V.reciprocal(rinv[:, q:q + 1], rsum[:, q:q + 1]))
                        V.tensor_scalar(pr[:, q, 0:w], pr[:, q, 0:w], rinv[:, q:q + 1], None, ALU.mult).then_inc(sg("probs_ready"), 1)
                dve.wait_ge(sg("operand_hi_ready"), i + (KT + NPAIR + 1))
                V.tensor_tensor(a_lo[:, bass.ds(i + NPAIR, 1), :], og[:, :].rearrange("p (a t) -> p a t", a=1), a_hi[:, bass.ds(i + NPAIR, 1), :].bitcast(F32), ALU.subtract).then_inc(sg("operand_split"), 1)
                dve.wait_ge(sg("operand_split"), i + (KT + NPAIR + 1))
                dve.sem_inc(sg("fox_made"), 1)
            unchained(NPAIR, end)

            def grow(i, b, n):
                V.tensor_tensor(h[:, bass.ds(2 * i + b, 1), :], h[:, bass.ds(2 * i + b, 1), :], acc[b][:, :].rearrange("p (a t) -> p a t", a=1),
                                ALU.add).then_inc(sg("acc_taken"), 1)

            def grown(hi, lo, gain, n_h, n_op, n_acc):
                def body(i, b):
                    grow(i, b, None)
                    dve.wait_ge(sg("acc_taken"), 2 * i + (n_acc + b + 3))
                    dve.sem_inc(sg("h_ready"), 1)
                    fold(hi, lo, gain, 2 * i + b, 2 * i + (b + n_op))
                return body

            dve.wait_ge(sg("h_landed"), 64)
            stage(M_OUT, KT, body=grown(b_hi, b_lo, "norm_mlp", KT, 2 * KT, M_OUT))
            invert_rms(1)

            def hidden(g):
                def body(i, b):
                    V.scalar_tensor_tensor(ev[:, b, :], acc[b][:, :], 0.0, rstd[:, :], ALU.max, ALU.mult).then_inc(sg("acc_taken"), 1)
                    dve.wait_ge(sg("acc_taken"), 2 * i + g * (2 * KT) + (M_FF + b + 3))
                    V.tensor_tensor(sq[:, b, :], ev[:, b, :], ev[:, b, :], ALU.mult).then_inc(sg("relu_squared"), 1)
                    dve.wait_ge(sg("operand_hi_ready"), 2 * i + g * KT + (b + 3 * KT + 1))
                    V.tensor_tensor(a_lo[:, bass.ds(2 * i + b, 1), :], sq[:, b:b + 1, :], a_hi[:, bass.ds(2 * i + b, 1), :].bitcast(F32),
                                    ALU.subtract).then_inc(sg("operand_split"), 1)
                return body

            with dve.Fori(0, FG - 1) as g:
                stage(M_FF, KT, outer=g * (2 * KT), body=hidden(g))
                stage(M_FF + KT, KT, outer=g * (2 * KT), body=lambda i, b: grow(i, b, None))
            stage(M_GATE - 2 * KT, KT, body=hidden(FG - 1))
            stage(M_GATE - KT, KT, body=grown(b_hi, b_lo, "norm_ple", 2 * KT, 7 * KT, M_GATE - KT))
            invert_rms(2)

            dve.wait_ge(sg("p_hi_ready"), 1)
            V.tensor_tensor(p_lo[:, :, :], p_t[:, :, :], p_hi[:, :, :].bitcast(F32), ALU.subtract).then_inc(sg("p_split"), 1)

            def ple_unit(n, b):
                dve.wait_ge(sg("ple_hi_ready"), n + 1)
                V.tensor_tensor(pw_lo[:, b, :, :], pw[:, b, :, :], pw_hi[:, b, :, :].bitcast(F32), ALU.subtract).then_inc(sg("ple_split"), 1)

            def gated(i, b):
                n = 2 * i + b
                dve.wait_ge(sg("unit_done"), i * 4 + (2 + Z_ODD + 2 * (M_GATE + b + 1)))
                V.tensor_tensor(ev[:, b, :], acc[b][:, :], rstd[:, :], ALU.mult).then_inc(sg("acc_taken"), 1)
                dve.wait_ge(sg("acc_taken"), 2 * i + (M_GATE + b + 3))
                dve.sem_inc(sg("gate_scaled"), 1)
                dve.wait_ge(sg("gate_ready"), n + 1)
                dve.wait_ge(sg("ple_done"), n + 3)
                V.tensor_tensor(gt[:, b, :], gt[:, b, :], bank[b][:, :], ALU.mult).then_inc(sg("ple_taken"), 1)
                dve.wait_ge(sg("ple_taken"), n + 3)
                V.tensor_tensor(h[:, bass.ds(n, 1), :], h[:, bass.ds(n, 1), :], gt[:, b:b + 1, :], ALU.add).then_inc(sg("h_ready"), 1)

            with dve.Fori(0, KT // 2 - 1) as i:
                for b in range(2):
                    ple_unit(2 * i + b, b)
                    next_units(i, M_GATE + b)
                    gated(i, b)
            i = KT // 2 - 1
            ple_unit(2 * i, 0)
            next_units(i, M_GATE)
            gated(i, 0)
            ple_unit(2 * i + 1, 1)
            gated(i, 1)
            dve.wait_ge(sg("h_ready"), 4 * KT)
            invert_rms(3)
            with dve.Fori(0, KT // 2) as i:
                for b in range(2):
                    dve.wait_ge(sg("final_transposed"), 2 * i + b + 1)
                    V.scalar_tensor_tensor(hn[:, b:b + 1, :], h[:, bass.ds(2 * i + b, 1), :], pc("norm_final", 2 * i + b),
                                           rstd[:, None, :], ALU.mult, ALU.mult).then_inc(sg("final_ready"), 1)

        @block.gpsimd
        def _(pool):
            G = nc.gpsimd
            pool.sem_inc(sg("squares_summed"), 2)
            G.memset(prow[:, :, :], 0.0).then_inc(sg("rows_cleared"), 1)

            def sums(n):
                if n:
                    pool.wait_ge(sg("sumsq_spread"), n)
                G.memset(sumsq[:, :], 0.0).then_inc(sg("sumsq_cleared"), 1)
                pool.wait_ge(sg("sumsq_cleared"), n + 1)
                with pool.Fori(0, KT // 2) as i:
                    for b in range(2):
                        pool.wait_ge(sg("squares_ready"), 2 * i + (n * KT + b + 1))
                        G.tensor_tensor(sumsq[:, :], sumsq[:, :], sq[:, b, :], ALU.add).then_inc(sg("squares_summed"), 1)
                        pool.wait_ge(sg("squares_summed"), 2 * i + (n * KT + b + 3))

            sums(0)
            pool.wait_ge(sg("h_ready"), KT)
            for k in range(4):
                pool.dma_start(h_v[:, 4 * k:4 * k + 4, :], h[:, 4 * k:4 * k + 4, :]).then_inc(sg("h_stored"), 16)
            pool.wait_ge(sg("odd_ready"), 1)
            pool.dma_start(zo_d, ev[0:48, 0, :]).then_inc(sg("ev_free0"), 16)
            with pool.Fori(0, Z_TILES // 2) as i:
                for b in range(2):
                    pool.wait_ge(sg("acc_taken"), 2 * i + (b + 3))
                    pool.dma_start(z_d[bass.ds(2 * i + b, 1), :, :].rearrange("a p t -> (a p) t"), ev[:, b, :]).then_inc(sg(f"ev_free{b}"), 16)

            pool.wait_ge(sg("operand_split"), KT)
            pool.wait_ge(sg("h_stored"), 64)
            for t in (kin, rin, vin, xin_l, xin_g):
                G.memset(t[:, 0:1], 0.0).then_inc(sg("first_columns_zero"), 1)
            with pool.Fori(0, NPAIR) as i:
                pool.wait_ge(sg("features_made"), i + 2)
                pool.dma_start(ab_d[:, :, bass.ds(i, 1), :, :].rearrange("c p a k t -> p c (a k t)"), ab[:, :, :, :].rearrange("p c k t -> p c (k t)")).then_inc(sg("features_stored"), 16)
                pool.dma_start(v_d[:, :, bass.ds(i, 1), :].rearrange("c p a t -> p c (a t)"), vs[:, :].rearrange("p (c t) -> p c t", c=NC)).then_inc(sg("features_stored"), 16)
                pool.dma_start(bonus_d[bass.ds(i, 1), :, :].rearrange("a p t -> (a p) t"), bon[:, :]).then_inc(sg("features_stored"), 16)

            pool.wait_ge(sg("features_stored"), 48 * NPAIR)
            pool.wait_ge(sg("ends_ready"), NPAIR)
            for t in diagonals:
                G.memset(t, 0.0).then_inc(sg("diagonals_cleared"), 1)
            pool.wait_ge(sg("diagonals_cleared"), N_CLEAR)
            halves = ((slice(0, 64), 0), (slice(64, 128), 1))

            def level(c, lv):
                if lv > 2:
                    pool.wait_ge(sg("pt_done"), 5 * c + (lv - 2))
                for ph, a in halves:
                    last = G.tensor_tensor(nbd[ph, lv % 2, :, a, :], gb[ph, :, 0, :],
                                           const(C_LVL + lv * C, C, ph)[:, None, :].broadcast_to([64, NPAIR, C]), ALU.mult)
                last.then_inc(sg("n_ready"), 1)

            with pool.Fori(0, NC) as c:
                pool.wait_ge(sg("products_ready"), 4 * c + 2)
                level(c, 1)
                level(c, 2)
                pool.wait_ge(sg("products_ready"), 4 * c + 4)
                pool.sem_inc(sg("pool_waits_taken"), 1)
                for ph, a in halves:
                    last = G.tensor_copy(mbd[ph, :, a, :], gk[ph, :, 0, :])
                last.then_inc(sg("m_ready"), 1)
                pool.wait_ge(sg("transposes_taken"), 6 * c + 8)
                pool.sem_inc(sg("pool_waits_taken"), 1)
                for ph, a in halves:
                    last = G.tensor_copy(vst[ph, :, :], vt[ph, :, a * C:(a + 1) * C])
                last.then_inc(sg("v_stacked"), 1)
                for lv in (3, 4, 5):
                    level(c, lv)
                pool.wait_ge(sg("y_taken"), c + 1)
                pool.dma_start(y_d[bass.ds(c, 1), :, :, :].rearrange("a p n t -> (a p) n t"), yo[:, :, :]).then_inc(sg("y_stored"), 16)

            pool.wait_ge(sg("c_ready"), 1)
            pool.dma_start(c_d, f3[:, :]).then_inc(sg("c_stored"), 16)
            for n in (1, 2, 3):
                sums(n)


    ctx.close()


_INS = ["x", "p", "norm_mix", "w_in", "mu_shift", "w0", "w2", "a0", "a2", "g2", "k_k", "k_a", "r_k", "gn_w", "gn_b",
        "b_f", "q_norm", "k_norm", "w_out", "norm_mlp", "w_ff1", "w_ff2", "norm_ple", "w_ple_gate", "w_ple_proj",
        "norm_final"]


def kernel(**inputs):
    import concourse.bacc as bacc
    from concourse.bass_utils import run_bass_kernel_spmd

    nc = bacc.Bacc("TRN2", target_bir_lowering=False, num_devices=1)
    arrays, args = {}, []
    for name in _INS + ["consts"]:
        a = constants() if name == "consts" else np.ascontiguousarray(inputs[name])
        arrays[f"in_{name}"] = a
        args.append(nc.dram_tensor(f"in_{name}", a.shape, mybir.dt.from_np(a.dtype), kind="ExternalInput").ap())
    args.append(nc.dram_tensor("out", (1, T, D), F32, kind="ExternalOutput").ap())
    build(nc, *args)
    r = run_bass_kernel_spmd(nc, [arrays], core_ids=[0])
    return r.results[0]["out"]
```

```python
import numpy as np
from contextlib import ExitStack

import concourse.bass as bass
from concourse import mybir

F32 = mybir.dt.float32
F32R = mybir.dt.float32r
ALU = mybir.AluOpType
ACT = mybir.ActivationFunctionType
AX = mybir.AxisListType

P = 128
D = 2048
T = 512
KT = D // P
HD = 64
DR = 1024
NPAIR = DR // P
FF = 4 * D
FG = FF // D
DPLE = 256
C = 64
NC = T // C
N_SHIFT = 3 * DR + 64 + 64 + 160
EPS = 1e-6
GN_EPS = 64e-5
UK = KT // 2
NEG = -1e30

Z_TILES = 50
Z_PAIR = 6
Z_COLUMNS = (DR, 0, 2 * DR, N_SHIFT, N_SHIFT + DR, N_SHIFT + 2 * DR)

C_ID, C_ONE, C_MASK, C_LVL = 0, 128, 256, 384
C_BLK, C_HEAD, C_HEADT, C_CAUS = 768, 896, 898, 1026
C_EYE2, C_RESET = 1154, 1218
C_SPREAD = C_RESET + T
C_COLS = C_SPREAD + 4 * P


def constants():
    c = np.zeros((P, C_COLS), np.float32)
    p = np.arange(P)
    j = p % C
    t = np.arange(C)
    c[:, C_ID:C_ID + P] = np.eye(P)
    c[:, C_ONE:C_ONE + P] = 1.0
    c[:, C_MASK:C_MASK + C] = t[None, :] > j[:, None]
    c[:, C_MASK + C:C_MASK + 2 * C] = t[None, :] >= j[:, None]
    for n in range(6):
        b = 1 << n
        c[:, C_LVL + n * C:C_LVL + (n + 1) * C] = (
            (j[:, None] // (2 * b) == t[None, :] // (2 * b)) & (j[:, None] % (2 * b) < b) & (t[None, :] % (2 * b) >= b))
    c[:, C_BLK:C_BLK + P] = (p[:, None] // HD == p[None, :] // HD) / HD
    c[:, C_HEAD:C_HEAD + 2] = p[:, None] // HD == np.arange(2)[None, :]
    c[0:2, C_HEADT:C_HEADT + P] = np.arange(2)[:, None] == p[None, :] // HD
    c[:, C_EYE2:C_EYE2 + C] = t[None, :] == j[:, None]
    c[:, C_CAUS:C_CAUS + P] = np.where(p[:, None] >= p[None, :], 0.0, NEG)
    for s in range(4):
        c[0:8, C_SPREAD + s * P:C_SPREAD + (s + 1) * P] = np.arange(8)[:, None] == 2 * s + p[None, :] // HD
    c[:, C_RESET:C_RESET + T] = np.arange(T)[None, :] % C != 0
    return c




def build(nc, x, p, norm_mix, w_in, mu_shift, w0, w2, a0, a2, g2, k_k, k_a, r_k, gn_w, gn_b, b_f, q_norm,
          k_norm, w_out, norm_mlp, w_ff1, w_ff2, norm_ple, w_ple_gate, w_ple_proj, norm_final, consts, out):
    ctx = ExitStack()
    sems = {}

    def sg(name):
        if name not in sems:
            sems[name] = ctx.enter_context(nc.semaphore(name))
        return sems[name]

    def sb(name, shape, where, dt=F32):
        n = 4
        for s in shape[1:]:
            n *= s
        t = nc.alloc_sbuf_tensor_at(name, shape, dt, offset=where[0])
        where[0] += (n + 63) // 64 * 64
        return t

    top = [(nc.sbuf_base + 63) // 64 * 64]
    a_hi = sb("a_hi", [P, KT, T], top, F32R)
    a_lo = sb("a_lo", [P, KT, T], top, F32R)
    arena = top[0]
    b_hi = sb("b_hi", [P, KT, T], top, F32R)
    b_lo = sb("b_lo", [P, KT, T], top, F32R)
    arena_h = top[0]
    h = sb("h", [P, KT, T], top)
    h_end = top[0]
    w_raw = sb("w_raw", [P, 2, UK, P], top)
    w_hi = sb("w_hi", [P, 2, UK, P], top, F32R)
    w_lo = sb("w_lo", [P, 2, UK, P], top, F32R)
    rstd = sb("rstd", [P, T], top)
    sumsq = sb("sumsq", [P, T], top)
    sq = sb("sq", [P, 2, T], top)
    ev = sb("ev", [P, 2, T], top)
    tmp = sb("tmp", [P, T], top)
    par = sb("par", [P, 160], top)
    cst = sb("cst", [P, C_RESET], top)
    assert top[0] <= nc.sbuf_usable_end, (top[0], nc.sbuf_usable_end)

    def const(c, n, parts=slice(0, P)):
        return cst[parts, c:c + n]

    ident, ones, eye2 = const(C_ID, P), const(C_ONE, P), const(C_EYE2, C)
    head_of = const(C_HEAD, 2)

    acc = [nc.alloc_psum_tensor(f"acc{i}", [P, T], F32) for i in range(2)]
    bank = [nc.alloc_psum_tensor(f"bank{i}", [P, T], F32) for i in range(6)]

    def dram(name, shape):
        return nc.dram_tensor(name, shape, F32, kind="Internal").ap()

    z_d = dram("z_d", (Z_TILES, P, T))
    zo_d = dram("zo_d", (48, T))
    h_d = dram("h_d", (KT, P, T))
    ab_d = dram("ab_d", (NC, P, NPAIR, 4, C))
    v_d = dram("v_d", (NC, P, NPAIR, C))
    bonus_d = dram("bonus_d", (NPAIR, P, T))
    fox_d = dram("fox_d", (NPAIR, P, T))
    c_d = dram("c_d", (2 * NPAIR, T))
    h_v = h_d.rearrange("k p t -> p k t")

    rows = [("norm_mix", norm_mix, 16), ("norm_mlp", norm_mlp, 16), ("norm_ple", norm_ple, 16),
            ("norm_final", norm_final, 16), ("w0", w0, 8), ("a0", a0, 8), ("k_k", k_k, 8), ("k_a", k_a, 8),
            ("r_k", r_k, 8), ("gn_w", gn_w, 8), ("gn_b", gn_b, 8)]
    col = {"q_norm": 120, "k_norm": 121, "mu": P}
    for n, row in enumerate(rows):
        col[row[0]] = sum(r[2] for r in rows[:n])
    N_PAR = len(rows) + 4 + 2

    def pc(name, i=0):
        return par[:, bass.ds(col[name] + i, 1)]

    def flat(a):
        if len(a.shape) == 3:
            a = a.rearrange("a h d -> a (h d)")
        return a.rearrange("(a n) -> a n", a=1) if len(a.shape) == 1 else a

    def w_view(w):
        return w.rearrange("a (k p) n -> p (a k) n", p=P)

    w_in_v, w_out_v, ff1_v, ff2_v, gate_v = (w_view(w) for w in (w_in, w_out, w_ff1, w_ff2, w_ple_gate))
    ple_v = w_view(w_ple_proj)

    at = [arena]
    xin = sb("xin", [P, 2, T // P, P], at)
    prow = sb("prow", [P, 2, P], at)
    at = [arena]
    kin = sb("kin", [P, T + 1], at)
    rin = sb("rin", [P, T + 1], at)
    vin = sb("vin", [P, T + 1], at)
    reset = sb("reset", [P, T], at)
    spread = sb("spread", [6, 3, P], at)
    wa_in = sb("wa_in", [P, P], at)
    dif = sb("dif", [P, T], at)
    ks = sb("ks", [P, T], at)
    rs = sb("rs", [P, T], at)
    vs = sb("vs", [P, T], at)
    lw = sb("lw", [P, T], at)
    cum = sb("cum", [P, T], at)
    cex = sb("cex", [P, T], at)
    av = sb("av", [P, T], at)
    e_in = sb("e_in", [P, T], at)
    e_ex = sb("e_ex", [P, T], at)
    e_no = sb("e_no", [P, T], at)
    kkr = sb("kkr", [P, T], at)
    kk = sb("kk", [P, T], at)
    km = sb("km", [P, T], at)
    t1 = sb("t1", [P, T], at)
    t2 = sb("t2", [P, T], at)
    ab = sb("ab", [P, NC, 4, C], at)
    bon = sb("bon", [P, T], at)
    cq = sb("cq", [P, T // P, 16], at)
    qin = sb("qin", [P, T], at)
    k_in = sb("k_in", [P, T], at)
    v_in = sb("v_in", [P, T], at)
    qh = sb("qh", [P, T], at)
    kh = sb("kh", [P, T], at)
    vtm = sb("vtm", [P, T // P, P], at)
    ncb = sb("ncb", [P, 2, T], at)
    mx = sb("mx", [P, 4], at)
    nmx = sb("nmx", [P, 4], at)
    rsum = sb("rsum", [P, 4], at)
    rinv = sb("rinv", [P, 4], at)
    og = sb("og", [P, T], at)
    once = at[0]
    pr = sb("pr", [P, T // P, T], at)
    prt = sb("prt", [P, T // P, T], at)
    side_end = at[0]
    at = [once]
    xin_wa = sb("xin_wa", [P, T + 1], at)
    xin_g = sb("xin_g", [P, T + 1], at)
    xin_h = sb("xin_h", [32, T + 1], at)
    fin = sb("fin", [16, T], at)
    f1 = sb("f1", [16, T], at)
    f2 = sb("f2", [16, T], at)
    f3 = sb("f3", [16, T], at)
    bf = sb("bf", [16, 1], at)
    assert at[0] <= side_end
    at = [(nc.sbuf_base + 63) // 64 * 64]
    loads = [[sb(f"{name}{b}", [P, NPAIR, 2, C], at) for name in ("abd", "bbd", "kbd", "vbd", "ars")] for b in range(2)]
    mbd = sb("mbd", [P, NPAIR, 2, C], at)
    nbd = sb("nbd", [P, 2, NPAIR, 2, C], at)
    xbd = sb("xbd", [P, NPAIR, 2, C], at)
    ptbd = sb("ptbd", [P, NPAIR, 2, C], at)
    sabd = sb("sabd", [P, NPAIR, 2, C], at)
    assert at[0] <= arena
    at = [arena]
    st = sb("st", [P, NPAIR, C], at)
    stbd = sb("stbd", [P, NPAIR, 2, C], at)
    after_state = at[0]
    y_all = sb("y_all", [P, NPAIR, T], at)
    yb = sb("yb", [P, NPAIR, T], at)
    g2a = sb("g2a", [P, DR], at)
    g2b = sb("g2b", [32, DR], at)
    after_y = at[0]
    gb = sb("gb", [P, NPAIR, 2, C], at)
    gk = sb("gk", [P, NPAIR, 2, C], at)
    xs = sb("xs", [P, NPAIR, C], at)
    xt = sb("xt", [P, NPAIR, C], at)
    pt = sb("pt", [P, NPAIR, C], at)
    bt = sb("bt", [P, NPAIR, P], at)
    ktm = sb("ktm", [P, NPAIR, P], at)
    vt = sb("vt", [P, NPAIR, P], at)
    vst = sb("vst", [P, NPAIR, C], at)
    rr = sb("rr", [P, NPAIR, C], at)
    sa = sb("sa", [P, NPAIR, C], at)
    sn = sb("sn", [P, NPAIR, C], at)
    assert at[0] <= h_end, at[0] - h_end
    diagonals = [t[:, :, :, :] for b in range(2) for t in loads[b][:4]] + [t[:, :, :, :] for t in (mbd, xbd, ptbd, sabd)] + [
        nbd[:, 0, :, :, :], nbd[:, 1, :, :, :], stbd[:, :, :, :], st[:, :, :]]
    N_CLEAR = len(diagonals)
    H = NPAIR // 2
    gbank = [bank[0:4], acc + bank[4:6]]
    pairs = [slice(g * H, (g + 1) * H) for g in range(2)]

    def flat2(t):
        return t.rearrange("p a t -> p (a t)")

    def m3(b, n=NPAIR):
        return b.rearrange("p (n t) -> p n t", n=n)

    def half(g, k, parts=slice(0, P)):
        return m3(gbank[g][k][parts, 0:H * C], H)

    keep = [h_end - 3 * 2048 - 256 - 2048]
    tx = sb("tx", [P, T], keep)
    sga = sb("sga", [P, T], keep)
    sgb = sb("sgb", [32, T], keep)
    ec = sb("ec", [P, NPAIR, NC], keep)
    assert side_end <= h_end - 3 * 2048 - 256 - 2048, side_end - h_end
    assert keep[0] <= h_end and at[0] <= h_end - 3 * 2048 - 256 - 2048, (at[0], h_end)
    at = [arena]
    spread4 = sb("spread4", [8, 4, P], at)
    assert at[0] <= after_state
    at = [after_y]
    yf = sb("yf", [P, NPAIR, T], at)
    assert at[0] <= arena_h
    NB = 4
    gate_banks = [bank[4], acc[0], acc[1], bank[5]]
    squares = [sq[:, 0, :], sq[:, 1, :], ev[:, 0, :], ev[:, 1, :]]
    at = [(nc.sbuf_base + 63) // 64 * 64]
    p_in = sb("p_in", [P, T // P, DPLE], at)
    p_hi = sb("p_hi", [P, 2, T], at, F32R)
    p_lo = sb("p_lo", [P, 2, T], at, F32R)
    pw = sb("pw", [P, 2, 2, P], at)
    pw_hi = sb("pw_hi", [P, 2, 2, P], at, F32R)
    pw_lo = sb("pw_lo", [P, 2, 2, P], at, F32R)
    p_t = sb("p_t", [P, 2, T], at)
    gt = sb("gt", [P, 2, T], at)
    hn = sb("hn", [P, 2, T], at)
    ot = sb("ot", [P, 2, T // P, P], at)
    hs = sb("hs", [P, 32], top)
    hr = sb("hr", [P, 32], top)
    hrt = sb("hrt", [8, T], top)
    qs = sb("qs", [P, 1], top)
    assert top[0] <= nc.sbuf_usable_end, (top[0], nc.sbuf_usable_end)

    Z_ODD = 2
    M_OUT = Z_TILES
    M_FF = M_OUT + KT
    M_GATE = M_FF + FG * 2 * KT
    M_END = M_GATE + KT


    logit_banks = [bank[2][:, 0:P], bank[2][:, P:3 * P], bank[3][:, 0:3 * P], bank[4][:, :]]
    prob_banks = [bank[0][:, :], bank[5][:, P:], bank[2][:, 0:2 * P], bank[5][:, 0:P]]

    with nc.Block() as block:

        @block.sync
        def _(sp):
            def unit(slot, src, n):
                sp.wait_ge(sg("w_split"), n + 1)
                sp.dma_start(w_raw[:, slot, :, :], src).then_inc(sg(f"w_landed{slot}"), 16)

            def stream(view, row, column, m, tiles, outer=0):
                with sp.Fori(0, tiles // 2) as i:
                    for b in range(2):
                        for s in range(2):
                            unit(s, view[:, row + s * UK:row + (s + 1) * UK, bass.ds(i * (2 * P) + (column + b * P), P)],
                                 i * 4 + outer + Z_ODD + 2 * m + 2 * b + s)

            sp.dma_start(cst[:, :], consts[:, 0:C_RESET]).then_inc(sg("constants_landed"), 16)
            sp.wait_ge(sg("rows_cleared"), 1)
            for name, a, n in rows:
                sp.dma_start(prow[col[name]:col[name] + n, 0, :],
                             flat(a).rearrange("a (n q) -> (a n) q", q=P)).then_inc(sg("parameters_landed"), 16)
            for k, a in enumerate((q_norm, k_norm)):
                for half in range(2):
                    sp.dma_start(prow[120 + k:121 + k, 0, half * HD:(half + 1) * HD], a).then_inc(sg("parameters_landed"), 16)
            sp.dma_start(prow[0:26, 1, :], mu_shift[0, 0:26 * P].rearrange("(n q) -> n q", q=P)).then_inc(sg("parameters_landed"), 16)
            sp.dma_start(prow[26:27, 1, 0:32], mu_shift[0:1, 26 * P:N_SHIFT]).then_inc(sg("parameters_landed"), 16)
            x_v = x.rearrange("a (b q) n -> q (a b) n", q=P)
            with sp.Fori(0, KT // 2) as i:
                for b in range(2):
                    sp.wait_ge(sg("x_transposed"), 2 * i + b + 1)
                    sp.dma_start(xin[:, b, :, :], x_v[:, :, bass.ds(i * (2 * P) + b * P, P)]).then_inc(sg(f"x_landed{b}"), 16)
            for s in range(2):
                r = slice(s * UK, (s + 1) * UK)
                sp.wait_ge(sg("w_split"), s + 1)
                sp.dma_start(w_raw[:, s, :, 0:32], w_in_v[:, r, N_SHIFT - 32:N_SHIFT]).then_inc(sg(f"w_landed{s}"), 16)
                sp.dma_start(w_raw[:, s, :, 32:48], w_in_v[:, r, N_SHIFT + 3 * DR:N_SHIFT + 3 * DR + 16]).then_inc(sg(f"w_landed{s}"), 16)
            stream(w_in_v, 0, 3 * DR, 0, 2)

            def pair_units(i, m, t):
                for s in range(2):
                    unit(s, w_in_v[:, s * UK:(s + 1) * UK, bass.ds(i * P + (Z_COLUMNS[t] + (m - 2) // Z_PAIR * P), P)],
                         i * (2 * Z_PAIR) + (Z_ODD + 2 * m + s))

            def load_pair(i):
                sp.wait_ge(sg("ev_free0"), i * 48 + 80)
                sp.sem_inc(sg("sp_waits_taken"), 1)
                sp.wait_ge(sg("ev_free1"), i * 48 + 64)
                sp.sem_inc(sg("sp_waits_taken"), 1)
                sp.wait_ge(sg("side_inputs_used"), i + 1)
                for t, dst in enumerate((kin, rin, vin, qin, k_in)):
                    dst = dst[:, 1:] if t < 3 else dst[:, :]
                    sp.dma_start(dst, z_d[bass.ds(i * Z_PAIR + (2 + t), 1), :, :].rearrange("a p t -> (a p) t")).then_inc(sg("side_landed"), 16)
                sp.dma_start(wa_in[0:64, :], w2[0, :, bass.ds(i * P, P)]).then_inc(sg("side_landed"), 16)
                sp.dma_start(wa_in[64:128, :], a2[0, :, bass.ds(i * P, P)]).then_inc(sg("side_landed"), 16)
                sp.wait_ge(sg("c_stored"), 16)
                for k in range(2):
                    sp.dma_start(ncb[:, k, :], c_d[bass.ds(i * 2 + k, 1), :].broadcast_to([P, T])).then_inc(sg("side_landed"), 16)

            def load_fox_v(i):
                sp.wait_ge(sg("ev_free1"), i * 48 + 80)
                sp.dma_start(v_in[:, :], z_d[bass.ds(i * Z_PAIR + 7, 1), :, :].rearrange("a p t -> (a p) t")).then_inc(sg("fv_landed"), 16)

            pair_units(0, 2, 0)
            for b in range(2):
                sp.wait_ge(sg(f"ev_free{b}"), 32)
            sp.wait_ge(sg("operand_split"), KT)
            sp.wait_ge(sg("h_stored"), 64)
            for dst, src in ((xin_wa[:, 1:], z_d[0]), (xin_g[:, 1:], z_d[1]), (xin_h[:, 1:], zo_d[0:32, :]),
                             (reset[:, :], consts[:, C_RESET:C_RESET + T]),
                             (spread[:, :, :], consts[0:6, C_SPREAD:C_SPREAD + 3 * P].rearrange("p (s n) -> p s n", s=3)),
                             (fin[:, :], zo_d[32:48, :]), (bf[:, :], b_f.rearrange("a n -> n a"))):
                sp.dma_start(dst, src).then_inc(sg("once_landed"), 16)
            for t in range(1, Z_PAIR):
                pair_units(0, 2 + t, t)
            with sp.Fori(0, NPAIR - 1) as i:
                for t in range(Z_PAIR):
                    pair_units(i, 2 + Z_PAIR + t, t)
                    if t == 0:
                        load_pair(i)
                    if t == 1:
                        load_fox_v(i)
            for s in range(2):
                unit(s, w_out_v[:, s * UK:(s + 1) * UK, 0:P], Z_ODD + 2 * M_OUT + s)
            load_pair(NPAIR - 1)
            load_fox_v(NPAIR - 1)

            sp.wait_ge(sg("features_stored"), 48 * NPAIR + 48)
            sp.wait_ge(sg("diagonals_cleared"), N_CLEAR)

            def load_chunk(b, n, j=0):
                chunk = bass.ds(j * 2 + n, 1)
                a, be, ka, v, ar = loads[b]
                for hf in range(2):
                    ph = slice(hf * HD, (hf + 1) * HD)
                    for dst, kind in ((a, 0), (be, 2), (ka, 3)):
                        sp.dma_start(dst[ph, :, hf, :], ab_d[chunk, ph, :, kind, :].rearrange("a p n t -> (a p) n t")).then_inc(sg(f"chunk_landed{b}"), 16)
                    sp.dma_start(v[ph, :, hf, :], v_d[chunk, ph, :, :].rearrange("a p n t -> (a p) n t")).then_inc(sg(f"chunk_landed{b}"), 16)
                sp.dma_start(ar[:, :, :, :], ab_d[chunk, :, :, 0:2, :].rearrange("a p n k t -> (a p) n k t")).then_inc(sg(f"chunk_landed{b}"), 16)

            load_chunk(0, 0)
            load_chunk(1, 1)
            sp.wait_ge(sg("fox_stored"), 16 * NPAIR + 16)
            for k in range(4):
                sp.dma_start(yb[:, 2 * k:2 * k + 2, :], bonus_d[2 * k:2 * k + 2, :, :].rearrange("n p t -> p n t")).then_inc(sg("output_landed"), 16)
            sp.dma_start(g2a[:, :], g2[0, 0:P, :]).then_inc(sg("output_landed"), 16)
            sp.dma_start(g2b[:, :], g2[0, P:P + 32, :]).then_inc(sg("output_landed"), 16)
            with sp.Fori(0, NC // 2 - 1) as j:
                for b in range(2):
                    sp.wait_ge(sg("y_multiplied"), j * 4 + (2 * b + 4))
                    load_chunk(b, b + 2, j)

            sp.wait_ge(sg("y_taken"), 2 * NC + 2)
            sp.wait_ge(sg("state_ready"), 2 * NC + 2)
            sp.wait_ge(sg("state_bd_ready_a"), 2 * NC + 2)
            sp.wait_ge(sg("state_bd_ready_b"), 2 * NC + 2)
            sp.dma_start(spread4[:, :, :], consts[0:8, C_SPREAD:C_SPREAD + 4 * P].rearrange("p (s n) -> p s n", s=4)).then_inc(sg("output_landed"), 16)
            for k in range(4):
                sp.dma_start(yf[:, 2 * k:2 * k + 2, :], fox_d[2 * k:2 * k + 2, :, :].rearrange("n p t -> p n t")).then_inc(sg("output_landed"), 16)

            for k in range(4):
                if k == 2:
                    for hf in range(2):
                        unit(hf, w_out_v[:, hf * UK:(hf + 1) * UK, P:2 * P], Z_ODD + 2 * M_OUT + 2 + hf)
                    sp.wait_ge(sg("gates_done"), NPAIR)
                sp.dma_start(h[:, 4 * k:4 * k + 4, :], h_v[:, 4 * k:4 * k + 4, :]).then_inc(sg("h_landed"), 16)
            stream(w_out_v, 0, 2 * P, M_OUT + 2, KT - 2)
            with sp.Fori(0, FG) as g:
                for view, m0, row, cc in ((ff1_v, 0, 0, D), (ff2_v, KT, KT, 0)):
                    with sp.Fori(0, KT // 2) as i:
                        for b in range(2):
                            for s in range(2):
                                r0 = s * UK
                                src = (view[:, r0:r0 + UK, bass.ds(g * D + i * (2 * P) + b * P, P)] if cc else
                                       view[:, bass.ds(g * KT + r0, UK), bass.ds(i * (2 * P) + b * P, P)])
                                unit(s, src, g * (4 * KT) + i * 4 + (Z_ODD + 2 * (M_FF + m0) + 2 * b + s))
            def gate_units(n, i=0):
                for s in range(2):
                    unit(s, gate_v[:, s * UK:(s + 1) * UK, bass.ds(i * (2 * P) + n * P, P)], i * 4 + (Z_ODD + 2 * (M_GATE + n) + s))

            gate_units(0)
            sp.wait_ge(sg("unit_done"), 2 + Z_ODD + 2 * M_GATE)
            sp.dma_start(p_in[:, :, :], p.rearrange("l a (b q) n -> q (l a b) n", q=P)).then_inc(sg("p_landed"), 16)

            def ple_weights(b, c0, n):
                sp.wait_ge(sg("ple_split"), n + 1)
                sp.dma_start(pw[:, b, :, :], ple_v[:, :, bass.ds(c0, P)]).then_inc(sg(f"ple_landed{b}"), 16)

            ple_weights(0, 0, 0)
            ple_weights(1, P, 1)
            gate_units(1)
            with sp.Fori(0, KT // 2 - 1) as i:
                for b in range(2):
                    ple_weights(b, i * (2 * P) + (b + 2) * P, 2 * i + (b + 2))
                    gate_units(b + 2, i)
            o_v = out.rearrange("a (b q) n -> q (a b) n", q=P)
            with sp.Fori(0, KT // 2) as i:
                for b in range(2):
                    sp.wait_ge(sg("out_ready"), 2 * i + b + 3)
                    sp.dma_start(o_v[:, :, bass.ds(i * (2 * P) + b * P, P)], ot[:, b, :, :]).then_inc(sg(f"out_stored{b}"), 16)
            for b in range(2):
                sp.wait_ge(sg(f"out_stored{b}"), 16 * (KT // 2))

        @block.tensor
        def _(pe):
            pe.sem_inc(sg("unit_done"), 2)
            pe.sem_inc(sg("x_transposed"), 2)
            pe.sem_inc(sg("ple_done"), 2)
            pe.sem_inc(sg("final_transposed"), 2)
            pe.sem_inc(sg("y_multiplied"), 2)

            mm = nc.tensor.matmul

            def gemm(dst, hi, lo, n, width=P, ready=None, beside=None):
                for s in range(2):
                    pe.wait_ge(sg("w_split"), n + s + 3)
                    for k in range(UK):
                        kt = s * UK + k
                        if ready is not None and k == 0:
                            pe.wait_ge(sg("operand_split"), ready + (UK if s == 0 else KT))
                        wh, wl = w_hi[:, s, k, 0:width], w_lo[:, s, k, 0:width]
                        mm(dst, wh, hi[:, kt, :], start=kt == 0, stop=False)
                        mm(dst, wh, lo[:, kt, :], start=False, stop=False)
                        last = mm(dst, wl, hi[:, kt, :], start=False, stop=kt == KT - 1)
                        if k == UK - 1:
                            last.then_inc(sg("unit_done"), 1)
                        if beside and k % (UK // 2) == UK // 2 - 1:
                            beside(s + (k + 1) / UK)

            def tiles(m, count, hi, lo, ready=None, outer=0, after=None):
                with pe.Fori(0, count // 2) as i:
                    for b in range(2):
                        pe.wait_ge(sg("acc_taken"), i * 2 + outer + (m + b + 1))
                        gemm(acc[b][:, :], hi, lo, i * 4 + outer * 2 + (Z_ODD + 2 * m + 2 * b), ready=ready)
                        if after:
                            after(i, b)

            def spread_sumsq(n):
                pe.wait_ge(sg("squares_summed"), 2 + KT * (n + 1))
                mm(bank[3][:, :], ones, sumsq[:, :], start=True, stop=True).then_inc(sg("sumsq_spread"), 1)

            pe.wait_ge(sg("constants_landed"), 16)
            pe.wait_ge(sg("parameters_landed"), 16 * N_PAR)
            for k in range(2):
                last = nc.tensor.transpose(bank[0][:, k * P:(k + 1) * P], prow[:, k, :], ident)
            last.then_inc(sg("parameters_transposed"), 1)
            with pe.Fori(0, KT // 2) as i:
                for b in range(2):
                    pe.wait_ge(sg(f"x_landed{b}"), 16 * i + 16)
                    if b == 0:
                        pe.wait_ge(sg("parameters_ready"), 1)
                    pe.wait_ge(sg("xt_taken"), 2 * i + b + 1)
                    for q in range(T // P):
                        last = nc.tensor.transpose(bank[1 + b][:, q * P:(q + 1) * P], xin[:, b, q, :], ident)
                    last.then_inc(sg("x_transposed"), 1)
            gemm(bank[0][0:48, :], a_hi, a_lo, 0, width=48, ready=0)
            spread_sumsq(0)
            tiles(0, 2, a_hi, a_lo)

            def pair_tiles(i, m, beside):
                for t in range(Z_PAIR):
                    pe.wait_ge(sg("acc_taken"), i * Z_PAIR + (m + t + 1))
                    gemm(acc[t % 2][:, :], a_hi, a_lo, i * (2 * Z_PAIR) + (Z_ODD + 2 * (m + t)), beside=lambda u: beside(i, 2 * t + u))

            def once(i, at):
                if at == 8:
                    pe.wait_ge(sg("f_cumulated"), 1)
                    for q in range(T // P):
                        last = mm(bank[0][:, q * 16:(q + 1) * 16], f1[:, q * P:(q + 1) * P], ident[0:16, 0:16], start=True, stop=True)
                    last.then_inc(sg("c_transposed"), 1)

            def logits(i, k):
                ph = slice(k * HD, (k + 1) * HD)
                for q, dst in enumerate(logit_banks):
                    mm(dst, qh[ph, q * P:(q + 1) * P], kh[ph, 0:(q + 1) * P], start=True, stop=True).then_inc(sg("logits_done"), 1)

            def transpose_probs(i, k):
                pe.wait_ge(sg("probs_ready"), i * 2 + (k + 1))
                for j, dst in enumerate(prob_banks):
                    for q in range(j, T // P):
                        last = nc.tensor.transpose(dst[:, (q - j) * P:(q - j + 1) * P], pr[:, q, j * P:(j + 1) * P], ident)
                last.then_inc(sg("probs_t_done"), 1)

            def weigh_values(i, k):
                ph = slice(k * HD, (k + 1) * HD)
                pe.wait_ge(sg("probs_t_taken"), i * 2 + (k + 1))
                for j in range(T // P):
                    last = mm(bank[1][ph, j * P:], vtm[:, j, ph], prt[:, j, j * P:], start=j == 0, stop=j == T // P - 1)
                last.then_inc(sg("heads_done"), 1)

            def side(i, at):
                if at == 2:
                    pe.wait_ge(sg("side_landed"), i * 144 + 144)
                    pe.wait_ge(sg("fox_taken"), i + 1)
                    mm(bank[0][:, :], wa_in[0:64, :], tx[0:64, :], start=True, stop=True)
                    mm(bank[1][:, :], wa_in[64:128, :], tx[64:128, :], start=True, stop=True).then_inc(sg("lora_multiplied"), 1)
                    pe.wait_ge(sg("k_squares_ready"), i + 1)
                    pe.wait_ge(sg("qk_squares_ready"), i * 2 + 2)
                    for q in range(T // P):
                        for n, src in enumerate((t1[:, :], sq[:, 0, :], sq[:, 1, :])):
                            last = mm(bank[5][:, 6 * q + 2 * n:6 * q + 2 * n + 2], src[:, q * P:(q + 1) * P], head_of, start=True, stop=True)
                    last.then_inc(sg("head_sums_done"), 1)
                if at == 3:
                    pe.wait_ge(sg("head_inverse_ready"), i + 1)
                    for q in range(T // P):
                        last = mm(bank[5][0:6, q * P:(q + 1) * P], hr[:, 6 * q:6 * q + 6], ident, start=True, stop=True)
                    last.then_inc(sg("head_rows_done"), 1)
                if at == 4:
                    pe.wait_ge(sg("head_rows_ready"), i + 1)
                    for n in range(3):
                        last = mm(bank[2 + n][:, :], spread[:, n, :], hrt[0:6, :], start=True, stop=True)
                    last.then_inc(sg("head_spread"), 1)
                if at == 5:
                    pe.wait_ge(sg("qk_ready"), i * 3 + 3)
                    logits(i, 0)
                    pe.wait_ge(sg("fv_landed"), i * 16 + 16)
                    for q in range(T // P):
                        last = nc.tensor.transpose(bank[0][:, q * P:(q + 1) * P], v_in[:, q * P:(q + 1) * P], ident)
                    last.then_inc(sg("fv_done"), 1)
                if at == 7:
                    pe.wait_ge(sg("rk_ready"), i + 1)
                    mm(bank[1][:, :], const(C_BLK, P), t2[:, :], start=True, stop=True).then_inc(sg("bonus_summed"), 1)
                if at == 7.5:
                    pe.wait_ge(sg("fv_ready"), i + 1)
                    transpose_probs(i, 0)
                if at == 8:
                    pe.wait_ge(sg("bonus_taken"), i + 1)
                    weigh_values(i, 0)
                    logits(i, 1)
                if at == 10.5:
                    transpose_probs(i, 1)
                if at == 11.5:
                    weigh_values(i, 1)

            pair_tiles(0, 2, once)
            with pe.Fori(0, NPAIR - 1) as i:
                pair_tiles(i, 2 + Z_PAIR, side)
            for at in (2, 3, 4, 5, 7, 7.5, 8, 10.5, 11.5):
                side(NPAIR - 1, at)

            pe.wait_ge(sg("diagonals_cleared"), N_CLEAR)
            pe.wait_ge(sg("fox_taken"), NPAIR + 1)

            def each(g, dst, lhs, rhs, sem):
                for n in range(H):
                    last = mm(m3(dst, H)[:, n, :], lhs(g * H + n), rhs(g * H + n), start=True, stop=True)
                last.then_inc(sg(sem), 1)

            def chunk(j, b):
                abd, bbd, kbd, vbd, ars = loads[b]

                def wait(name, g, n, k):
                    pe.wait_ge(sg(name), j * (4 * n) + (2 * (b * n + k) - 1 + g))

                pe.wait_ge(sg(f"chunk_landed{b}"), 144 * j + 144)
                for k, src in enumerate((bbd, kbd)):
                    for g in range(2):
                        each(g, gbank[g][k][:, :], lambda n: flat2(src[:, n, :, :]), lambda n: flat2(ars[:, n, :, :]), "products_done")
                for k, src, free in ((2, bbd, "state_ready"), (3, kbd, "y_taken"), (0, vbd, "products_ready")):
                    for g in range(2):
                        if k:
                            wait(free, g, 1, 1)
                        else:
                            wait(free, g, 2, 1)
                        for n in range(H):
                            last = nc.tensor.transpose(gbank[g][k][:, n * P:(n + 1) * P], flat2(src[:, g * H + n, :, :]), ident)
                        last.then_inc(sg("transposes_done"), 1)
                for g in range(2):
                    wait("products_ready", g, 2, 2)
                    wait("x_bd_ready", g, 6, 1)
                    each(g, gbank[g][1][:, 0:H * C], lambda n: flat2(xbd[:, n, :, :]), lambda n: eye2, "xt0_done")
                for lv in range(1, 6):
                    for g in range(2):
                        wait("n_ready", g, 5, lv)
                        wait("xt_ready", g, 5, lv)
                        each(g, gbank[g][1][:, 0:H * C], lambda n: flat2(nbd[:, lv % 2, n, :, :]), lambda n: xt[:, n, :], "pt_done")
                    for g in range(2):
                        if lv == 1:
                            wait("transposes_taken", g, 3, 1)
                        wait("pt_ready_a", g, 5, lv)
                        wait("pt_ready_b", g, 5, lv)
                        each(g, gbank[g][2][:, 0:H * C], lambda n: flat2(ptbd[:, n, :, :]), lambda n: xs[:, n, :], "dx_done")
                    if lv < 5:
                        for g in range(2):
                            if lv == 1:
                                wait("transposes_taken", g, 3, 2)
                            wait("x_bd_ready", g, 6, lv)
                            each(g, gbank[g][3][:, 0:H * C], lambda n: flat2(xbd[:, n, :, :]), lambda n: pt[:, n, :], "dxt_done")
                for g in range(2):
                    wait("m_ready", g, 1, 1)
                    wait("v_stacked", g, 1, 1)
                    wait("state_ready", g, 1, 1)
                    for n in range(g * H, (g + 1) * H):
                        o = half(g, 0)[:, n % H, :]
                        mm(o, flat2(abd[:, n, :, :]), st[:, n, :], start=True, stop=False)
                        last = mm(o, flat2(mbd[:, n, :, :]), vst[:, n, :], start=False, stop=True)
                    last.then_inc(sg("r_done"), 1)
                for g in range(2):
                    wait("r_ready", g, 1, 1)
                    wait("x_bd_ready", g, 6, 6)
                    each(g, gbank[g][1][:, 0:H * C], lambda n: flat2(xbd[:, n, :, :]), lambda n: rr[:, n, :], "sa_done")
                for g in range(2):
                    wait("sa_ready_a", g, 1, 1)
                    wait("sa_ready_b", g, 1, 1)
                    for n in range(g * H, (g + 1) * H):
                        o = half(g, 2)[:, n % H, :]
                        mm(o, bt[:, n, :], sa[:, n, :], start=True, stop=False)
                        last = mm(o, ktm[:, n, :], vst[:, n, :], start=False, stop=True)
                    last.then_inc(sg("s_done"), 1)
                for g in range(2):
                    wait("state_bd_ready_a", g, 1, 1)
                    wait("state_bd_ready_b", g, 1, 1)
                    for n in range(g * H, (g + 1) * H):
                        o = half(g, 3)[:, n % H, :]
                        mm(o, flat2(stbd[:, n, :, :]), ars[:, n, 1, :], start=True, stop=False)
                        mm(o, flat2(sabd[:, n, :, :]), gb[:, n, 1, :], start=False, stop=False)
                        last = mm(o, vt[:, n, :], gk[:, n, 1, :], start=False, stop=True)
                    last.then_inc(sg("y_multiplied"), 1)

            with pe.Fori(0, NC // 2) as j:
                for b in range(2):
                    chunk(j, b)

            pe.wait_ge(sg("output_landed"), 16 * 6)
            pe.wait_ge(sg("y_taken"), 2 * NC + 2)
            for i in range(NPAIR // NB):
                for n in range(NB):
                    if i:
                        pe.wait_ge(sg("y_scaled"), NB * (i - 1) + n + 1)
                    mm(bank[n][:, :], const(C_BLK, P), y_all[:, NB * i + n, :], start=True, stop=True).then_inc(sg("mean_done"), 1)

                def gate(n):
                    if i:
                        pe.wait_ge(sg("y_finished"), NB * (i - 1) + n + 1)
                    else:
                        pe.wait_ge(sg("state_ready"), 2 * NC + 2)
                    f = slice((NB * i + n) * P, (NB * i + n + 1) * P)
                    mm(gate_banks[n][:, :], g2a[:, f], sga[:, :], start=True, stop=False)
                    mm(gate_banks[n][:, :], g2b[:, f], sgb[:, :], start=False, stop=True).then_inc(sg("gates_done"), 1)

                for n in range(NB - 1):
                    gate(n)
                if i:
                    pe.wait_ge(sg("y_finished"), NB * i)
                for n in range(NB):
                    pe.wait_ge(sg("y_squares_ready"), NB * i + n + 1)
                    for q in range(T // P):
                        last = mm(bank[5][:, 8 * q + 2 * n:8 * q + 2 * n + 2], squares[n][:, q * P:(q + 1) * P], head_of, start=True, stop=True)
                last.then_inc(sg("head_sums_done"), 1)
                pe.wait_ge(sg("head_inverse_ready"), NPAIR + i + 1)
                for q in range(T // P):
                    last = mm(bank[5][0:8, q * P:(q + 1) * P], hr[:, 8 * q:8 * q + 8], ident, start=True, stop=True)
                last.then_inc(sg("head_rows_done"), 1)
                pe.wait_ge(sg("head_rows_ready"), NPAIR + i + 1)
                pe.wait_ge(sg("output_landed"), 16 * 11)
                for n in range(NB):
                    mm(bank[n][:, :], spread4[:, n, :], hrt[:, :], start=True, stop=True).then_inc(sg("head_spread"), 1)
                gate(NB - 1)

            pe.wait_ge(sg("operand_split"), 2 * KT)
            tiles(M_OUT, KT, a_hi, a_lo)
            spread_sumsq(1)
            with pe.Fori(0, FG) as g:
                tiles(M_FF, KT, b_hi, b_lo, ready=2 * KT, outer=g * (2 * KT))
                tiles(M_FF + KT, KT, a_hi, a_lo, ready=g * KT + 3 * KT, outer=g * (2 * KT))
            spread_sumsq(2)

            pe.wait_ge(sg("p_landed"), 16)
            for k in range(2):
                for q in range(T // P):
                    last = nc.tensor.transpose(bank[k][:, q * P:(q + 1) * P], p_in[:, q, k * P:(k + 1) * P], ident)
            last.then_inc(sg("p_transposed"), 1)
            pe.wait_ge(sg("p_split"), 1)

            def embed(i, b):
                pe.wait_ge(sg("ple_split"), 2 * i + b + 3)
                pe.wait_ge(sg("ple_taken"), 2 * i + b + 1)
                for k in range(2):
                    mm(bank[b][:, :], pw_hi[:, b, k, :], p_hi[:, k, :], start=k == 0, stop=False)
                    mm(bank[b][:, :], pw_hi[:, b, k, :], p_lo[:, k, :], start=False, stop=False)
                    last = mm(bank[b][:, :], pw_lo[:, b, k, :], p_hi[:, k, :], start=False, stop=k == 1)
                last.then_inc(sg("ple_done"), 1)

            tiles(M_GATE, KT, b_hi, b_lo, ready=(3 + FG) * KT, after=embed)
            spread_sumsq(3)
            with pe.Fori(0, KT // 2) as i:
                for b in range(2):
                    pe.wait_ge(sg("final_ready"), 2 * i + b + 1)
                    pe.wait_ge(sg("out_ready"), 2 * i + b + 1)
                    for q in range(T // P):
                        last = nc.tensor.transpose(bank[4 + b][:, q * P:(q + 1) * P], hn[:, b, q * P:(q + 1) * P], ident)
                    last.then_inc(sg("final_transposed"), 1)

        @block.scalar
        def _(act):
            act.sem_inc(sg("xt_taken"), 2)
            act.sem_inc(sg("y_taken"), 2)
            act.sem_inc(sg("state_bd_ready_a"), 2)
            act.sem_inc(sg("fox_taken"), 1)
            act.sem_inc(sg("fox_stored"), 16)
            act.sem_inc(sg("features_stored"), 48)
            act.sem_inc(sg("out_ready"), 2)
            A = nc.scalar.activation

            def settled():
                act.sem_inc(sg("act_waits_taken"), 1)

            def hi_unit(s, i, m, outer=0, a_turn=2):
                act.wait_ge(sg(f"w_landed{s}"), i * (16 * a_turn) + outer * 16 + 16 * (m + 3))
                act.wait_ge(sg("unit_done"), i * (2 * a_turn) + outer * 2 + (Z_ODD + 2 * m + s + 1))
                A(w_hi[:, s, :, :], w_raw[:, s, :, :], ACT.Copy).then_inc(sg("w_hi_ready"), 1)

            def next_units(i, m, outer=0):
                for s in range(2):
                    hi_unit(s, i, m + 1, outer)

            def fold(hi, gain, f, n, b, gains=True):
                act.wait_ge(sg("h_ready"), n + 1)
                if gains:
                    A(hi[:, bass.ds(f, 1), :], h[:, bass.ds(f, 1), :], ACT.Copy, scale=pc(gain, f)).then_inc(sg("operand_hi_ready"), 1)
                act.wait_ge(sg("squares_summed"), n + 1)
                settled()
                A(sq[:, b:b + 1, :], h[:, bass.ds(f, 1), :], ACT.Square).then_inc(sg("squares_ready"), 1)

            def root(n):
                act.wait_ge(sg("mean_square_ready"), n + 1)
                A(tmp[:, :], tmp[:, :], ACT.Sqrt).then_inc(sg("rms_ready"), 1)

            act.wait_ge(sg("parameters_transposed"), 1)
            A(par[:, :], bank[0][:, 0:160], ACT.Copy).then_inc(sg("parameters_ready"), 1)
            act.wait_ge(sg("parameters_ready"), 1)
            with act.Fori(0, KT // 2) as i:
                for b in range(2):
                    act.wait_ge(sg("x_transposed"), 2 * i + b + 3)
                    settled()
                    A(h[:, bass.ds(2 * i + b, 1), :], bank[1 + b][:, :].rearrange("p (a t) -> p a t", a=1), ACT.Copy).then_inc(sg("h_ready"), 1)
                    act.wait_ge(sg("h_ready"), 2 * i + b + 1)
                    act.sem_inc(sg("xt_taken"), 1)
                    fold(a_hi, "norm_mix", 2 * i + b, 2 * i + b, b)
            for s in range(2):
                act.wait_ge(sg(f"w_landed{s}"), 32)
                act.wait_ge(sg("unit_done"), s + 1)
                A(w_hi[:, s, :, 0:48], w_raw[:, s, :, 0:48], ACT.Copy).then_inc(sg("w_hi_ready"), 1)
            next_units(0, -1)
            root(0)

            def stage(m, count, outer=0, body=None, peel=False):
                with act.Fori(0, count // 2) as i:
                    for b in range(2):
                        next_units(i, m + b, outer)
                        if body:
                            body(i, b)

            stage(0, 2)

            def pair_tiles(i, m, beside):
                for t in range(Z_PAIR):
                    for s in range(2):
                        hi_unit(s, i, m + t + 1, a_turn=Z_PAIR)
                        beside(i, 2 * t + s + 1)

            def once(i, at):
                if at == 5:
                    act.wait_ge(sg("lora_shifted"), 1)
                    A(tx[0:64, :], t1[0:64, :], ACT.Tanh)
                    A(tx[64:128, :], t1[64:128, :], ACT.Copy)
                    act.wait_ge(sg("lora_shifted"), 2)
                    A(sga[:, :], t2[:, :], ACT.Sigmoid)
                    act.wait_ge(sg("lora_shifted"), 3)
                    A(sgb[:, :], ks[0:32, :], ACT.Sigmoid).then_inc(sg("lora_features_ready"), 1)
                if at == 6:
                    act.wait_ge(sg("f_prepared"), 1)
                    A(f2[:, :], f2[:, :], ACT.Exp, scale=-1.0).then_inc(sg("f_exp"), 1)
                    act.wait_ge(sg("f_exp"), 1)
                    A(f2[:, :], f2[:, :], ACT.Ln, bias=cst[0:16, C_ONE:C_ONE + 1]).then_inc(sg("f_log"), 1)
                if at == 8:
                    act.wait_ge(sg("c_ready"), 1)
                    act.dma_start(c_d, f3[:, :]).then_inc(sg("c_stored"), 16)
                    act.wait_ge(sg("c_transposed"), 1)
                    A(cq[:, :, :], bank[0][:, 0:64].rearrange("p (q n) -> p q n", q=4), ACT.Copy).then_inc(sg("cq_ready"), 1)

            def exps(i, k):
                for q in range(T // P):
                    act.wait_ge(sg("logits_max_ready"), i * 8 + (4 * k + q + 1))
                    w = pr[:, q, 0:(q + 1) * P]
                    A(w, w, ACT.Exp, bias=nmx[:, q:q + 1], accum_out=rsum[:, q:q + 1]).then_inc(sg("exp_ready"), 1)

            def normalize(i, k):
                act.wait_ge(sg("sums_inverted"), i * 2 + (k + 1))
                for q in range(T // P):
                    w = pr[:, q, 0:(q + 1) * P]
                    last = A(w, w, ACT.Copy, scale=rinv[:, q:q + 1])
                last.then_inc(sg("probs_ready"), 1)

            def take_probs(i, k):
                act.wait_ge(sg("probs_t_done"), i * 2 + (k + 1))
                if k:
                    act.wait_ge(sg("heads_done"), i * 2 + 1)
                for j, src in enumerate(prob_banks):
                    last = A(prt[:, j, j * P:], src, ACT.Copy)
                last.then_inc(sg("probs_t_taken"), 1)

            def side(i, at):
                if at == 1:
                    act.wait_ge(sg("side_landed"), i * 144 + 144)
                    for k, src in enumerate((qin, k_in)):
                        A(sq[:, k, :], src[:, :], ACT.Square).then_inc(sg("qk_squares_ready"), 1)
                if at == 2:
                    act.wait_ge(sg("lora_multiplied"), i + 1)
                    settled()
                    A(lw[:, :], bank[0][:, :], ACT.Sigmoid, bias=pc("w0", i)).then_inc(sg("sigmoids_ready"), 1)
                    A(av[:, :], bank[1][:, :], ACT.Sigmoid, bias=pc("a0", i)).then_inc(sg("sigmoids_ready"), 1)
                    act.wait_ge(sg("head_means_ready"), i + 1)
                    A(hr[:, 0:24], hs[:, 0:24], ACT.Sqrt).then_inc(sg("head_roots_ready"), 1)
                if at == 3:
                    act.wait_ge(sg("head_rows_done"), i + 1)
                    A(hrt[0:6, :], bank[5][0:6, :], ACT.Copy).then_inc(sg("head_rows_ready"), 1)
                    act.wait_ge(sg("cum_ready"), i + 1)
                    A(e_in[:, :], cum[:, :], ACT.Exp).then_inc(sg("exps_ready"), 1)
                    A(e_no[:, :], cum[:, :], ACT.Exp, scale=-1.0).then_inc(sg("exps_ready"), 1)
                    A(e_ex[:, :], cex[:, :], ACT.Exp).then_inc(sg("exps_ready"), 1)
                if at == 4:
                    act.wait_ge(sg("exps_ready"), i * 3 + 1)
                    settled()
                    A(ec[:, bass.ds(i, 1), :], e_in[:, :].rearrange("p (a c t) -> p a c t", a=1, c=NC)[:, :, :, C - 1], ACT.Copy).then_inc(sg("ends_ready"), 1)
                if at == 5:
                    act.wait_ge(sg("fv_done"), i + 1)
                    A(vtm[:, :, :], bank[0][:, :].rearrange("p (q n) -> p q n", q=4), ACT.Copy).then_inc(sg("fv_ready"), 1)
                    exps(i, 0)
                if at == 6:
                    normalize(i, 0)
                if at == 7:
                    take_probs(i, 0)
                if at == 8:
                    act.wait_ge(sg("features_made"), i + 1)
                    act.dma_start(ab_d[:, :, bass.ds(i, 1), :, :].rearrange("c p a k t -> p c (a k t)"), ab[:, :, :, :].rearrange("p c k t -> p c (k t)")).then_inc(sg("features_stored"), 16)
                    act.dma_start(v_d[:, :, bass.ds(i, 1), :].rearrange("c p a t -> p c (a t)"), vs[:, :].rearrange("p (c t) -> p c t", c=NC)).then_inc(sg("features_stored"), 16)
                    act.dma_start(bonus_d[bass.ds(i, 1), :, :].rearrange("a p t -> (a p) t"), bon[:, :]).then_inc(sg("features_stored"), 16)
                    exps(i, 1)
                if at == 9:
                    normalize(i, 1)
                if at == 10:
                    take_probs(i, 1)
                if at == 12:
                    act.wait_ge(sg("heads_done"), i * 2 + 2)
                    act.wait_ge(sg("fox_stored"), i * 16 + 16)
                    A(og[:, :], bank[1][:, :], ACT.Copy).then_inc(sg("fox_taken"), 1)
                    act.wait_ge(sg("fox_taken"), i + 2)
                    act.dma_start(fox_d[bass.ds(i, 1), :, :].rearrange("a p t -> (a p) t"), og[:, :]).then_inc(sg("fox_stored"), 16)

            pair_tiles(0, 2, once)
            with act.Fori(0, NPAIR - 1) as i:
                pair_tiles(i, 2 + Z_PAIR, side)
            for at in range(1, 13):
                side(NPAIR - 1, at)

            def chunk(j, b):
                def wait(name, g, n, k):
                    act.wait_ge(sg(name), j * (4 * n) + (2 * (b * n + k) - 1 + g))

                lo = slice(0, HD)

                def transposed(k):
                    dst = (bt, ktm, vt)[k]
                    for g in range(2):
                        wait("transposes_done", g, 3, k + 1)
                        A(dst[:, pairs[g], :], m3(gbank[g][(2, 3, 0)[k]][:, :], H), ACT.Copy).then_inc(sg("transposes_taken"), 1)

                def x_on_diagonal(g):
                    A(xbd[0:HD, pairs[g], 0, :], xs[0:HD, pairs[g], :], ACT.Copy)
                    A(xbd[HD:P, pairs[g], 1, :], xs[HD:P, pairs[g], :], ACT.Copy).then_inc(sg("x_bd_ready"), 1)

                for g in range(2):
                    wait("x_ready", g, 6, 1)
                    x_on_diagonal(g)
                transposed(0)
                for lv in range(1, 6):
                    for g in range(2):
                        wait("pt_done", g, 5, lv)
                        A(ptbd[lo, pairs[g], 0, :], half(g, 1, lo), ACT.Copy)
                        A(pt[lo, pairs[g], :], half(g, 1, lo), ACT.Copy).then_inc(sg("pt_ready_a"), 1)
                    if lv < 3:
                        transposed(lv)
                    for g in range(2):
                        wait("x_ready", g, 6, lv + 1)
                        if lv < 5:
                            wait("dxt_done", g, 4, lv)
                        x_on_diagonal(g)
                for g in range(2):
                    wait("sa_done", g, 1, 1)
                    wait("y_multiplied", g, 1, 1)
                    A(sabd[lo, pairs[g], 0, :], half(g, 1, lo), ACT.Copy)
                    A(sa[lo, pairs[g], :], half(g, 1, lo), ACT.Copy).then_inc(sg("sa_ready_a"), 1)
                for g in range(2):
                    wait("y_multiplied", g, 1, 2)
                    settled()
                    A(y_all[:, pairs[g], bass.ds(j * (2 * C) + b * C, C)], half(g, 3), ACT.Copy).then_inc(sg("y_taken"), 1)
                    wait("state_ready", g, 1, 2)
                    A(stbd[lo, pairs[g], 0, :], st[lo, pairs[g], :], ACT.Copy).then_inc(sg("state_bd_ready_a"), 1)

            with act.Fori(0, NC // 2) as j:
                for b in range(2):
                    chunk(j, b)

            for i in range(NPAIR // NB):
                for n in range(NB):
                    act.wait_ge(sg("y_centred"), NB * i + n + 1)
                    A(squares[n], y_all[:, NB * i + n, :], ACT.Square).then_inc(sg("y_squares_ready"), 1)
                act.wait_ge(sg("head_means_ready"), NPAIR + i + 1)
                A(hr[:, :], hs[:, :], ACT.Sqrt).then_inc(sg("head_roots_ready"), 1)
                act.wait_ge(sg("head_rows_done"), NPAIR + i + 1)
                A(hrt[:, :], bank[5][0:8, :], ACT.Copy).then_inc(sg("head_rows_ready"), 1)
                if i == 0:
                    act.wait_ge(sg("output_landed"), 16 * 11)
                for n in range(NB):
                    A(a_hi[:, NPAIR + NB * i + n, :], yf[:, NB * i + n, :], ACT.Copy).then_inc(sg("operand_hi_ready"), 1)
                    act.wait_ge(sg("y_scaled"), NB * i + n + 1)
                    y = y_all[:, NB * i + n, :]
                    A(y, y, ACT.Identity, bias=pc("gn_b", NB * i + n), scale=pc("gn_w", NB * i + n)).then_inc(sg("y_affine"), 1)
                for n in range(NB):
                    act.wait_ge(sg("y_finished"), NB * i + n + 1)
                    A(a_hi[:, NB * i + n, :], y_all[:, NB * i + n, :], ACT.Copy).then_inc(sg("operand_hi_ready"), 1)

            stage(M_OUT, KT, body=lambda i, b: fold(b_hi, "norm_mlp", 2 * i + b, 2 * i + (b + KT), b))
            root(1)

            def hidden(g):
                def body(i, b):
                    act.wait_ge(sg("relu_squared"), 2 * i + g * KT + (b + 1))
                    settled()
                    A(a_hi[:, bass.ds(2 * i + b, 1), :], sq[:, b:b + 1, :], ACT.Copy).then_inc(sg("operand_hi_ready"), 1)
                return body

            with act.Fori(0, FG - 1) as g:
                stage(M_FF, KT, outer=g * (2 * KT), body=hidden(g))
                stage(M_FF + KT, KT, outer=g * (2 * KT))
            stage(M_GATE - 2 * KT, KT, body=hidden(FG - 1))
            stage(M_GATE - KT, KT, body=lambda i, b: fold(b_hi, "norm_ple", 2 * i + b, 2 * i + (b + 2 * KT), b))
            root(2)

            act.wait_ge(sg("p_transposed"), 1)
            for k in range(2):
                A(p_t[:, k, :], bank[k][:, :], ACT.Copy).then_inc(sg("p_taken"), 1)
            act.wait_ge(sg("p_taken"), 2)
            A(p_hi[:, :, :], p_t[:, :, :], ACT.Copy).then_inc(sg("p_hi_ready"), 1)

            def gated(i, b):
                act.wait_ge(sg("gate_scaled"), 2 * i + (b + 1))
                A(gt[:, b, :], ev[:, b, :], ACT.Sigmoid).then_inc(sg("gate_ready"), 1)
                fold(None, None, 2 * i + b, 2 * i + (b + 3 * KT), b, gains=False)

            def ple_units(i, b):
                act.wait_ge(sg(f"ple_landed{b}"), i * 16 + 16)
                act.wait_ge(sg("ple_done"), i * 2 + b + 1)
                A(pw_hi[:, b, :, :], pw[:, b, :, :], ACT.Copy).then_inc(sg("ple_hi_ready"), 1)

            with act.Fori(0, KT // 2 - 1) as i:
                for b in range(2):
                    ple_units(i, b)
                    next_units(i, M_GATE + b)
                    gated(i, b)
            i = KT // 2 - 1
            ple_units(i, 0)
            next_units(i, M_GATE)
            gated(i, 0)
            ple_units(i, 1)
            gated(i, 1)
            root(3)
            with act.Fori(0, KT // 2) as i:
                for b in range(2):
                    act.wait_ge(sg("final_transposed"), 2 * i + b + 3)
                    act.wait_ge(sg(f"out_stored{b}"), 16 * i)
                    A(ot[:, b, :, :], bank[4 + b][:, :].rearrange("p (q n) -> p q n", q=4), ACT.Copy).then_inc(sg("out_ready"), 1)

        @block.vector
        def _(dve):
            V = nc.vector
            for name, n in (("w_split", 2), ("acc_taken", 2), ("side_inputs_used", 1),
                            ("ple_split", 2), ("ple_taken", 2)):
                dve.sem_inc(sg(name), n)
            chain = [0, 0, 0]

            def then(ins):
                ins.then_inc(sg("dve_chain"), 1)
                chain[0] += 1
                dve.wait_ge(sg("dve_chain"), chain[0] + (chain[1] * chain[2] if chain[2] else 0))

            def chained(i, steps):
                chain[1], chain[2] = i, steps
                return chain[0] + steps

            def unchained(turns, end):
                assert end == chain[0], f"steps a turn: {chain[0] - end + chain[2]}"
                chain[0] += chain[2] * (turns - 1)
                chain[1], chain[2] = 0, 0

            def lo_unit(s, n, width=P):
                dve.wait_ge(sg("w_hi_ready"), n + 1)
                V.tensor_tensor(w_lo[:, s, :, 0:width], w_raw[:, s, :, 0:width], w_hi[:, s, :, 0:width].bitcast(F32),
                                ALU.subtract).then_inc(sg("w_split"), 1)

            def next_units(i, m, outer=0):
                for s in range(2):
                    lo_unit(s, i * 4 + outer * 2 + (Z_ODD + 2 * (m + 1) + s))

            def fold(hi, lo, gain, f, n):
                dve.wait_ge(sg("operand_hi_ready"), n + 1)
                V.scalar_tensor_tensor(lo[:, bass.ds(f, 1), :], h[:, bass.ds(f, 1), :], pc(gain, f), hi[:, bass.ds(f, 1), :].bitcast(F32),
                                       ALU.mult, ALU.subtract).then_inc(sg("operand_split"), 1)

            def invert_rms(n):
                dve.wait_ge(sg("sumsq_spread"), n + 1)
                V.tensor_scalar(tmp[:, :], bank[3][:, :], 1.0 / D, EPS, ALU.mult, ALU.add).then_inc(sg("mean_square_ready"), 1)
                dve.wait_ge(sg("rms_ready"), n + 1)
                then(V.reciprocal(rstd[:, :], tmp[:, :]))

            def stage(m, count, outer=0, body=None):
                with dve.Fori(0, count // 2) as i:
                    for b in range(2):
                        next_units(i, m + b, outer)
                        dve.wait_ge(sg("unit_done"), i * 4 + outer * 2 + (2 + Z_ODD + 2 * (m + b + 1)))
                        body(i, b)

            dve.wait_ge(sg("parameters_ready"), 1)
            with dve.Fori(0, KT) as i:
                fold(a_hi, a_lo, "norm_mix", i, 1 * i)
            dve.wait_ge(sg("operand_split"), KT)
            lo_unit(0, 0, 48)
            lo_unit(1, 1, 48)
            next_units(0, -1)
            invert_rms(0)
            dve.wait_ge(sg("unit_done"), 2 + Z_ODD)
            V.tensor_tensor(ev[0:48, 0, :], bank[0][0:48, :], rstd[0:48, :], ALU.mult).then_inc(sg("odd_ready"), 1)

            def project(i, b):
                for part in range(2):
                    dve.wait_ge(sg(f"ev_free{part}"), 16)
                V.tensor_tensor(ev[:, b, :], acc[b][:, :], rstd[:, :], ALU.mult).then_inc(sg("acc_taken"), 1)

            stage(0, 2, body=project)

            def pair_tiles(i, m, beside):
                for t in range(Z_PAIR):
                    b = t % 2
                    for s in range(2):
                        lo_unit(s, i * (2 * Z_PAIR) + (Z_ODD + 2 * (m + t + 1) + s))
                        if s:
                            dve.wait_ge(sg("unit_done"), i * (2 * Z_PAIR) + (2 + Z_ODD + 2 * (m + t + 1)))
                            dve.wait_ge(sg(f"ev_free{b}"), i * 48 + 16 * ((m + t) // 2 + 1))
                            V.tensor_tensor(ev[:, b, :], acc[b][:, :], rstd[:, :], ALU.mult).then_inc(sg("acc_taken"), 1)
                        beside(i, 2 * t + s + 1)

            def shift(dst, src, mu, parts=P):
                then(V.tensor_tensor(dif[0:parts, :], src[0:parts, 0:T], src[0:parts, 1:], ALU.subtract))
                return V.scalar_tensor_tensor(dst, dif[0:parts, :], mu[0:parts, :], src[0:parts, 1:], ALU.mult, ALU.add)

            def once(i, at):
                if at == 5:
                    dve.wait_ge(sg("once_landed"), 16 * 7)
                    dve.wait_ge(sg("first_columns_zero"), 6)
                    shift(t1[:, :], xin_wa, pc("mu", 24)).then_inc(sg("lora_shifted"), 1)
                    dve.wait_ge(sg("lora_shifted"), 1)
                    shift(t2[:, :], xin_g, pc("mu", 25)).then_inc(sg("lora_shifted"), 1)
                    dve.wait_ge(sg("lora_shifted"), 2)
                    shift(ks[0:32, :], xin_h, pc("mu", 26), 32).then_inc(sg("lora_shifted"), 1)
                if at == 6:
                    then(V.tensor_scalar(fin[:, :], fin[:, :], bf[:, :], None, ALU.add))
                    then(V.tensor_scalar(f1[:, :], fin[:, :], -1.0, None, ALU.mult))
                    V.tensor_tensor(f2[:, :], fin[:, :], f1[:, :], ALU.max).then_inc(sg("f_prepared"), 1)
                    then(V.tensor_scalar(f3[:, :], fin[:, :], 0.0, None, ALU.min))
                if at == 7:
                    dve.wait_ge(sg("f_log"), 1)
                    then(V.tensor_tensor(f3[:, :], f3[:, :], f2[:, :], ALU.subtract))
                    then(V.memset(f2[:, :], 1.0))
                    V.tensor_tensor_scan(f1[:, :], f2[:, :], f3[:, :], 0.0, ALU.mult, ALU.add).then_inc(sg("f_cumulated"), 1)
                    dve.wait_ge(sg("f_cumulated"), 1)
                    V.tensor_scalar(f3[:, :], f1[:, :], -1.0, None, ALU.mult).then_inc(sg("c_ready"), 1)
                    then(V.tensor_scalar(qs[:, :], par[:, 120:121], HD ** -0.5, None, ALU.mult))
                if at == 12:
                    dve.wait_ge(sg("lora_features_ready"), 1)
                    dve.wait_ge(sg("cq_ready"), 1)
                    dve.wait_ge(sg("c_stored"), 16)

            def by_chunk(t):
                return t[:, :].rearrange("p (c t) -> p c t", c=NC)

            def logits(i, k):
                for q, src in enumerate(logit_banks):
                    w = (q + 1) * P
                    dve.wait_ge(sg("logits_done"), i * 8 + (4 * k + max(q, 1) + 1))
                    if k and q == 0:
                        dve.wait_ge(sg("probs_t_done"), i * 2 + 1)
                    then(V.scalar_tensor_tensor(pr[:, q, 0:w], src, cq[:, q, bass.ds(i * 2 + k, 1)], ncb[:, k, 0:w], ALU.add, ALU.add))
                    then(V.tensor_tensor(pr[:, q, q * P:w], pr[:, q, q * P:w], const(C_CAUS, P), ALU.add))
                    then(V.reduce_max(mx[:, q:q + 1], pr[:, q, 0:w], AX.X))
                    V.tensor_scalar(nmx[:, q:q + 1], mx[:, q:q + 1], -1.0, None, ALU.mult).then_inc(sg("logits_max_ready"), 1)

            def invert_sums(i, k):
                dve.wait_ge(sg("exp_ready"), i * 8 + (4 * k + 4))
                V.reciprocal(rinv[:, :], rsum[:, :]).then_inc(sg("sums_inverted"), 1)

            def side(i, at):
                if at == 1:
                    dve.wait_ge(sg("side_landed"), i * 144 + 144)
                    then(shift(ks[:, :], kin, pc("mu", i + 8)))
                    then(V.tensor_scalar(kkr[:, :], ks[:, :], pc("k_k", i), None, ALU.mult))
                    V.tensor_tensor(t1[:, :], kkr[:, :], kkr[:, :], ALU.mult).then_inc(sg("k_squares_ready"), 1)
                if at == 2:
                    dve.wait_ge(sg("head_sums_done"), i + 1)
                    sums, means = (x[:, 0:24].rearrange("p (q n) -> p q n", q=4) for x in (bank[5], hs))
                    V.tensor_scalar(means[:, :, 0:2], sums[:, :, 0:2], 1e-24, None, ALU.max, ALU.bypass)
                    V.tensor_scalar(means[:, :, 2:6], sums[:, :, 2:6], 1.0 / HD, EPS, ALU.mult, ALU.add).then_inc(sg("head_means_ready"), 1)
                    then(shift(rs[:, :], rin, pc("mu", i)))
                    dve.wait_ge(sg("head_roots_ready"), i + 1)
                    V.reciprocal(hr[:, 0:24], hr[:, 0:24]).then_inc(sg("head_inverse_ready"), 1)
                if at == 3:
                    dve.wait_ge(sg("sigmoids_ready"), i * 2 + 2)
                    then(V.tensor_scalar(lw[:, :], lw[:, :], -float(np.exp(-0.5)), None, ALU.mult))
                    then(V.tensor_tensor_scan(cum[:, :], reset[:, :], lw[:, :], 0.0, ALU.mult, ALU.add))
                    V.tensor_tensor(cex[:, :], cum[:, :], lw[:, :], ALU.subtract).then_inc(sg("cum_ready"), 1)
                    dve.wait_ge(sg("features_stored"), i * 48 + 48)
                    then(shift(vs[:, :], vin, pc("mu", i + 16)))
                if at == 4:
                    dve.wait_ge(sg("head_spread"), i + 1)
                    V.tensor_tensor(kk[:, :], kkr[:, :], bank[2][:, :], ALU.mult).then_inc(sg("qk_ready"), 1)
                    V.scalar_tensor_tensor(qh[:, :], qin[:, :], qs[:, :], bank[3][:, :], ALU.mult, ALU.mult).then_inc(sg("qk_ready"), 1)
                    V.scalar_tensor_tensor(kh[:, :], k_in[:, :], par[:, 121:122], bank[4][:, :], ALU.mult, ALU.mult).then_inc(sg("qk_ready"), 1)
                    dve.wait_ge(sg("exps_ready"), i * 3 + 3)
                    V.tensor_tensor(ab[:, :, 1, :], by_chunk(rs), by_chunk(e_in), ALU.mult)
                    dve.wait_ge(sg("qk_ready"), i * 3 + 1)
                    V.scalar_tensor_tensor(ab[:, :, 0, :], by_chunk(kk), -1.0, by_chunk(e_ex), ALU.mult, ALU.mult)
                if at == 5:
                    logits(i, 0)
                if at == 6:
                    invert_sums(i, 0)
                    then(V.tensor_scalar(t1[:, :], av[:, :], -1.0, pc("k_a", i), ALU.add, ALU.mult))
                    then(V.scalar_tensor_tensor(km[:, :], t1[:, :], 1.0, ks[:, :], ALU.add, ALU.mult))
                    then(V.tensor_tensor(t1[:, :], rs[:, :], km[:, :], ALU.mult))
                    V.tensor_scalar(t2[:, :], t1[:, :], pc("r_k", i), None, ALU.mult).then_inc(sg("rk_ready"), 1)
                if at == 7:
                    dve.wait_ge(sg("bonus_summed"), i + 1)
                    V.scalar_tensor_tensor(bon[:, :], bank[1][:, :], float(HD), vs[:, :], ALU.mult, ALU.mult).then_inc(sg("bonus_taken"), 1)
                    then(V.tensor_tensor(t2[:, :], kk[:, :], av[:, :], ALU.mult))
                    V.tensor_tensor(ab[:, :, 2, :], by_chunk(t2), by_chunk(e_no), ALU.mult)
                    V.tensor_tensor(ab[:, :, 3, :], by_chunk(km), by_chunk(e_no), ALU.mult).then_inc(sg("features_made"), 1)
                if at == 8:
                    logits(i, 1)
                    dve.wait_ge(sg("logits_max_ready"), i * 8 + 8)
                    dve.sem_inc(sg("side_inputs_used"), 1)
                if at == 9:
                    invert_sums(i, 1)

            pair_tiles(0, 2, once)
            with dve.Fori(0, NPAIR - 1) as i:
                end = chained(i, 37)
                pair_tiles(i, 2 + Z_PAIR, side)
            unchained(NPAIR - 1, end)
            for at in range(1, 13):
                side(NPAIR - 1, at)

            dve.sem_inc(sg("state_ready"), 2)
            dve.sem_inc(sg("state_bd_ready_b"), 2)

            def chunk(j, b):
                def wait(name, g, n, k):
                    dve.wait_ge(sg(name), j * (4 * n) + (2 * (b * n + k) - 1 + g))

                hi = slice(HD, P)

                def masked(g, dst, k):
                    wait("products_done", g, 2, k + 1)
                    V.tensor_tensor(dst[:, pairs[g], :, :].rearrange("p n a t -> p n (a t)"), m3(gbank[g][k][:, :], H),
                                    const(C_MASK, P)[:, None, :].broadcast_to([P, H, P]), ALU.mult).then_inc(sg("products_ready"), 1)

                for g in range(2):
                    masked(g, gb, 0)
                    wait("products_ready", g, 2, 1)
                    then(V.tensor_tensor(xs[:, pairs[g], :], gb[:, pairs[g], 0, :], const(C_LVL, C)[:, None, :].broadcast_to([P, H, C]), ALU.mult))
                    V.tensor_tensor(xs[:, pairs[g], :], xs[:, pairs[g], :], eye2[:, None, :].broadcast_to([P, H, C]), ALU.add).then_inc(sg("x_ready"), 1)
                for g in range(2):
                    masked(g, gk, 1)
                for g in range(2):
                    wait("xt0_done", g, 1, 1)
                    V.tensor_copy(xt[:, pairs[g], :], half(g, 1)).then_inc(sg("xt_ready"), 1)
                for lv in range(1, 6):
                    for g in range(2):
                        wait("pt_done", g, 5, lv)
                        V.tensor_copy(ptbd[hi, pairs[g], 1, :], half(g, 1, hi))
                        V.tensor_copy(pt[hi, pairs[g], :], half(g, 1, hi)).then_inc(sg("pt_ready_b"), 1)
                    for g in range(2):
                        wait("dx_done", g, 5, lv)
                        wait("x_bd_ready", g, 6, lv)
                        wait("x_ready", g, 6, lv)
                        V.tensor_tensor(xs[:, pairs[g], :], xs[:, pairs[g], :], half(g, 2), ALU.add).then_inc(sg("x_ready"), 1)
                    if lv < 5:
                        for g in range(2):
                            wait("dxt_done", g, 4, lv)
                            wait("xt_ready", g, 5, lv)
                            V.tensor_tensor(xt[:, pairs[g], :], xt[:, pairs[g], :], half(g, 3), ALU.add).then_inc(sg("xt_ready"), 1)
                for g in range(2):
                    wait("r_done", g, 1, 1)
                    V.tensor_copy(rr[:, pairs[g], :], half(g, 0)).then_inc(sg("r_ready"), 1)
                for g in range(2):
                    wait("sa_done", g, 1, 1)
                    V.tensor_copy(sabd[hi, pairs[g], 1, :], half(g, 1, hi))
                    V.tensor_copy(sa[hi, pairs[g], :], half(g, 1, hi)).then_inc(sg("sa_ready_b"), 1)
                for g in range(2):
                    wait("s_done", g, 1, 1)
                    then(V.tensor_tensor(sn[:, pairs[g], :], st[:, pairs[g], :], half(g, 2), ALU.add))
                    wait("state_bd_ready_a", g, 1, 1)
                    V.tensor_tensor(st[:, pairs[g], :], sn[:, pairs[g], :], ec[:, pairs[g], bass.ds(j * 2 + b, 1)].broadcast_to([P, H, C]),
                                    ALU.mult).then_inc(sg("state_ready"), 1)
                for g in range(2):
                    wait("y_multiplied", g, 1, 2)
                    wait("state_ready", g, 1, 2)
                    V.tensor_copy(stbd[hi, pairs[g], 1, :], st[hi, pairs[g], :]).then_inc(sg("state_bd_ready_b"), 1)

            dve.wait_ge(sg("diagonals_cleared"), N_CLEAR)
            dve.wait_ge(sg("fox_stored"), 16 * NPAIR + 16)
            with dve.Fori(0, NC // 2) as j:
                end = chained(j, 8)
                for b in range(2):
                    chunk(j, b)
            unchained(NC // 2, end)
            dve.wait_ge(sg("state_bd_ready_b"), 2 * NC + 2)

            for i in range(NPAIR // NB):
                for n in range(NB):
                    y = y_all[:, NB * i + n, :]
                    dve.wait_ge(sg("mean_done"), NB * i + n + 1)
                    V.tensor_tensor(y, y, bank[n][:, :], ALU.subtract).then_inc(sg("y_centred"), 1)
                dve.wait_ge(sg("head_sums_done"), NPAIR + i + 1)
                V.tensor_scalar(hs[:, :], bank[5][:, 0:32], 1.0 / HD, GN_EPS, ALU.mult, ALU.add).then_inc(sg("head_means_ready"), 1)
                dve.wait_ge(sg("head_roots_ready"), NPAIR + i + 1)
                V.reciprocal(hr[:, :], hr[:, :]).then_inc(sg("head_inverse_ready"), 1)
                for n in range(NB):
                    y = y_all[:, NB * i + n, :]
                    dve.wait_ge(sg("y_centred"), NB * i + n + 1)
                    dve.wait_ge(sg("head_spread"), NPAIR + NB * i + n + 1)
                    V.tensor_tensor(y, y, bank[n][:, :], ALU.mult).then_inc(sg("y_scaled"), 1)
                for n in range(NB):
                    k = NB * i + n
                    y = y_all[:, k, :]
                    dve.wait_ge(sg("y_affine"), k + 1)
                    then(V.tensor_tensor(y, y, yb[:, k, :], ALU.add))
                    dve.wait_ge(sg("gates_done"), k + 1)
                    V.tensor_tensor(y, y, gate_banks[n][:, :], ALU.mult).then_inc(sg("y_finished"), 1)
                    dve.wait_ge(sg("operand_hi_ready"), KT + 2 * NB * i + n + 1)
                    V.tensor_tensor(a_lo[:, NPAIR + k, :], yf[:, k, :], a_hi[:, NPAIR + k, :].bitcast(F32), ALU.subtract).then_inc(sg("operand_split"), 1)
                for n in range(NB):
                    k = NB * i + n
                    dve.wait_ge(sg("operand_hi_ready"), KT + 2 * NB * i + NB + n + 1)
                    V.tensor_tensor(a_lo[:, k, :], y_all[:, k, :], a_hi[:, k, :].bitcast(F32), ALU.subtract).then_inc(sg("operand_split"), 1)

            def grow(i, b, n):
                V.tensor_tensor(h[:, bass.ds(2 * i + b, 1), :], h[:, bass.ds(2 * i + b, 1), :], acc[b][:, :].rearrange("p (a t) -> p a t", a=1),
                                ALU.add).then_inc(sg("acc_taken"), 1)

            def grown(hi, lo, gain, n_h, n_op, n_acc):
                def body(i, b):
                    grow(i, b, None)
                    dve.wait_ge(sg("acc_taken"), 2 * i + (n_acc + b + 3))
                    dve.sem_inc(sg("h_ready"), 1)
                    fold(hi, lo, gain, 2 * i + b, 2 * i + (b + n_op))
                return body

            dve.wait_ge(sg("h_landed"), 64)
            stage(M_OUT, KT, body=grown(b_hi, b_lo, "norm_mlp", KT, 2 * KT, M_OUT))
            invert_rms(1)

            def hidden(g):
                def body(i, b):
                    V.scalar_tensor_tensor(ev[:, b, :], acc[b][:, :], 0.0, rstd[:, :], ALU.max, ALU.mult).then_inc(sg("acc_taken"), 1)
                    dve.wait_ge(sg("acc_taken"), 2 * i + g * (2 * KT) + (M_FF + b + 3))
                    V.tensor_tensor(sq[:, b, :], ev[:, b, :], ev[:, b, :], ALU.mult).then_inc(sg("relu_squared"), 1)
                    dve.wait_ge(sg("operand_hi_ready"), 2 * i + g * KT + (b + 3 * KT + 1))
                    V.tensor_tensor(a_lo[:, bass.ds(2 * i + b, 1), :], sq[:, b:b + 1, :], a_hi[:, bass.ds(2 * i + b, 1), :].bitcast(F32),
                                    ALU.subtract).then_inc(sg("operand_split"), 1)
                return body

            with dve.Fori(0, FG - 1) as g:
                stage(M_FF, KT, outer=g * (2 * KT), body=hidden(g))
                stage(M_FF + KT, KT, outer=g * (2 * KT), body=lambda i, b: grow(i, b, None))
            stage(M_GATE - 2 * KT, KT, body=hidden(FG - 1))
            stage(M_GATE - KT, KT, body=grown(b_hi, b_lo, "norm_ple", 2 * KT, 7 * KT, M_GATE - KT))
            invert_rms(2)

            dve.wait_ge(sg("p_hi_ready"), 1)
            V.tensor_tensor(p_lo[:, :, :], p_t[:, :, :], p_hi[:, :, :].bitcast(F32), ALU.subtract).then_inc(sg("p_split"), 1)

            def ple_unit(n, b):
                dve.wait_ge(sg("ple_hi_ready"), n + 1)
                V.tensor_tensor(pw_lo[:, b, :, :], pw[:, b, :, :], pw_hi[:, b, :, :].bitcast(F32), ALU.subtract).then_inc(sg("ple_split"), 1)

            def gated(i, b):
                n = 2 * i + b
                dve.wait_ge(sg("unit_done"), i * 4 + (2 + Z_ODD + 2 * (M_GATE + b + 1)))
                V.tensor_tensor(ev[:, b, :], acc[b][:, :], rstd[:, :], ALU.mult).then_inc(sg("acc_taken"), 1)
                dve.wait_ge(sg("acc_taken"), 2 * i + (M_GATE + b + 3))
                dve.sem_inc(sg("gate_scaled"), 1)
                dve.wait_ge(sg("gate_ready"), n + 1)
                dve.wait_ge(sg("ple_done"), n + 3)
                V.tensor_tensor(gt[:, b, :], gt[:, b, :], bank[b][:, :], ALU.mult).then_inc(sg("ple_taken"), 1)
                dve.wait_ge(sg("ple_taken"), n + 3)
                V.tensor_tensor(h[:, bass.ds(n, 1), :], h[:, bass.ds(n, 1), :], gt[:, b:b + 1, :], ALU.add).then_inc(sg("h_ready"), 1)

            with dve.Fori(0, KT // 2 - 1) as i:
                for b in range(2):
                    ple_unit(2 * i + b, b)
                    next_units(i, M_GATE + b)
                    gated(i, b)
            i = KT // 2 - 1
            ple_unit(2 * i, 0)
            next_units(i, M_GATE)
            gated(i, 0)
            ple_unit(2 * i + 1, 1)
            gated(i, 1)
            dve.wait_ge(sg("h_ready"), 4 * KT)
            invert_rms(3)
            with dve.Fori(0, KT // 2) as i:
                for b in range(2):
                    dve.wait_ge(sg("final_transposed"), 2 * i + b + 1)
                    V.scalar_tensor_tensor(hn[:, b:b + 1, :], h[:, bass.ds(2 * i + b, 1), :], pc("norm_final", 2 * i + b),
                                           rstd[:, None, :], ALU.mult, ALU.mult).then_inc(sg("final_ready"), 1)

        @block.gpsimd
        def _(pool):
            G = nc.gpsimd
            pool.sem_inc(sg("squares_summed"), 2)
            G.memset(prow[:, :, :], 0.0).then_inc(sg("rows_cleared"), 1)

            def sums(n):
                if n:
                    pool.wait_ge(sg("sumsq_spread"), n)
                G.memset(sumsq[:, :], 0.0).then_inc(sg("sumsq_cleared"), 1)
                pool.wait_ge(sg("sumsq_cleared"), n + 1)
                with pool.Fori(0, KT // 2) as i:
                    for b in range(2):
                        pool.wait_ge(sg("squares_ready"), 2 * i + (n * KT + b + 1))
                        G.tensor_tensor(sumsq[:, :], sumsq[:, :], sq[:, b, :], ALU.add).then_inc(sg("squares_summed"), 1)
                        pool.wait_ge(sg("squares_summed"), 2 * i + (n * KT + b + 3))

            sums(0)
            pool.wait_ge(sg("h_ready"), KT)
            for k in range(4):
                pool.dma_start(h_v[:, 4 * k:4 * k + 4, :], h[:, 4 * k:4 * k + 4, :]).then_inc(sg("h_stored"), 16)
            pool.wait_ge(sg("odd_ready"), 1)
            for b, r in enumerate((slice(0, 32), slice(32, 48))):
                pool.dma_start(zo_d[r, :], ev[r, 0, :]).then_inc(sg(f"ev_free{b}"), 16)
            pool.wait_ge(sg("operand_split"), KT)
            pool.wait_ge(sg("h_stored"), 64)
            for t in (kin, rin, vin, xin_wa, xin_g, xin_h):
                G.memset(t[:, 0:1], 0.0).then_inc(sg("first_columns_zero"), 1)
            with pool.Fori(0, Z_TILES // 2) as i:
                for b in range(2):
                    pool.wait_ge(sg("acc_taken"), 2 * i + (b + 3))
                    pool.dma_start(z_d[bass.ds(2 * i + b, 1), :, :].rearrange("a p t -> (a p) t"), ev[:, b, :]).then_inc(sg(f"ev_free{b}"), 16)

            pool.wait_ge(sg("unit_done"), 2 + Z_ODD + 2 * Z_TILES)
            for n, t in enumerate(diagonals):
                if n == N_CLEAR - 2:
                    pool.wait_ge(sg("features_made"), NPAIR)
                G.memset(t, 0.0).then_inc(sg("diagonals_cleared"), 1)
            pool.wait_ge(sg("diagonals_cleared"), N_CLEAR)
            halves = ((slice(0, 64), 0), (slice(64, 128), 1))

            def chunk(j, b):
                def wait(name, g, n, k):
                    pool.wait_ge(sg(name), j * (4 * n) + (2 * (b * n + k) - 1 + g))

                def level(lv):
                    for g in range(2):
                        if lv > 2:
                            wait("pt_done", g, 5, lv - 2)
                        else:
                            wait("products_ready", g, 2, 1)
                        for ph, a in halves:
                            last = G.tensor_tensor(nbd[ph, lv % 2, pairs[g], a, :], gb[ph, pairs[g], 0, :],
                                                   const(C_LVL + lv * C, C, ph)[:, None, :].broadcast_to([64, H, C]), ALU.mult)
                        last.then_inc(sg("n_ready"), 1)

                level(1)
                level(2)
                for g in range(2):
                    wait("products_ready", g, 2, 2)
                    pool.sem_inc(sg("pool_waits_taken"), 1)
                    for ph, a in halves:
                        last = G.tensor_copy(mbd[ph, pairs[g], a, :], gk[ph, pairs[g], 0, :])
                    last.then_inc(sg("m_ready"), 1)
                level(3)
                level(4)
                for g in range(2):
                    wait("transposes_taken", g, 3, 3)
                    pool.sem_inc(sg("pool_waits_taken"), 1)
                    for ph, a in halves:
                        last = G.tensor_copy(vst[ph, pairs[g], :], vt[ph, pairs[g], a * C:(a + 1) * C])
                    last.then_inc(sg("v_stacked"), 1)
                level(5)

            with pool.Fori(0, NC // 2) as j:
                for b in range(2):
                    chunk(j, b)

            pool.wait_ge(sg("n_ready"), 10 * NC)
            for n in (1, 2, 3):
                sums(n)


    ctx.close()


_INS = ["x", "p", "norm_mix", "w_in", "mu_shift", "w0", "w2", "a0", "a2", "g2", "k_k", "k_a", "r_k", "gn_w", "gn_b",
        "b_f", "q_norm", "k_norm", "w_out", "norm_mlp", "w_ff1", "w_ff2", "norm_ple", "w_ple_gate", "w_ple_proj",
        "norm_final"]


def kernel(**inputs):
    import concourse.bacc as bacc
    from concourse.bass_utils import run_bass_kernel_spmd

    nc = bacc.Bacc("TRN2", target_bir_lowering=False, num_devices=1)
    arrays, args = {}, []
    for name in _INS + ["consts"]:
        a = constants() if name == "consts" else np.ascontiguousarray(inputs[name])
        arrays[f"in_{name}"] = a
        args.append(nc.dram_tensor(f"in_{name}", a.shape, mybir.dt.from_np(a.dtype), kind="ExternalInput").ap())
    args.append(nc.dram_tensor("out", (1, T, D), F32, kind="ExternalOutput").ap())
    build(nc, *args)
    r = run_bass_kernel_spmd(nc, [arrays], core_ids=[0])
    return r.results[0]["out"]
```

```python
import numpy as np
from contextlib import ExitStack

import concourse.bass as bass
from concourse import mybir

F32 = mybir.dt.float32
F32R = mybir.dt.float32r
ALU = mybir.AluOpType
ACT = mybir.ActivationFunctionType
AX = mybir.AxisListType

P = 128
D = 2048
T = 512
KT = D // P
HD = 64
DR = 1024
NPAIR = DR // P
FF = 4 * D
FG = FF // D
DPLE = 256
C = 64
NC = T // C
N_SHIFT = 3 * DR + 64 + 64 + 160
EPS = 1e-6
GN_EPS = 64e-5
UK = KT // 2
NEG = -1e30

Z_TILES = 50
Z_PAIR = 6
Z_COLUMNS = (DR, 0, 2 * DR, N_SHIFT, N_SHIFT + DR, N_SHIFT + 2 * DR)

C_ID, C_ONE, C_MASK, C_LVL = 0, 128, 256, 384
C_BLK, C_HEAD, C_CAUS = 768, 896, 898
C_EYE2, C_RESET = 1026, 1090
C_SPREAD = C_RESET + T
C_COLS = C_SPREAD + 4 * P


def constants():
    c = np.zeros((P, C_COLS), np.float32)
    p = np.arange(P)
    j = p % C
    t = np.arange(C)
    c[:, C_ID:C_ID + P] = np.eye(P)
    c[:, C_ONE:C_ONE + P] = 1.0
    c[:, C_MASK:C_MASK + C] = t[None, :] > j[:, None]
    c[:, C_MASK + C:C_MASK + 2 * C] = t[None, :] >= j[:, None]
    for n in range(6):
        b = 1 << n
        c[:, C_LVL + n * C:C_LVL + (n + 1) * C] = (
            (j[:, None] // (2 * b) == t[None, :] // (2 * b)) & (j[:, None] % (2 * b) < b) & (t[None, :] % (2 * b) >= b))
    c[:, C_BLK:C_BLK + P] = (p[:, None] // HD == p[None, :] // HD) / HD
    c[:, C_HEAD:C_HEAD + 2] = p[:, None] // HD == np.arange(2)[None, :]
    c[:, C_EYE2:C_EYE2 + C] = t[None, :] == j[:, None]
    c[:, C_CAUS:C_CAUS + P] = np.where(p[:, None] >= p[None, :], 0.0, NEG)
    for s in range(4):
        c[0:8, C_SPREAD + s * P:C_SPREAD + (s + 1) * P] = np.arange(8)[:, None] == 2 * s + p[None, :] // HD
    c[:, C_RESET:C_RESET + T] = np.arange(T)[None, :] % C != 0
    return c


def build(nc, x, p, norm_mix, w_in, mu_shift, w0, w2, a0, a2, g2, k_k, k_a, r_k, gn_w, gn_b, b_f, q_norm,
          k_norm, w_out, norm_mlp, w_ff1, w_ff2, norm_ple, w_ple_gate, w_ple_proj, norm_final, consts, out):
    ctx = ExitStack()
    sems = {}

    def sg(name):
        if name not in sems:
            sems[name] = ctx.enter_context(nc.semaphore(name))
        return sems[name]

    def sb(name, shape, where, dt=F32):
        n = 4
        for s in shape[1:]:
            n *= s
        t = nc.alloc_sbuf_tensor_at(name, shape, dt, offset=where[0])
        where[0] += (n + 63) // 64 * 64
        return t

    top = [(nc.sbuf_base + 63) // 64 * 64]
    a_hi = sb("a_hi", [P, KT, T], top, F32R)
    a_lo = sb("a_lo", [P, KT, T], top, F32R)
    arena = top[0]
    b_hi = sb("b_hi", [P, KT, T], top, F32R)
    b_lo = sb("b_lo", [P, KT, T], top, F32R)
    arena_h = top[0]
    h = sb("h", [P, KT, T], top)
    h_end = top[0]
    w_raw = sb("w_raw", [P, 2, UK, P], top)
    w_hi = sb("w_hi", [P, 2, UK, P], top, F32R)
    w_lo = sb("w_lo", [P, 2, UK, P], top, F32R)
    rstd = sb("rstd", [P, T], top)
    sumsq = sb("sumsq", [P, T], top)
    sq = sb("sq", [P, 2, T], top)
    ev = sb("ev", [P, 2, T], top)
    tmp = sb("tmp", [P, T], top)
    par = sb("par", [P, 160], top)
    cst = sb("cst", [P, C_RESET], top)
    assert top[0] <= nc.sbuf_usable_end, (top[0], nc.sbuf_usable_end)

    def const(c, n, parts=slice(0, P)):
        return cst[parts, c:c + n]

    ident, ones, eye2 = const(C_ID, P), const(C_ONE, P), const(C_EYE2, C)
    head_of = const(C_HEAD, 2)

    acc = [nc.alloc_psum_tensor(f"acc{i}", [P, T], F32) for i in range(2)]
    bank = [nc.alloc_psum_tensor(f"bank{i}", [P, T], F32) for i in range(6)]

    def dram(name, shape):
        return nc.dram_tensor(name, shape, F32, kind="Internal").ap()

    z_d = dram("z_d", (Z_TILES, P, T))
    zo_d = dram("zo_d", (48, T))
    h_d = dram("h_d", (KT, P, T))
    ab_d = dram("ab_d", (NC, P, NPAIR, 4, C))
    v_d = dram("v_d", (NC, P, NPAIR, C))
    bonus_d = dram("bonus_d", (NPAIR, P, T))
    fox_d = dram("fox_d", (NPAIR, P, T))
    c_d = dram("c_d", (2 * NPAIR, T))
    h_v = h_d.rearrange("k p t -> p k t")

    rows = [("norm_mix", norm_mix, 16), ("norm_mlp", norm_mlp, 16), ("norm_ple", norm_ple, 16),
            ("norm_final", norm_final, 16), ("w0", w0, 8), ("a0", a0, 8), ("k_k", k_k, 8), ("k_a", k_a, 8),
            ("r_k", r_k, 8), ("gn_w", gn_w, 8), ("gn_b", gn_b, 8)]
    col = {"q_norm": 120, "k_norm": 121, "mu": P}
    for n, row in enumerate(rows):
        col[row[0]] = sum(r[2] for r in rows[:n])
    N_PAR = len(rows) + 4 + 2

    def pc(name, i=0):
        return par[:, bass.ds(col[name] + i, 1)]

    def flat(a):
        if len(a.shape) == 3:
            a = a.rearrange("a h d -> a (h d)")
        return a.rearrange("(a n) -> a n", a=1) if len(a.shape) == 1 else a

    def w_view(w):
        return w.rearrange("a (k p) n -> p (a k) n", p=P)

    w_in_v, w_out_v, ff1_v, ff2_v, gate_v = (w_view(w) for w in (w_in, w_out, w_ff1, w_ff2, w_ple_gate))
    ple_v = w_view(w_ple_proj)

    at = [arena]
    xin = sb("xin", [P, 4, T // P, P], at)
    prow = sb("prow", [P, 2, P], at)
    at = [arena]
    kin = sb("kin", [P, T + 1], at)
    rin = sb("rin", [P, T + 1], at)
    vin = sb("vin", [P, T + 1], at)
    reset = sb("reset", [P, T], at)
    spread = sb("spread", [6, 3, P], at)
    wa_in = sb("wa_in", [P, P], at)
    dif = sb("dif", [P, T], at)
    ks = sb("ks", [P, T], at)
    rs = sb("rs", [P, T], at)
    vs = sb("vs", [P, T], at)
    lw = sb("lw", [P, T], at)
    cum = sb("cum", [P, T], at)
    cex = sb("cex", [P, T], at)
    av = sb("av", [P, T], at)
    e_in = sb("e_in", [P, T], at)
    e_ex = sb("e_ex", [P, T], at)
    e_no = sb("e_no", [P, T], at)
    kkr = sb("kkr", [P, T], at)
    kk = sb("kk", [P, T], at)
    km = sb("km", [P, T], at)
    t1 = sb("t1", [P, T], at)
    t2 = sb("t2", [P, T], at)
    ab = sb("ab", [P, NC, 4, C], at)
    bon = sb("bon", [P, T], at)
    cq = sb("cq", [P, T // P, 16], at)
    qin = sb("qin", [P, T], at)
    k_in = sb("k_in", [P, T], at)
    v_in = sb("v_in", [P, T], at)
    qh = sb("qh", [P, T], at)
    kh = sb("kh", [P, T], at)
    vtm = sb("vtm", [P, T // P, P], at)
    ncb = sb("ncb", [P, 2, T], at)
    mx = sb("mx", [P, 4], at)
    nmx = sb("nmx", [P, 4], at)
    rsum = sb("rsum", [P, 4], at)
    rinv = sb("rinv", [P, 4], at)
    og = sb("og", [P, T], at)
    once_at = at[0]
    pr = sb("pr", [P, T // P, T], at)
    prt = sb("prt", [P, T // P, T], at)
    side_end = at[0]
    at = [once_at]
    xin_wa = sb("xin_wa", [P, T + 1], at)
    xin_g = sb("xin_g", [P, T + 1], at)
    xin_h = sb("xin_h", [32, T + 1], at)
    fin = sb("fin", [16, T], at)
    f1 = sb("f1", [16, T], at)
    f2 = sb("f2", [16, T], at)
    f3 = sb("f3", [16, T], at)
    bf = sb("bf", [16, 1], at)
    assert at[0] <= side_end
    at = [(nc.sbuf_base + 63) // 64 * 64]
    loads = [[sb(f"{name}{b}", [P, NPAIR, 2, C], at) for name in ("abd", "bbd", "kbd", "vbd", "ars")] for b in range(2)]
    mbd = sb("mbd", [P, NPAIR, 2, C], at)
    nbd = sb("nbd", [P, 2, NPAIR, 2, C], at)
    xbd = sb("xbd", [P, NPAIR, 2, C], at)
    ptbd = sb("ptbd", [P, NPAIR, 2, C], at)
    sabd = sb("sabd", [P, NPAIR, 2, C], at)
    assert at[0] <= arena
    at = [arena]
    st = sb("st", [P, NPAIR, C], at)
    stbd = sb("stbd", [P, NPAIR, 2, C], at)
    after_state = at[0]
    y_all = sb("y_all", [P, NPAIR, T], at)
    yb = sb("yb", [P, NPAIR, T], at)
    g2a = sb("g2a", [P, DR], at)
    g2b = sb("g2b", [32, DR], at)
    after_y = at[0]
    gb = sb("gb", [P, NPAIR, 2, C], at)
    gk = sb("gk", [P, NPAIR, 2, C], at)
    xs = sb("xs", [P, NPAIR, C], at)
    xt = sb("xt", [P, NPAIR, C], at)
    pt = sb("pt", [P, NPAIR, C], at)
    bt = sb("bt", [P, NPAIR, P], at)
    ktm = sb("ktm", [P, NPAIR, P], at)
    vt = sb("vt", [P, NPAIR, P], at)
    vst = sb("vst", [P, NPAIR, C], at)
    rr = sb("rr", [P, NPAIR, C], at)
    sa = sb("sa", [P, NPAIR, C], at)
    sn = sb("sn", [P, NPAIR, C], at)
    assert at[0] <= h_end, at[0] - h_end
    diagonals = [t[:, :, :, :] for b in range(2) for t in loads[b][:4]] + [t[:, :, :, :] for t in (mbd, xbd, ptbd, sabd)] + [
        nbd[:, 0, :, :, :], nbd[:, 1, :, :, :], stbd[:, :, :, :], st[:, :, :]]
    N_CLEAR = len(diagonals)
    H = NPAIR // 2
    gbank = [bank[0:4], acc + bank[4:6]]
    pairs = [slice(g * H, (g + 1) * H) for g in range(2)]

    def flat2(t):
        return t.rearrange("p a t -> p (a t)")

    def m3(b, n=NPAIR):
        return b.rearrange("p (n t) -> p n t", n=n)

    def half(g, k, parts=slice(0, P)):
        return m3(gbank[g][k][parts, 0:H * C], H)

    keep = [h_end - 3 * 2048 - 256 - 2048]
    tx = sb("tx", [P, T], keep)
    sga = sb("sga", [P, T], keep)
    sgb = sb("sgb", [32, T], keep)
    ec = sb("ec", [P, NPAIR, NC], keep)
    assert side_end <= h_end - 3 * 2048 - 256 - 2048, side_end - h_end
    assert keep[0] <= h_end and at[0] <= h_end - 3 * 2048 - 256 - 2048, (at[0], h_end)
    at = [arena]
    spread4 = sb("spread4", [8, 4, P], at)
    assert at[0] <= after_state
    at = [after_y]
    yf = sb("yf", [P, NPAIR, T], at)
    assert at[0] <= arena_h
    NB = 4
    gate_banks = [bank[4], acc[0], acc[1], bank[5]]
    squares = [sq[:, 0, :], sq[:, 1, :], ev[:, 0, :], ev[:, 1, :]]
    at = [(nc.sbuf_base + 63) // 64 * 64]
    p_in = sb("p_in", [P, T // P, DPLE], at)
    p_hi = sb("p_hi", [P, 2, T], at, F32R)
    p_lo = sb("p_lo", [P, 2, T], at, F32R)
    pw = sb("pw", [P, 2, 2, P], at)
    pw_hi = sb("pw_hi", [P, 2, 2, P], at, F32R)
    pw_lo = sb("pw_lo", [P, 2, 2, P], at, F32R)
    p_t = sb("p_t", [P, 2, T], at)
    gt = sb("gt", [P, 2, T], at)
    hn = sb("hn", [P, 4, T], at)
    ot = sb("ot", [P, 4, T // P, P], at)
    hs = sb("hs", [P, 32], top)
    hr = sb("hr", [P, 32], top)
    hrt = sb("hrt", [8, T], top)
    qs = sb("qs", [P, 1], top)
    assert top[0] <= nc.sbuf_usable_end, (top[0], nc.sbuf_usable_end)

    Z_ODD = 2
    M_OUT = Z_TILES
    M_FF = M_OUT + KT
    M_GATE = M_FF + FG * 2 * KT

    logit_banks = [bank[2][:, 0:P], bank[2][:, P:3 * P], bank[3][:, 0:3 * P], bank[4][:, :]]
    prob_banks = [bank[0][:, :], bank[5][:, P:], bank[2][:, 0:2 * P], bank[5][:, 0:P]]

    with nc.Block() as block:

        @block.sync
        def _(sp):
            def unit(slot, src, n):
                sp.wait_ge(sg("w_split"), n + 1)
                sp.dma_start(w_raw[:, slot, :, :], src).then_inc(sg(f"w_landed{slot}"), 16)

            def stream(view, row, column, m, tiles, outer=0):
                with sp.Fori(0, tiles // 2) as i:
                    for b in range(2):
                        for s in range(2):
                            unit(s, view[:, row + s * UK:row + (s + 1) * UK, bass.ds(i * (2 * P) + (column + b * P), P)],
                                 i * 4 + outer + Z_ODD + 2 * m + 2 * b + s)

            sp.dma_start(cst[:, :], consts[:, 0:C_RESET]).then_inc(sg("constants_landed"), 16)
            sp.wait_ge(sg("rows_cleared"), 1)
            def row_pair(name, a, n):
                return prow[col[name]:col[name] + n, 0, :], flat(a).rearrange("a (n q) -> (a n) q", q=P)

            sp.dma_start(*row_pair(*rows[0])).then_inc(sg("gain_landed"), 16)
            others = [row_pair(*row) for row in rows[1:]]
            others += [(prow[120 + k:121 + k, 0, half * HD:(half + 1) * HD], a) for k, a in enumerate((q_norm, k_norm)) for half in range(2)]
            others += [(prow[0:26, 1, :], mu_shift[0, 0:26 * P].rearrange("(n q) -> n q", q=P)),
                       (prow[26:27, 1, 0:32], mu_shift[0:1, 26 * P:N_SHIFT])]
            assert len(others) == N_PAR - 1
            x_v = x.rearrange("a (b q) n -> q (a b) n", q=P)
            for f in range(KT):
                if f >= 4:
                    sp.wait_ge(sg("x_transposed"), f + 1)
                sp.dma_start(xin[:, f % 4, :, :], x_v[:, :, f * P:(f + 1) * P]).then_inc(sg(f"x_landed{f % 4}"), 16)
                if f >= 3:
                    for dst, src in others[(f - 3) * 2:(f - 2) * 2]:
                        sp.dma_start(dst, src).then_inc(sg("parameters_landed"), 16)
            for s in range(2):
                r = slice(s * UK, (s + 1) * UK)
                sp.wait_ge(sg("w_split"), s + 1)
                sp.dma_start(w_raw[:, s, :, 0:32], w_in_v[:, r, N_SHIFT - 32:N_SHIFT]).then_inc(sg(f"w_landed{s}"), 16)
                sp.dma_start(w_raw[:, s, :, 32:48], w_in_v[:, r, N_SHIFT + 3 * DR:N_SHIFT + 3 * DR + 16]).then_inc(sg(f"w_landed{s}"), 16)
            stream(w_in_v, 0, 3 * DR, 0, 2)

            def pair_units(i, m, t):
                for s in range(2):
                    unit(s, w_in_v[:, s * UK:(s + 1) * UK, bass.ds(i * P + (Z_COLUMNS[t] + (m - 2) // Z_PAIR * P), P)],
                         i * (2 * Z_PAIR) + (Z_ODD + 2 * m + s))

            def load_pair(i):
                sp.wait_ge(sg("ev_free0"), i * 48 + 80)
                sp.sem_inc(sg("sp_waits_taken"), 1)
                sp.wait_ge(sg("ev_free1"), i * 48 + 64)
                sp.sem_inc(sg("sp_waits_taken"), 1)
                sp.wait_ge(sg("side_inputs_used"), i + 1)
                for t, dst in enumerate((kin, rin, vin, qin, k_in)):
                    dst = dst[:, 1:] if t < 3 else dst[:, :]
                    sp.dma_start(dst, z_d[bass.ds(i * Z_PAIR + (2 + t), 1), :, :].rearrange("a p t -> (a p) t")).then_inc(sg("side_landed"), 16)
                sp.dma_start(wa_in[0:64, :], w2[0, :, bass.ds(i * P, P)]).then_inc(sg("side_landed"), 16)
                sp.dma_start(wa_in[64:128, :], a2[0, :, bass.ds(i * P, P)]).then_inc(sg("side_landed"), 16)
                sp.wait_ge(sg("c_stored"), 16)
                for k in range(2):
                    sp.dma_start(ncb[:, k, :], c_d[bass.ds(i * 2 + k, 1), :].broadcast_to([P, T])).then_inc(sg("side_landed"), 16)

            def load_fox_v(i):
                sp.wait_ge(sg("ev_free1"), i * 48 + 80)
                sp.dma_start(v_in[:, :], z_d[bass.ds(i * Z_PAIR + 7, 1), :, :].rearrange("a p t -> (a p) t")).then_inc(sg("fv_landed"), 16)

            for t in range(2):
                pair_units(0, 2 + t, t)
            for b in range(2):
                sp.wait_ge(sg(f"ev_free{b}"), 32)
            sp.wait_ge(sg("operand_split"), KT)
            sp.wait_ge(sg("h_stored"), 64)
            for dst, src in ((xin_wa[:, 1:], z_d[0]), (xin_g[:, 1:], z_d[1]), (xin_h[:, 1:], zo_d[0:32, :]),
                             (reset[:, :], consts[:, C_RESET:C_RESET + T]),
                             (spread[:, :, :], consts[0:6, C_SPREAD:C_SPREAD + 3 * P].rearrange("p (s n) -> p s n", s=3)),
                             (fin[:, :], zo_d[32:48, :]), (bf[:, :], b_f.rearrange("a n -> n a"))):
                sp.dma_start(dst, src).then_inc(sg("once_landed"), 16)
            for t in range(2, Z_PAIR):
                pair_units(0, 2 + t, t)
            with sp.Fori(0, NPAIR - 1) as i:
                for t in range(Z_PAIR):
                    pair_units(i, 2 + Z_PAIR + t, t)
                    if t == 0:
                        load_pair(i)
                    if t == 1:
                        load_fox_v(i)
            for s in range(2):
                unit(s, w_out_v[:, s * UK:(s + 1) * UK, 0:P], Z_ODD + 2 * M_OUT + s)
            load_pair(NPAIR - 1)
            load_fox_v(NPAIR - 1)

            sp.wait_ge(sg("features_stored"), 48 * NPAIR + 48)
            sp.wait_ge(sg("diagonals_cleared"), N_CLEAR)

            def load_chunk(b, n, j=0):
                chunk = bass.ds(j * 2 + n, 1)
                a, be, ka, v, ar = loads[b]
                for hf in range(2):
                    ph = slice(hf * HD, (hf + 1) * HD)
                    for dst, kind in ((a, 0), (be, 2), (ka, 3)):
                        sp.dma_start(dst[ph, :, hf, :], ab_d[chunk, ph, :, kind, :].rearrange("a p n t -> (a p) n t")).then_inc(sg(f"chunk_landed{b}"), 16)
                    sp.dma_start(v[ph, :, hf, :], v_d[chunk, ph, :, :].rearrange("a p n t -> (a p) n t")).then_inc(sg(f"chunk_landed{b}"), 16)
                sp.dma_start(ar[:, :, :, :], ab_d[chunk, :, :, 0:2, :].rearrange("a p n k t -> (a p) n k t")).then_inc(sg(f"chunk_landed{b}"), 16)

            load_chunk(0, 0)
            load_chunk(1, 1)
            sp.wait_ge(sg("fox_stored"), 16 * NPAIR + 16)
            for k in range(4):
                sp.dma_start(yb[:, 2 * k:2 * k + 2, :], bonus_d[2 * k:2 * k + 2, :, :].rearrange("n p t -> p n t")).then_inc(sg("output_landed"), 16)
            sp.dma_start(g2a[:, :], g2[0, 0:P, :]).then_inc(sg("output_landed"), 16)
            sp.dma_start(g2b[:, :], g2[0, P:P + 32, :]).then_inc(sg("output_landed"), 16)
            with sp.Fori(0, NC // 2 - 1) as j:
                for b in range(2):
                    sp.wait_ge(sg("y_multiplied"), j * 4 + (2 * b + 4))
                    load_chunk(b, b + 2, j)

            sp.wait_ge(sg("y_taken"), 2 * NC + 2)
            sp.wait_ge(sg("state_ready"), 2 * NC + 2)
            sp.wait_ge(sg("state_bd_ready_a"), 2 * NC + 2)
            sp.wait_ge(sg("state_bd_ready_b"), 2 * NC + 2)
            sp.dma_start(spread4[:, :, :], consts[0:8, C_SPREAD:C_SPREAD + 4 * P].rearrange("p (s n) -> p s n", s=4)).then_inc(sg("output_landed"), 16)
            for k in range(4):
                sp.dma_start(yf[:, 2 * k:2 * k + 2, :], fox_d[2 * k:2 * k + 2, :, :].rearrange("n p t -> p n t")).then_inc(sg("output_landed"), 16)

            for k in range(4):
                if k == 2:
                    for hf in range(2):
                        unit(hf, w_out_v[:, hf * UK:(hf + 1) * UK, P:2 * P], Z_ODD + 2 * M_OUT + 2 + hf)
                    sp.wait_ge(sg("gates_done"), NPAIR)
                sp.dma_start(h[:, 4 * k:4 * k + 4, :], h_v[:, 4 * k:4 * k + 4, :]).then_inc(sg("h_landed"), 16)
            stream(w_out_v, 0, 2 * P, M_OUT + 2, KT - 2)
            with sp.Fori(0, FG) as g:
                for view, m0, row, cc in ((ff1_v, 0, 0, D), (ff2_v, KT, KT, 0)):
                    with sp.Fori(0, KT // 2) as i:
                        for b in range(2):
                            for s in range(2):
                                r0 = s * UK
                                src = (view[:, r0:r0 + UK, bass.ds(g * D + i * (2 * P) + b * P, P)] if cc else
                                       view[:, bass.ds(g * KT + r0, UK), bass.ds(i * (2 * P) + b * P, P)])
                                unit(s, src, g * (4 * KT) + i * 4 + (Z_ODD + 2 * (M_FF + m0) + 2 * b + s))
            def gate_units(n, i=0):
                for s in range(2):
                    unit(s, gate_v[:, s * UK:(s + 1) * UK, bass.ds(i * (2 * P) + n * P, P)], i * 4 + (Z_ODD + 2 * (M_GATE + n) + s))

            gate_units(0)
            sp.wait_ge(sg("unit_done"), 2 + Z_ODD + 2 * M_GATE)
            sp.dma_start(p_in[:, :, :], p.rearrange("l a (b q) n -> q (l a b) n", q=P)).then_inc(sg("p_landed"), 16)

            def ple_weights(b, c0, n):
                sp.wait_ge(sg("ple_split"), n + 1)
                sp.dma_start(pw[:, b, :, :], ple_v[:, :, bass.ds(c0, P)]).then_inc(sg(f"ple_landed{b}"), 16)

            ple_weights(0, 0, 0)
            ple_weights(1, P, 1)
            gate_units(1)
            with sp.Fori(0, KT // 2 - 1) as i:
                for b in range(2):
                    ple_weights(b, i * (2 * P) + (b + 2) * P, 2 * i + (b + 2))
                    gate_units(b + 2, i)
            o_v = out.rearrange("a (b q) n -> q (a b) n", q=P)
            with sp.Fori(0, KT // 4) as i:
                for b in range(4):
                    sp.wait_ge(sg("out_ready"), 4 * i + b + 5)
                    sp.dma_start(o_v[:, :, bass.ds(i * (4 * P) + b * P, P)], ot[:, b, :, :]).then_inc(sg(f"out_stored{b}"), 16)
            for b in range(4):
                sp.wait_ge(sg(f"out_stored{b}"), 16 * (KT // 4) + 16)

        @block.tensor
        def _(pe):
            pe.sem_inc(sg("unit_done"), 2)
            pe.sem_inc(sg("x_transposed"), 4)
            pe.sem_inc(sg("ple_done"), 2)
            pe.sem_inc(sg("final_transposed"), 4)
            pe.sem_inc(sg("y_multiplied"), 2)

            mm = nc.tensor.matmul

            def gemm(dst, hi, lo, n, width=P, ready=None, beside=None):
                for s in range(2):
                    pe.wait_ge(sg("w_split"), n + s + 3)
                    for k in range(UK):
                        kt = s * UK + k
                        if ready is not None and k == 0:
                            pe.wait_ge(sg("operand_split"), ready + (UK if s == 0 else KT))
                        wh, wl = w_hi[:, s, k, 0:width], w_lo[:, s, k, 0:width]
                        mm(dst, wh, hi[:, kt, :], start=kt == 0, stop=False)
                        mm(dst, wh, lo[:, kt, :], start=False, stop=False)
                        last = mm(dst, wl, hi[:, kt, :], start=False, stop=kt == KT - 1)
                        if k == UK - 1:
                            last.then_inc(sg("unit_done"), 1)
                        if beside and k % (UK // 2) == UK // 2 - 1:
                            beside(s + (k + 1) / UK)

            def tiles(m, count, hi, lo, ready=None, outer=0, after=None, beside=None):
                with pe.Fori(0, count // 2) as i:
                    for b in range(2):
                        pe.wait_ge(sg("acc_taken"), i * 2 + outer + (m + b + 1))
                        gemm(acc[b][:, :], hi, lo, i * 4 + outer * 2 + (Z_ODD + 2 * m + 2 * b), ready=ready, beside=None if b else beside)
                        if after:
                            after(i, b)

            def spread_sumsq(n):
                pe.wait_ge(sg("squares_summed"), 2 + KT * (n + 1))
                mm(bank[3][:, :], ones, sumsq[:, :], start=True, stop=True).then_inc(sg("sumsq_spread"), 1)

            pe.wait_ge(sg("constants_landed"), 16)
            pe.wait_ge(sg("gain_landed"), 16)
            mm(bank[0][:, 0:16], prow[0:16, 0, :], ident[0:16, 0:16], start=True, stop=True).then_inc(sg("gain_transposed"), 1)
            with pe.Fori(0, KT // 4) as i:
                for b in range(4):
                    pe.wait_ge(sg(f"x_landed{b}"), 16 * i + 16)
                    pe.wait_ge(sg("xt_taken"), 4 * i + b + 1)
                    for q in range(T // P):
                        last = nc.tensor.transpose(bank[1 + b % 2][:, q * P:(q + 1) * P], xin[:, b, q, :], ident)
                    last.then_inc(sg("x_transposed"), 1)
            pe.wait_ge(sg("gain_ready"), 1)
            pe.wait_ge(sg("parameters_landed"), 16 * (N_PAR - 1))
            for k in range(2):
                last = nc.tensor.transpose(bank[4][:, k * P:(k + 1) * P], prow[:, k, :], ident)
            last.then_inc(sg("parameters_transposed"), 1)
            gemm(bank[0][0:48, :], a_hi, a_lo, 0, width=48, ready=0)
            spread_sumsq(0)
            tiles(0, 2, a_hi, a_lo)

            def pair_tiles(i, m, beside):
                for t in range(Z_PAIR):
                    pe.wait_ge(sg("acc_taken"), i * Z_PAIR + (m + t + 1))
                    gemm(acc[t % 2][:, :], a_hi, a_lo, i * (2 * Z_PAIR) + (Z_ODD + 2 * (m + t)), beside=lambda u: beside(i, 2 * t + u))

            def once(_, at):
                if at == 9:
                    pe.wait_ge(sg("f_cumulated"), 1)
                    for q in range(T // P):
                        last = mm(bank[0][:, q * 16:(q + 1) * 16], f1[:, q * P:(q + 1) * P], ident[0:16, 0:16], start=True, stop=True)
                    last.then_inc(sg("c_transposed"), 1)

            def logits(i, k):
                ph = slice(k * HD, (k + 1) * HD)
                for q, dst in enumerate(logit_banks):
                    mm(dst, qh[ph, q * P:(q + 1) * P], kh[ph, 0:(q + 1) * P], start=True, stop=True).then_inc(sg("logits_done"), 1)

            def transpose_probs(i, k):
                pe.wait_ge(sg("probs_ready"), i * 2 + (k + 1))
                for j, dst in enumerate(prob_banks):
                    for q in range(j, T // P):
                        last = nc.tensor.transpose(dst[:, (q - j) * P:(q - j + 1) * P], pr[:, q, j * P:(j + 1) * P], ident)
                last.then_inc(sg("probs_t_done"), 1)

            def weigh_values(i, k):
                ph = slice(k * HD, (k + 1) * HD)
                pe.wait_ge(sg("probs_t_taken"), i * 2 + (k + 1))
                for j in range(T // P):
                    last = mm(bank[1][ph, j * P:], vtm[:, j, ph], prt[:, j, j * P:], start=j == 0, stop=j == T // P - 1)
                last.then_inc(sg("heads_done"), 1)

            def side(i, at):
                if at == 2:
                    pe.wait_ge(sg("side_landed"), i * 144 + 144)
                    pe.wait_ge(sg("lora_features_ready"), 1)
                    pe.wait_ge(sg("fox_taken"), i + 1)
                    mm(bank[0][:, :], wa_in[0:64, :], tx[0:64, :], start=True, stop=True)
                    mm(bank[1][:, :], wa_in[64:128, :], tx[64:128, :], start=True, stop=True).then_inc(sg("lora_multiplied"), 1)
                    pe.wait_ge(sg("k_squares_ready"), i + 1)
                    pe.wait_ge(sg("qk_squares_ready"), i * 2 + 2)
                    for q in range(T // P):
                        for n, src in enumerate((t1[:, :], sq[:, 0, :], sq[:, 1, :])):
                            last = mm(bank[5][:, 6 * q + 2 * n:6 * q + 2 * n + 2], src[:, q * P:(q + 1) * P], head_of, start=True, stop=True)
                    last.then_inc(sg("head_sums_done"), 1)
                if at == 3:
                    pe.wait_ge(sg("head_inverse_ready"), i + 1)
                    for q in range(T // P):
                        last = mm(bank[5][0:6, q * P:(q + 1) * P], hr[:, 6 * q:6 * q + 6], ident, start=True, stop=True)
                    last.then_inc(sg("head_rows_done"), 1)
                if at == 4:
                    pe.wait_ge(sg("head_rows_ready"), i + 1)
                    for n in range(3):
                        last = mm(bank[2 + n][:, :], spread[:, n, :], hrt[0:6, :], start=True, stop=True)
                    last.then_inc(sg("head_spread"), 1)
                if at == 5:
                    pe.wait_ge(sg("qk_ready"), i * 3 + 3)
                    logits(i, 0)
                    pe.wait_ge(sg("fv_landed"), i * 16 + 16)
                    for q in range(T // P):
                        last = nc.tensor.transpose(bank[0][:, q * P:(q + 1) * P], v_in[:, q * P:(q + 1) * P], ident)
                    last.then_inc(sg("fv_done"), 1)
                if at == 7:
                    pe.wait_ge(sg("rk_ready"), i + 1)
                    mm(bank[1][:, :], const(C_BLK, P), t2[:, :], start=True, stop=True).then_inc(sg("bonus_summed"), 1)
                if at == 7.5:
                    pe.wait_ge(sg("fv_ready"), i + 1)
                    transpose_probs(i, 0)
                if at == 8:
                    pe.wait_ge(sg("probs_t_taken"), i * 2 + 1)
                    logits(i, 1)
                    pe.wait_ge(sg("bonus_taken"), i + 1)
                    weigh_values(i, 0)
                if at == 10.5:
                    transpose_probs(i, 1)
                if at == 11.5:
                    weigh_values(i, 1)

            pair_tiles(0, 2, once)
            with pe.Fori(0, NPAIR - 1) as i:
                pair_tiles(i, 2 + Z_PAIR, side)
            for at in (2, 3, 4, 5, 7, 7.5, 8, 10.5, 11.5):
                side(NPAIR - 1, at)

            pe.wait_ge(sg("diagonals_cleared"), N_CLEAR)
            pe.wait_ge(sg("fox_taken"), NPAIR + 1)

            def each(g, dst, lhs, rhs, sem):
                for n in range(H):
                    last = mm(m3(dst, H)[:, n, :], lhs(g * H + n), rhs(g * H + n), start=True, stop=True)
                last.then_inc(sg(sem), 1)

            def chunk(j, b):
                abd, bbd, kbd, vbd, ars = loads[b]

                def wait(name, g, n, k):
                    pe.wait_ge(sg(name), j * (4 * n) + (2 * (b * n + k) - 1 + g))

                pe.wait_ge(sg(f"chunk_landed{b}"), 144 * j + 144)
                for k, src in enumerate((bbd, kbd)):
                    for g in range(2):
                        each(g, gbank[g][k][:, :], lambda n: flat2(src[:, n, :, :]), lambda n: flat2(ars[:, n, :, :]), "products_done")
                for k, src, free in ((2, bbd, "state_ready"), (3, kbd, "y_taken"), (0, vbd, "products_ready")):
                    for g in range(2):
                        if k:
                            wait(free, g, 1, 1)
                        else:
                            wait(free, g, 2, 1)
                        for n in range(H):
                            last = nc.tensor.transpose(gbank[g][k][:, n * P:(n + 1) * P], flat2(src[:, g * H + n, :, :]), ident)
                        last.then_inc(sg("transposes_done"), 1)
                for g in range(2):
                    wait("products_ready", g, 2, 2)
                    wait("x_bd_ready", g, 6, 1)
                    each(g, gbank[g][1][:, 0:H * C], lambda n: flat2(xbd[:, n, :, :]), lambda n: eye2, "xt0_done")
                for lv in range(1, 6):
                    for g in range(2):
                        wait("n_ready", g, 5, lv)
                        wait("xt_ready", g, 5, lv)
                        each(g, gbank[g][1][:, 0:H * C], lambda n: flat2(nbd[:, lv % 2, n, :, :]), lambda n: xt[:, n, :], "pt_done")
                    for g in range(2):
                        if lv == 1:
                            wait("transposes_taken", g, 3, 1)
                        wait("pt_ready_a", g, 5, lv)
                        wait("pt_ready_b", g, 5, lv)
                        each(g, gbank[g][2][:, 0:H * C], lambda n: flat2(ptbd[:, n, :, :]), lambda n: xs[:, n, :], "dx_done")
                    if lv < 5:
                        for g in range(2):
                            if lv == 1:
                                wait("transposes_taken", g, 3, 2)
                            wait("x_bd_ready", g, 6, lv)
                            each(g, gbank[g][3][:, 0:H * C], lambda n: flat2(xbd[:, n, :, :]), lambda n: pt[:, n, :], "dxt_done")
                for g in range(2):
                    wait("m_ready", g, 1, 1)
                    wait("v_stacked", g, 1, 1)
                    wait("state_ready", g, 1, 1)
                    for n in range(g * H, (g + 1) * H):
                        o = half(g, 0)[:, n % H, :]
                        mm(o, flat2(abd[:, n, :, :]), st[:, n, :], start=True, stop=False)
                        last = mm(o, flat2(mbd[:, n, :, :]), vst[:, n, :], start=False, stop=True)
                    last.then_inc(sg("r_done"), 1)
                for g in range(2):
                    wait("r_ready", g, 1, 1)
                    wait("x_bd_ready", g, 6, 6)
                    each(g, gbank[g][1][:, 0:H * C], lambda n: flat2(xbd[:, n, :, :]), lambda n: rr[:, n, :], "sa_done")
                for g in range(2):
                    wait("sa_ready_a", g, 1, 1)
                    wait("sa_ready_b", g, 1, 1)
                    for n in range(g * H, (g + 1) * H):
                        o = half(g, 2)[:, n % H, :]
                        mm(o, bt[:, n, :], sa[:, n, :], start=True, stop=False)
                        last = mm(o, ktm[:, n, :], vst[:, n, :], start=False, stop=True)
                    last.then_inc(sg("s_done"), 1)
                for g in range(2):
                    wait("state_bd_ready_a", g, 1, 1)
                    wait("state_bd_ready_b", g, 1, 1)
                    for n in range(g * H, (g + 1) * H):
                        o = half(g, 3)[:, n % H, :]
                        mm(o, flat2(stbd[:, n, :, :]), ars[:, n, 1, :], start=True, stop=False)
                        mm(o, flat2(sabd[:, n, :, :]), gb[:, n, 1, :], start=False, stop=False)
                        last = mm(o, vt[:, n, :], gk[:, n, 1, :], start=False, stop=True)
                    last.then_inc(sg("y_multiplied"), 1)

            with pe.Fori(0, NC // 2) as j:
                for b in range(2):
                    chunk(j, b)

            pe.wait_ge(sg("output_landed"), 16 * 6)
            pe.wait_ge(sg("y_taken"), 2 * NC + 2)
            for i in range(NPAIR // NB):
                for n in range(NB):
                    if i:
                        pe.wait_ge(sg("y_scaled"), NB * (i - 1) + n + 1)
                    mm(bank[n][:, :], const(C_BLK, P), y_all[:, NB * i + n, :], start=True, stop=True).then_inc(sg("mean_done"), 1)

                def gate(n):
                    if i:
                        pe.wait_ge(sg("y_finished"), NB * (i - 1) + n + 1)
                    else:
                        pe.wait_ge(sg("state_ready"), 2 * NC + 2)
                    f = slice((NB * i + n) * P, (NB * i + n + 1) * P)
                    mm(gate_banks[n][:, :], g2a[:, f], sga[:, :], start=True, stop=False)
                    mm(gate_banks[n][:, :], g2b[:, f], sgb[:, :], start=False, stop=True).then_inc(sg("gates_done"), 1)

                for n in range(NB - 1):
                    gate(n)
                if i:
                    pe.wait_ge(sg("y_finished"), NB * i)
                for n in range(NB):
                    pe.wait_ge(sg("y_squares_ready"), NB * i + n + 1)
                    for q in range(T // P):
                        last = mm(bank[5][:, 8 * q + 2 * n:8 * q + 2 * n + 2], squares[n][:, q * P:(q + 1) * P], head_of, start=True, stop=True)
                last.then_inc(sg("head_sums_done"), 1)
                pe.wait_ge(sg("head_inverse_ready"), NPAIR + i + 1)
                for q in range(T // P):
                    last = mm(bank[5][0:8, q * P:(q + 1) * P], hr[:, 8 * q:8 * q + 8], ident, start=True, stop=True)
                last.then_inc(sg("head_rows_done"), 1)
                pe.wait_ge(sg("head_rows_ready"), NPAIR + i + 1)
                pe.wait_ge(sg("output_landed"), 16 * 11)
                for n in range(NB):
                    mm(bank[n][:, :], spread4[:, n, :], hrt[:, :], start=True, stop=True).then_inc(sg("head_spread"), 1)
                gate(NB - 1)

            pe.wait_ge(sg("operand_split"), 2 * KT)
            tiles(M_OUT, KT, a_hi, a_lo)
            tiles(M_FF, 2, b_hi, b_lo, ready=2 * KT, beside=lambda u: spread_sumsq(1) if u == 1 else None)
            tiles(M_FF + 2, KT - 2, b_hi, b_lo)
            tiles(M_FF + KT, KT, a_hi, a_lo, ready=3 * KT)
            with pe.Fori(0, FG - 1) as g:
                tiles(M_FF + 2 * KT, KT, b_hi, b_lo, outer=g * (2 * KT))
                tiles(M_FF + 3 * KT, KT, a_hi, a_lo, ready=g * KT + 4 * KT, outer=g * (2 * KT))

            def prepare(u):
                if u == 1:
                    spread_sumsq(2)
                    pe.wait_ge(sg("p_landed"), 16)
                    for k in range(2):
                        for q in range(T // P):
                            last = nc.tensor.transpose(bank[k][:, q * P:(q + 1) * P], p_in[:, q, k * P:(k + 1) * P], ident)
                    last.then_inc(sg("p_transposed"), 1)

            def embed(i, b):
                pe.wait_ge(sg("p_split"), 1)
                pe.wait_ge(sg("ple_split"), 2 * i + b + 3)
                pe.wait_ge(sg("ple_taken"), 2 * i + b + 1)
                for k in range(2):
                    mm(bank[b][:, :], pw_hi[:, b, k, :], p_hi[:, k, :], start=k == 0, stop=False)
                    mm(bank[b][:, :], pw_hi[:, b, k, :], p_lo[:, k, :], start=False, stop=False)
                    last = mm(bank[b][:, :], pw_lo[:, b, k, :], p_hi[:, k, :], start=False, stop=k == 1)
                last.then_inc(sg("ple_done"), 1)

            tiles(M_GATE, 2, b_hi, b_lo, ready=(3 + FG) * KT, after=embed, beside=prepare)
            tiles(M_GATE + 2, KT - 2, b_hi, b_lo, after=lambda i, b: embed(i + 1, b))
            spread_sumsq(3)
            with pe.Fori(0, KT // 4) as i:
                for b in range(4):
                    pe.wait_ge(sg("final_ready"), 4 * i + b + 1)
                    pe.wait_ge(sg("out_ready"), 4 * i + b + 1)
                    for q in range(T // P):
                        last = nc.tensor.transpose(bank[2 + b][:, q * P:(q + 1) * P], hn[:, b, q * P:(q + 1) * P], ident)
                    last.then_inc(sg("final_transposed"), 1)

        @block.scalar
        def _(act):
            act.sem_inc(sg("y_taken"), 2)
            act.sem_inc(sg("state_bd_ready_a"), 2)
            act.sem_inc(sg("fox_taken"), 1)
            act.sem_inc(sg("fox_stored"), 16)
            act.sem_inc(sg("features_stored"), 48)
            act.sem_inc(sg("out_ready"), 4)
            for b in range(4):
                act.sem_inc(sg(f"out_stored{b}"), 16)
            A = nc.scalar.activation

            def settled():
                act.sem_inc(sg("act_waits_taken"), 1)

            def hi_unit(s, i, m, outer=0, a_turn=2):
                act.wait_ge(sg(f"w_landed{s}"), i * (16 * a_turn) + outer * 16 + 16 * (m + 3))
                act.wait_ge(sg("unit_done"), i * (2 * a_turn) + outer * 2 + (Z_ODD + 2 * m + s + 1))
                A(w_hi[:, s, :, :], w_raw[:, s, :, :], ACT.Copy).then_inc(sg("w_hi_ready"), 1)

            def next_units(i, m, outer=0, between=None):
                for s in range(2):
                    hi_unit(s, i, m + 1, outer)
                    if between and s == 0:
                        between()

            def fold(hi, gain, f, n, b, gains=True):
                act.wait_ge(sg("h_ready"), n + 1)
                if gains:
                    A(hi[:, bass.ds(f, 1), :], h[:, bass.ds(f, 1), :], ACT.Copy, scale=pc(gain, f)).then_inc(sg("operand_hi_ready"), 1)
                act.wait_ge(sg("squares_summed"), n + 1)
                settled()
                A(sq[:, b:b + 1, :], h[:, bass.ds(f, 1), :], ACT.Square).then_inc(sg("squares_ready"), 1)

            def root(n):
                act.wait_ge(sg("mean_square_ready"), n + 1)
                A(tmp[:, :], tmp[:, :], ACT.Sqrt).then_inc(sg("rms_ready"), 1)

            act.wait_ge(sg("gain_transposed"), 1)
            A(par[:, 0:16], bank[0][:, 0:16], ACT.Copy).then_inc(sg("gain_ready"), 1)
            act.wait_ge(sg("gain_ready"), 1)
            with act.Fori(0, KT // 2) as i:
                for b in range(2):
                    fold(a_hi, "norm_mix", 2 * i + b, 2 * i + b, b)
            for s in range(2):
                act.wait_ge(sg(f"w_landed{s}"), 32)
                act.wait_ge(sg("unit_done"), s + 1)
                A(w_hi[:, s, :, 0:48], w_raw[:, s, :, 0:48], ACT.Copy).then_inc(sg("w_hi_ready"), 1)
            next_units(0, -1)
            root(0)
            act.wait_ge(sg("parameters_transposed"), 1)
            A(par[:, 16:], bank[4][:, 16:160], ACT.Copy).then_inc(sg("parameters_ready"), 1)
            act.wait_ge(sg("parameters_ready"), 1)

            def stage(m, count, outer=0, body=None, between=None):
                with act.Fori(0, count // 2) as i:
                    for b in range(2):
                        next_units(i, m + b, outer, None if b else between)
                        if body:
                            body(i, b)

            stage(0, 2)

            def pair_tiles(i, m, beside):
                for t in range(Z_PAIR):
                    for s in range(2):
                        hi_unit(s, i, m + t + 1, a_turn=Z_PAIR)
                        beside(i, 2 * t + s + 1)

            def once(_, at):
                if at == 7:
                    act.wait_ge(sg("f_prepared"), 1)
                    A(f2[:, :], f2[:, :], ACT.Exp, scale=-1.0).then_inc(sg("f_exp"), 1)
                    act.wait_ge(sg("f_exp"), 1)
                    A(f2[:, :], f2[:, :], ACT.Ln, bias=cst[0:16, C_ONE:C_ONE + 1]).then_inc(sg("f_log"), 1)
                if at == 9:
                    act.wait_ge(sg("c_ready"), 1)
                    act.dma_start(c_d, f3[:, :]).then_inc(sg("c_stored"), 16)
                    act.wait_ge(sg("c_transposed"), 1)
                    A(cq[:, :, :], bank[0][:, 0:64].rearrange("p (q n) -> p q n", q=4), ACT.Copy).then_inc(sg("cq_ready"), 1)
                if at == 10:
                    act.wait_ge(sg("lora_shifted"), 1)
                    A(tx[0:64, :], t1[0:64, :], ACT.Tanh)
                    A(tx[64:128, :], t1[64:128, :], ACT.Copy)
                if at == 11:
                    act.wait_ge(sg("lora_shifted"), 3)
                    A(sga[:, :], t2[:, :], ACT.Sigmoid)
                    A(sgb[:, :], ks[0:32, :], ACT.Sigmoid).then_inc(sg("lora_features_ready"), 1)

            def exps(i, k):
                for q in range(T // P):
                    act.wait_ge(sg("logits_max_ready"), i * 8 + (4 * k + q + 1))
                    w = pr[:, q, 0:(q + 1) * P]
                    A(w, w, ACT.Exp, bias=nmx[:, q:q + 1], accum_out=rsum[:, q:q + 1]).then_inc(sg("exp_ready"), 1)

            def normalize(i, k):
                act.wait_ge(sg("sums_inverted"), i * 2 + (k + 1))
                for q in range(T // P):
                    w = pr[:, q, 0:(q + 1) * P]
                    last = A(w, w, ACT.Copy, scale=rinv[:, q:q + 1])
                last.then_inc(sg("probs_ready"), 1)

            def take_probs(i, k):
                act.wait_ge(sg("probs_t_done"), i * 2 + (k + 1))
                if k:
                    act.wait_ge(sg("heads_done"), i * 2 + 1)
                for j, src in enumerate(prob_banks):
                    last = A(prt[:, j, j * P:], src, ACT.Copy)
                last.then_inc(sg("probs_t_taken"), 1)

            def side(i, at):
                if at == 1:
                    act.wait_ge(sg("side_landed"), i * 144 + 144)
                    for k, src in enumerate((qin, k_in)):
                        A(sq[:, k, :], src[:, :], ACT.Square).then_inc(sg("qk_squares_ready"), 1)
                if at == 2:
                    act.wait_ge(sg("lora_multiplied"), i + 1)
                    settled()
                    A(lw[:, :], bank[0][:, :], ACT.Sigmoid, bias=pc("w0", i)).then_inc(sg("sigmoids_ready"), 1)
                    A(av[:, :], bank[1][:, :], ACT.Sigmoid, bias=pc("a0", i)).then_inc(sg("sigmoids_ready"), 1)
                    act.wait_ge(sg("head_means_ready"), i + 1)
                    A(hr[:, 0:24], hs[:, 0:24], ACT.Sqrt).then_inc(sg("head_roots_ready"), 1)
                if at == 3:
                    act.wait_ge(sg("head_rows_done"), i + 1)
                    A(hrt[0:6, :], bank[5][0:6, :], ACT.Copy).then_inc(sg("head_rows_ready"), 1)
                    act.wait_ge(sg("cum_ready"), i + 1)
                    A(e_in[:, :], cum[:, :], ACT.Exp).then_inc(sg("exps_ready"), 1)
                    A(e_no[:, :], cum[:, :], ACT.Exp, scale=-1.0).then_inc(sg("exps_ready"), 1)
                    A(e_ex[:, :], cex[:, :], ACT.Exp).then_inc(sg("exps_ready"), 1)
                if at == 4:
                    act.wait_ge(sg("exps_ready"), i * 3 + 1)
                    settled()
                    A(ec[:, bass.ds(i, 1), :], e_in[:, :].rearrange("p (a c t) -> p a c t", a=1, c=NC)[:, :, :, C - 1], ACT.Copy).then_inc(sg("ends_ready"), 1)
                if at == 5:
                    act.wait_ge(sg("fv_done"), i + 1)
                    A(vtm[:, :, :], bank[0][:, :].rearrange("p (q n) -> p q n", q=4), ACT.Copy).then_inc(sg("fv_ready"), 1)
                    exps(i, 0)
                if at == 6:
                    normalize(i, 0)
                if at == 7:
                    take_probs(i, 0)
                if at == 8:
                    act.wait_ge(sg("features_made"), i + 1)
                    act.dma_start(ab_d[:, :, bass.ds(i, 1), :, :].rearrange("c p a k t -> p c (a k t)"), ab[:, :, :, :].rearrange("p c k t -> p c (k t)")).then_inc(sg("features_stored"), 16)
                    act.dma_start(v_d[:, :, bass.ds(i, 1), :].rearrange("c p a t -> p c (a t)"), vs[:, :].rearrange("p (c t) -> p c t", c=NC)).then_inc(sg("features_stored"), 16)
                    act.dma_start(bonus_d[bass.ds(i, 1), :, :].rearrange("a p t -> (a p) t"), bon[:, :]).then_inc(sg("features_stored"), 16)
                    exps(i, 1)
                if at == 9:
                    normalize(i, 1)
                if at == 10:
                    take_probs(i, 1)
                if at == 12:
                    act.wait_ge(sg("heads_done"), i * 2 + 2)
                    act.wait_ge(sg("fox_stored"), i * 16 + 16)
                    A(og[:, :], bank[1][:, :], ACT.Copy).then_inc(sg("fox_taken"), 1)
                    act.wait_ge(sg("fox_taken"), i + 2)
                    act.dma_start(fox_d[bass.ds(i, 1), :, :].rearrange("a p t -> (a p) t"), og[:, :]).then_inc(sg("fox_stored"), 16)

            pair_tiles(0, 2, once)
            with act.Fori(0, NPAIR - 1) as i:
                pair_tiles(i, 2 + Z_PAIR, side)
            for at in range(1, 13):
                side(NPAIR - 1, at)

            def chunk(j, b):
                def wait(name, g, n, k):
                    act.wait_ge(sg(name), j * (4 * n) + (2 * (b * n + k) - 1 + g))

                lo = slice(0, HD)

                def transposed(k):
                    dst = (bt, ktm, vt)[k]
                    for g in range(2):
                        wait("transposes_done", g, 3, k + 1)
                        A(dst[:, pairs[g], :], m3(gbank[g][(2, 3, 0)[k]][:, :], H), ACT.Copy).then_inc(sg("transposes_taken"), 1)

                def x_on_diagonal(g):
                    A(xbd[0:HD, pairs[g], 0, :], xs[0:HD, pairs[g], :], ACT.Copy)
                    A(xbd[HD:P, pairs[g], 1, :], xs[HD:P, pairs[g], :], ACT.Copy).then_inc(sg("x_bd_ready"), 1)

                for g in range(2):
                    wait("x_ready", g, 6, 1)
                    x_on_diagonal(g)
                transposed(0)
                for lv in range(1, 6):
                    for g in range(2):
                        wait("pt_done", g, 5, lv)
                        A(ptbd[lo, pairs[g], 0, :], half(g, 1, lo), ACT.Copy)
                        A(pt[lo, pairs[g], :], half(g, 1, lo), ACT.Copy).then_inc(sg("pt_ready_a"), 1)
                    if lv < 3:
                        transposed(lv)
                    for g in range(2):
                        wait("x_ready", g, 6, lv + 1)
                        if lv < 5:
                            wait("dxt_done", g, 4, lv)
                        x_on_diagonal(g)
                for g in range(2):
                    wait("sa_done", g, 1, 1)
                    wait("y_multiplied", g, 1, 1)
                    A(sabd[lo, pairs[g], 0, :], half(g, 1, lo), ACT.Copy)
                    A(sa[lo, pairs[g], :], half(g, 1, lo), ACT.Copy).then_inc(sg("sa_ready_a"), 1)
                for g in range(2):
                    wait("y_multiplied", g, 1, 2)
                    settled()
                    A(y_all[:, pairs[g], bass.ds(j * (2 * C) + b * C, C)], half(g, 3), ACT.Copy).then_inc(sg("y_taken"), 1)
                    wait("state_ready", g, 1, 2)
                    A(stbd[lo, pairs[g], 0, :], st[lo, pairs[g], :], ACT.Copy).then_inc(sg("state_bd_ready_a"), 1)

            with act.Fori(0, NC // 2) as j:
                for b in range(2):
                    chunk(j, b)

            for i in range(NPAIR // NB):
                for n in range(NB):
                    act.wait_ge(sg("y_centred"), NB * i + n + 1)
                    A(squares[n], y_all[:, NB * i + n, :], ACT.Square).then_inc(sg("y_squares_ready"), 1)
                act.wait_ge(sg("head_means_ready"), NPAIR + i + 1)
                A(hr[:, :], hs[:, :], ACT.Sqrt).then_inc(sg("head_roots_ready"), 1)
                act.wait_ge(sg("head_rows_done"), NPAIR + i + 1)
                A(hrt[:, :], bank[5][0:8, :], ACT.Copy).then_inc(sg("head_rows_ready"), 1)
                if i == 0:
                    act.wait_ge(sg("output_landed"), 16 * 11)
                for n in range(NB):
                    A(a_hi[:, NPAIR + NB * i + n, :], yf[:, NB * i + n, :], ACT.Copy).then_inc(sg("operand_hi_ready"), 1)
                    act.wait_ge(sg("y_scaled"), NB * i + n + 1)
                    y = y_all[:, NB * i + n, :]
                    A(y, y, ACT.Identity, bias=pc("gn_b", NB * i + n), scale=pc("gn_w", NB * i + n)).then_inc(sg("y_affine"), 1)
                    for k in {0: (), NB - 1: (NB - 2, NB - 1)}.get(n, (n - 1,)):
                        act.wait_ge(sg("y_finished"), NB * i + k + 1)
                        A(a_hi[:, NB * i + k, :], y_all[:, NB * i + k, :], ACT.Copy).then_inc(sg("operand_hi_ready"), 1)

            stage(M_OUT, KT, body=lambda i, b: fold(b_hi, "norm_mlp", 2 * i + b, 2 * i + (b + KT), b))

            def hidden(g):
                def body(i, b):
                    act.wait_ge(sg("relu_squared"), 2 * i + g * KT + (b + 1))
                    settled()
                    A(a_hi[:, bass.ds(2 * i + b, 1), :], sq[:, b:b + 1, :], ACT.Copy).then_inc(sg("operand_hi_ready"), 1)
                return body

            stage(M_FF, 2, body=hidden(0), between=lambda: root(1))
            stage(M_FF + 2, KT - 2, body=lambda i, b: hidden(0)(i + 1, b))
            stage(M_FF + KT, KT)
            with act.Fori(0, FG - 2) as g:
                stage(M_FF + 2 * KT, KT, outer=g * (2 * KT), body=hidden(g + 1))
                stage(M_FF + 3 * KT, KT, outer=g * (2 * KT))
            stage(M_GATE - 2 * KT, KT, body=hidden(FG - 1))
            stage(M_GATE - KT, KT, body=lambda i, b: fold(b_hi, "norm_ple", 2 * i + b, 2 * i + (b + 2 * KT), b))

            def prepare():
                root(2)
                act.wait_ge(sg("p_transposed"), 1)
                for k in range(2):
                    A(p_t[:, k, :], bank[k][:, :], ACT.Copy).then_inc(sg("p_taken"), 1)
                act.wait_ge(sg("p_taken"), 2)
                A(p_hi[:, :, :], p_t[:, :, :], ACT.Copy).then_inc(sg("p_hi_ready"), 1)

            def gated(i, b):
                act.wait_ge(sg("gate_scaled"), 2 * i + (b + 1))
                A(gt[:, b, :], ev[:, b, :], ACT.Sigmoid).then_inc(sg("gate_ready"), 1)
                fold(None, None, 2 * i + b, 2 * i + (b + 3 * KT), b, gains=False)

            def ple_units(i, b):
                act.wait_ge(sg(f"ple_landed{b}"), i * 16 + 16)
                act.wait_ge(sg("ple_done"), i * 2 + b + 1)
                A(pw_hi[:, b, :, :], pw[:, b, :, :], ACT.Copy).then_inc(sg("ple_hi_ready"), 1)

            ple_units(0, 0)
            next_units(0, M_GATE, between=prepare)
            gated(0, 0)
            ple_units(0, 1)
            next_units(0, M_GATE + 1)
            gated(0, 1)
            with act.Fori(0, KT // 2 - 2) as i:
                for b in range(2):
                    ple_units(i + 1, b)
                    next_units(i, M_GATE + 2 + b)
                    gated(i + 1, b)
            i = KT // 2 - 1
            ple_units(i, 0)
            next_units(i, M_GATE)
            gated(i, 0)
            ple_units(i, 1)
            gated(i, 1)
            root(3)
            with act.Fori(0, KT // 4) as i:
                for b in range(4):
                    act.wait_ge(sg("final_transposed"), 4 * i + b + 5)
                    act.wait_ge(sg(f"out_stored{b}"), 16 * i + 16)
                    A(ot[:, b, :, :], bank[2 + b][:, :].rearrange("p (q n) -> p q n", q=4), ACT.Copy).then_inc(sg("out_ready"), 1)

        @block.vector
        def _(dve):
            V = nc.vector
            for name, n in (("xt_taken", 2), ("w_split", 2), ("acc_taken", 2), ("side_inputs_used", 1),
                            ("ple_split", 2), ("ple_taken", 2)):
                dve.sem_inc(sg(name), n)
            chain = [0, 0, 0]

            def then(ins):
                ins.then_inc(sg("dve_chain"), 1)
                chain[0] += 1
                dve.wait_ge(sg("dve_chain"), chain[0] + (chain[1] * chain[2] if chain[2] else 0))

            def chained(i, steps):
                chain[1], chain[2] = i, steps
                return chain[0] + steps

            def unchained(turns, end):
                assert end == chain[0], f"steps a turn: {chain[0] - end + chain[2]}"
                chain[0] += chain[2] * (turns - 1)
                chain[1], chain[2] = 0, 0

            def lo_unit(s, n, width=P):
                dve.wait_ge(sg("w_hi_ready"), n + 1)
                V.tensor_tensor(w_lo[:, s, :, 0:width], w_raw[:, s, :, 0:width], w_hi[:, s, :, 0:width].bitcast(F32),
                                ALU.subtract).then_inc(sg("w_split"), 1)

            def next_units(i, m, outer=0, early=None, between=None):
                if early:
                    early()
                for s in range(2):
                    lo_unit(s, i * 4 + outer * 2 + (Z_ODD + 2 * (m + 1) + s))
                    if between and s == 0:
                        between()

            def fold(hi, lo, gain, f, n):
                dve.wait_ge(sg("operand_hi_ready"), n + 1)
                V.scalar_tensor_tensor(lo[:, bass.ds(f, 1), :], h[:, bass.ds(f, 1), :], pc(gain, f), hi[:, bass.ds(f, 1), :].bitcast(F32),
                                       ALU.mult, ALU.subtract).then_inc(sg("operand_split"), 1)

            def mean_square(n):
                dve.wait_ge(sg("sumsq_spread"), n + 1)
                V.tensor_scalar(tmp[:, :], bank[3][:, :], 1.0 / D, EPS, ALU.mult, ALU.add).then_inc(sg("mean_square_ready"), 1)

            def invert_root(n):
                dve.wait_ge(sg("rms_ready"), n + 1)
                then(V.reciprocal(rstd[:, :], tmp[:, :]))

            def invert_rms(n):
                mean_square(n)
                invert_root(n)

            def stage(m, count, outer=0, body=None, early=None, between=None):
                with dve.Fori(0, count // 2) as i:
                    for b in range(2):
                        if b:
                            next_units(i, m + b, outer)
                        else:
                            next_units(i, m, outer, early, between)
                        dve.wait_ge(sg("unit_done"), i * 4 + outer * 2 + (2 + Z_ODD + 2 * (m + b + 1)))
                        body(i, b)

            def take_x(f, b):
                dve.wait_ge(sg("x_transposed"), f + 5)
                V.tensor_copy(h[:, bass.ds(f, 1), :], bank[1 + b][:, :].rearrange("p (a t) -> p a t", a=1)).then_inc(sg("h_ready"), 1)
                dve.wait_ge(sg("h_ready"), f + 1)
                dve.sem_inc(sg("xt_taken"), 1)

            dve.wait_ge(sg("gain_ready"), 1)
            take_x(0, 0)
            with dve.Fori(0, KT // 2 - 1) as i:
                for b in range(2):
                    take_x(2 * i + (b + 1), 1 - b)
                    fold(a_hi, a_lo, "norm_mix", 2 * i + b, 2 * i + b)
            take_x(KT - 1, 1)
            fold(a_hi, a_lo, "norm_mix", KT - 2, KT - 2)
            fold(a_hi, a_lo, "norm_mix", KT - 1, KT - 1)
            lo_unit(0, 0, 48)
            lo_unit(1, 1, 48)
            next_units(0, -1)
            invert_rms(0)
            dve.wait_ge(sg("parameters_ready"), 1)
            dve.wait_ge(sg("unit_done"), 2 + Z_ODD)
            V.tensor_tensor(ev[0:48, 0, :], bank[0][0:48, :], rstd[0:48, :], ALU.mult).then_inc(sg("odd_ready"), 1)

            def project(i, b):
                for part in range(2):
                    dve.wait_ge(sg(f"ev_free{part}"), 16)
                V.tensor_tensor(ev[:, b, :], acc[b][:, :], rstd[:, :], ALU.mult).then_inc(sg("acc_taken"), 1)

            stage(0, 2, body=project)

            def pair_tiles(i, m, beside):
                for t in range(Z_PAIR):
                    b = t % 2
                    for s in range(2):
                        lo_unit(s, i * (2 * Z_PAIR) + (Z_ODD + 2 * (m + t + 1) + s))
                        if s:
                            dve.wait_ge(sg("unit_done"), i * (2 * Z_PAIR) + (2 + Z_ODD + 2 * (m + t + 1)))
                            dve.wait_ge(sg(f"ev_free{b}"), i * 48 + 16 * ((m + t) // 2 + 1))
                            V.tensor_tensor(ev[:, b, :], acc[b][:, :], rstd[:, :], ALU.mult).then_inc(sg("acc_taken"), 1)
                        beside(i, 2 * t + s + 1)

            def shift(dst, src, mu, parts=P):
                then(V.tensor_tensor(dif[0:parts, :], src[0:parts, 0:T], src[0:parts, 1:], ALU.subtract))
                return V.scalar_tensor_tensor(dst, dif[0:parts, :], mu[0:parts, :], src[0:parts, 1:], ALU.mult, ALU.add)

            def once(_, at):
                if at == 7:
                    dve.wait_ge(sg("once_landed"), 16 * 7)
                    then(V.tensor_scalar(fin[:, :], fin[:, :], bf[:, :], None, ALU.add))
                    then(V.tensor_scalar(f1[:, :], fin[:, :], -1.0, None, ALU.mult))
                    V.tensor_tensor(f2[:, :], fin[:, :], f1[:, :], ALU.max).then_inc(sg("f_prepared"), 1)
                    then(V.tensor_scalar(f3[:, :], fin[:, :], 0.0, None, ALU.min))
                if at == 8:
                    dve.wait_ge(sg("f_log"), 1)
                    then(V.tensor_tensor(f3[:, :], f3[:, :], f2[:, :], ALU.subtract))
                    then(V.memset(f2[:, :], 1.0))
                    V.tensor_tensor_scan(f1[:, :], f2[:, :], f3[:, :], 0.0, ALU.mult, ALU.add).then_inc(sg("f_cumulated"), 1)
                    dve.wait_ge(sg("f_cumulated"), 1)
                    V.tensor_scalar(f3[:, :], f1[:, :], -1.0, None, ALU.mult).then_inc(sg("c_ready"), 1)
                    then(V.tensor_scalar(qs[:, :], par[:, 120:121], HD ** -0.5, None, ALU.mult))
                if at == 9:
                    dve.wait_ge(sg("first_columns_zero"), 6)
                    shift(t1[:, :], xin_wa, pc("mu", 24)).then_inc(sg("lora_shifted"), 1)
                    dve.wait_ge(sg("lora_shifted"), 1)
                    shift(t2[:, :], xin_g, pc("mu", 25)).then_inc(sg("lora_shifted"), 1)
                if at == 10:
                    dve.wait_ge(sg("lora_shifted"), 2)
                    shift(ks[0:32, :], xin_h, pc("mu", 26), 32).then_inc(sg("lora_shifted"), 1)
                if at == 12:
                    dve.wait_ge(sg("lora_features_ready"), 1)
                    dve.wait_ge(sg("cq_ready"), 1)
                    dve.wait_ge(sg("c_stored"), 16)

            def by_chunk(t):
                return t[:, :].rearrange("p (c t) -> p c t", c=NC)

            def logits(i, k):
                for q, src in enumerate(logit_banks):
                    w = (q + 1) * P
                    dve.wait_ge(sg("logits_done"), i * 8 + (4 * k + max(q, 1) + 1))
                    if k and q == 0:
                        dve.wait_ge(sg("probs_t_done"), i * 2 + 1)
                    then(V.scalar_tensor_tensor(pr[:, q, 0:w], src, cq[:, q, bass.ds(i * 2 + k, 1)], ncb[:, k, 0:w], ALU.add, ALU.add))
                    then(V.tensor_tensor(pr[:, q, q * P:w], pr[:, q, q * P:w], const(C_CAUS, P), ALU.add))
                    then(V.reduce_max(mx[:, q:q + 1], pr[:, q, 0:w], AX.X))
                    V.tensor_scalar(nmx[:, q:q + 1], mx[:, q:q + 1], -1.0, None, ALU.mult).then_inc(sg("logits_max_ready"), 1)

            def invert_sums(i, k):
                dve.wait_ge(sg("exp_ready"), i * 8 + (4 * k + 4))
                V.reciprocal(rinv[:, :], rsum[:, :]).then_inc(sg("sums_inverted"), 1)

            def side(i, at):
                if at == 1:
                    dve.wait_ge(sg("side_landed"), i * 144 + 144)
                    then(shift(ks[:, :], kin, pc("mu", i + 8)))
                    then(V.tensor_scalar(kkr[:, :], ks[:, :], pc("k_k", i), None, ALU.mult))
                    V.tensor_tensor(t1[:, :], kkr[:, :], kkr[:, :], ALU.mult).then_inc(sg("k_squares_ready"), 1)
                if at == 2:
                    dve.wait_ge(sg("head_sums_done"), i + 1)
                    sums, means = (x[:, 0:24].rearrange("p (q n) -> p q n", q=4) for x in (bank[5], hs))
                    V.tensor_scalar(means[:, :, 0:2], sums[:, :, 0:2], 1e-24, None, ALU.max, ALU.bypass)
                    V.tensor_scalar(means[:, :, 2:6], sums[:, :, 2:6], 1.0 / HD, EPS, ALU.mult, ALU.add).then_inc(sg("head_means_ready"), 1)
                    then(shift(rs[:, :], rin, pc("mu", i)))
                    dve.wait_ge(sg("head_roots_ready"), i + 1)
                    V.reciprocal(hr[:, 0:24], hr[:, 0:24]).then_inc(sg("head_inverse_ready"), 1)
                if at == 3:
                    dve.wait_ge(sg("sigmoids_ready"), i * 2 + 2)
                    then(V.tensor_scalar(lw[:, :], lw[:, :], -float(np.exp(-0.5)), None, ALU.mult))
                    then(V.tensor_tensor_scan(cum[:, :], reset[:, :], lw[:, :], 0.0, ALU.mult, ALU.add))
                    V.tensor_tensor(cex[:, :], cum[:, :], lw[:, :], ALU.subtract).then_inc(sg("cum_ready"), 1)
                    dve.wait_ge(sg("features_stored"), i * 48 + 48)
                    then(shift(vs[:, :], vin, pc("mu", i + 16)))
                if at == 4:
                    dve.wait_ge(sg("head_spread"), i + 1)
                    V.tensor_tensor(kk[:, :], kkr[:, :], bank[2][:, :], ALU.mult).then_inc(sg("qk_ready"), 1)
                    V.scalar_tensor_tensor(qh[:, :], qin[:, :], qs[:, :], bank[3][:, :], ALU.mult, ALU.mult).then_inc(sg("qk_ready"), 1)
                    V.scalar_tensor_tensor(kh[:, :], k_in[:, :], par[:, 121:122], bank[4][:, :], ALU.mult, ALU.mult).then_inc(sg("qk_ready"), 1)
                    then(V.tensor_scalar(t1[:, :], av[:, :], -1.0, pc("k_a", i), ALU.add, ALU.mult))
                    then(V.scalar_tensor_tensor(km[:, :], t1[:, :], 1.0, ks[:, :], ALU.add, ALU.mult))
                    then(V.tensor_tensor(t1[:, :], rs[:, :], km[:, :], ALU.mult))
                    V.tensor_scalar(t2[:, :], t1[:, :], pc("r_k", i), None, ALU.mult).then_inc(sg("rk_ready"), 1)
                if at == 5:
                    logits(i, 0)
                    invert_sums(i, 0)
                if at == 6:
                    dve.wait_ge(sg("exps_ready"), i * 3 + 3)
                    V.tensor_tensor(ab[:, :, 1, :], by_chunk(rs), by_chunk(e_in), ALU.mult)
                    dve.wait_ge(sg("qk_ready"), i * 3 + 1)
                    V.scalar_tensor_tensor(ab[:, :, 0, :], by_chunk(kk), -1.0, by_chunk(e_ex), ALU.mult, ALU.mult)
                if at == 7:
                    dve.wait_ge(sg("bonus_summed"), i + 1)
                    V.scalar_tensor_tensor(bon[:, :], bank[1][:, :], float(HD), vs[:, :], ALU.mult, ALU.mult).then_inc(sg("bonus_taken"), 1)
                    then(V.tensor_tensor(t2[:, :], kk[:, :], av[:, :], ALU.mult))
                    V.tensor_tensor(ab[:, :, 2, :], by_chunk(t2), by_chunk(e_no), ALU.mult)
                    V.tensor_tensor(ab[:, :, 3, :], by_chunk(km), by_chunk(e_no), ALU.mult).then_inc(sg("features_made"), 1)
                if at == 8:
                    logits(i, 1)
                    invert_sums(i, 1)
                    dve.wait_ge(sg("logits_max_ready"), i * 8 + 8)
                    dve.sem_inc(sg("side_inputs_used"), 1)

            pair_tiles(0, 2, once)
            with dve.Fori(0, NPAIR - 1) as i:
                end = chained(i, 37)
                pair_tiles(i, 2 + Z_PAIR, side)
            unchained(NPAIR - 1, end)
            for at in range(1, 13):
                side(NPAIR - 1, at)

            dve.sem_inc(sg("state_ready"), 2)
            dve.sem_inc(sg("state_bd_ready_b"), 2)

            def chunk(j, b):
                def wait(name, g, n, k):
                    dve.wait_ge(sg(name), j * (4 * n) + (2 * (b * n + k) - 1 + g))

                hi = slice(HD, P)

                def masked(g, dst, k):
                    wait("products_done", g, 2, k + 1)
                    V.tensor_tensor(dst[:, pairs[g], :, :].rearrange("p n a t -> p n (a t)"), m3(gbank[g][k][:, :], H),
                                    const(C_MASK, P)[:, None, :].broadcast_to([P, H, P]), ALU.mult).then_inc(sg("products_ready"), 1)

                for g in range(2):
                    masked(g, gb, 0)
                    wait("products_ready", g, 2, 1)
                    then(V.tensor_tensor(xs[:, pairs[g], :], gb[:, pairs[g], 0, :], const(C_LVL, C)[:, None, :].broadcast_to([P, H, C]), ALU.mult))
                    V.tensor_tensor(xs[:, pairs[g], :], xs[:, pairs[g], :], eye2[:, None, :].broadcast_to([P, H, C]), ALU.add).then_inc(sg("x_ready"), 1)
                for g in range(2):
                    masked(g, gk, 1)
                for g in range(2):
                    wait("xt0_done", g, 1, 1)
                    V.tensor_copy(xt[:, pairs[g], :], half(g, 1)).then_inc(sg("xt_ready"), 1)
                for lv in range(1, 6):
                    for g in range(2):
                        wait("pt_done", g, 5, lv)
                        V.tensor_copy(ptbd[hi, pairs[g], 1, :], half(g, 1, hi))
                        V.tensor_copy(pt[hi, pairs[g], :], half(g, 1, hi)).then_inc(sg("pt_ready_b"), 1)
                    for g in range(2):
                        wait("dx_done", g, 5, lv)
                        wait("x_bd_ready", g, 6, lv)
                        wait("x_ready", g, 6, lv)
                        V.tensor_tensor(xs[:, pairs[g], :], xs[:, pairs[g], :], half(g, 2), ALU.add).then_inc(sg("x_ready"), 1)
                    if lv < 5:
                        for g in range(2):
                            wait("dxt_done", g, 4, lv)
                            wait("xt_ready", g, 5, lv)
                            V.tensor_tensor(xt[:, pairs[g], :], xt[:, pairs[g], :], half(g, 3), ALU.add).then_inc(sg("xt_ready"), 1)
                for g in range(2):
                    wait("r_done", g, 1, 1)
                    V.tensor_copy(rr[:, pairs[g], :], half(g, 0)).then_inc(sg("r_ready"), 1)
                for g in range(2):
                    wait("sa_done", g, 1, 1)
                    V.tensor_copy(sabd[hi, pairs[g], 1, :], half(g, 1, hi))
                    V.tensor_copy(sa[hi, pairs[g], :], half(g, 1, hi)).then_inc(sg("sa_ready_b"), 1)
                for g in range(2):
                    wait("s_done", g, 1, 1)
                    then(V.tensor_tensor(sn[:, pairs[g], :], st[:, pairs[g], :], half(g, 2), ALU.add))
                    wait("state_bd_ready_a", g, 1, 1)
                    V.tensor_tensor(st[:, pairs[g], :], sn[:, pairs[g], :], ec[:, pairs[g], bass.ds(j * 2 + b, 1)].broadcast_to([P, H, C]),
                                    ALU.mult).then_inc(sg("state_ready"), 1)
                for g in range(2):
                    wait("y_multiplied", g, 1, 2)
                    wait("state_ready", g, 1, 2)
                    V.tensor_copy(stbd[hi, pairs[g], 1, :], st[hi, pairs[g], :]).then_inc(sg("state_bd_ready_b"), 1)

            dve.wait_ge(sg("diagonals_cleared"), N_CLEAR)
            dve.wait_ge(sg("fox_stored"), 16 * NPAIR + 16)
            with dve.Fori(0, NC // 2) as j:
                end = chained(j, 8)
                for b in range(2):
                    chunk(j, b)
            unchained(NC // 2, end)
            dve.wait_ge(sg("state_bd_ready_b"), 2 * NC + 2)

            for i in range(NPAIR // NB):
                for n in range(NB):
                    y = y_all[:, NB * i + n, :]
                    dve.wait_ge(sg("mean_done"), NB * i + n + 1)
                    V.tensor_tensor(y, y, bank[n][:, :], ALU.subtract).then_inc(sg("y_centred"), 1)
                dve.wait_ge(sg("head_sums_done"), NPAIR + i + 1)
                V.tensor_scalar(hs[:, :], bank[5][:, 0:32], 1.0 / HD, GN_EPS, ALU.mult, ALU.add).then_inc(sg("head_means_ready"), 1)
                dve.wait_ge(sg("head_roots_ready"), NPAIR + i + 1)
                V.reciprocal(hr[:, :], hr[:, :]).then_inc(sg("head_inverse_ready"), 1)
                def finish(k):
                    y = y_all[:, NB * i + k, :]
                    dve.wait_ge(sg("y_affine"), NB * i + k + 1)
                    then(V.tensor_tensor(y, y, yb[:, NB * i + k, :], ALU.add))
                    dve.wait_ge(sg("gates_done"), NB * i + k + 1)
                    V.tensor_tensor(y, y, gate_banks[k][:, :], ALU.mult).then_inc(sg("y_finished"), 1)

                def split(k):
                    dve.wait_ge(sg("operand_hi_ready"), KT + 2 * NB * i + min(2 * k + 3, 2 * NB))
                    V.tensor_tensor(a_lo[:, NB * i + k, :], y_all[:, NB * i + k, :], a_hi[:, NB * i + k, :].bitcast(F32),
                                    ALU.subtract).then_inc(sg("operand_split"), 1)

                for n in range(NB):
                    y = y_all[:, NB * i + n, :]
                    dve.wait_ge(sg("y_centred"), NB * i + n + 1)
                    dve.wait_ge(sg("head_spread"), NPAIR + NB * i + n + 1)
                    V.tensor_tensor(y, y, bank[n][:, :], ALU.mult).then_inc(sg("y_scaled"), 1)
                    if n > 0:
                        finish(n - 1)
                    if n > 1:
                        split(n - 2)
                finish(NB - 1)
                split(NB - 2)
                split(NB - 1)

            def grow(i, b):
                V.tensor_tensor(h[:, bass.ds(2 * i + b, 1), :], h[:, bass.ds(2 * i + b, 1), :], acc[b][:, :].rearrange("p (a t) -> p a t", a=1),
                                ALU.add).then_inc(sg("acc_taken"), 1)

            def grown(hi, lo, gain, n_h, n_op, n_acc):
                def body(i, b):
                    grow(i, b)
                    dve.wait_ge(sg("acc_taken"), 2 * i + (n_acc + b + 3))
                    dve.sem_inc(sg("h_ready"), 1)
                    fold(hi, lo, gain, 2 * i + b, 2 * i + (b + n_op))
                return body

            dve.wait_ge(sg("h_landed"), 64)
            stage(M_OUT, KT, body=grown(b_hi, b_lo, "norm_mlp", KT, 2 * KT, M_OUT))

            def hidden(g):
                def body(i, b):
                    V.scalar_tensor_tensor(ev[:, b, :], acc[b][:, :], 0.0, rstd[:, :], ALU.max, ALU.mult).then_inc(sg("acc_taken"), 1)
                    dve.wait_ge(sg("acc_taken"), 2 * i + g * (2 * KT) + (M_FF + b + 3))
                    V.tensor_tensor(sq[:, b, :], ev[:, b, :], ev[:, b, :], ALU.mult).then_inc(sg("relu_squared"), 1)
                    dve.wait_ge(sg("operand_hi_ready"), 2 * i + g * KT + (b + 3 * KT + 1))
                    V.tensor_tensor(a_lo[:, bass.ds(2 * i + b, 1), :], sq[:, b:b + 1, :], a_hi[:, bass.ds(2 * i + b, 1), :].bitcast(F32),
                                    ALU.subtract).then_inc(sg("operand_split"), 1)
                return body

            stage(M_FF, 2, body=hidden(0), early=lambda: mean_square(1), between=lambda: invert_root(1))
            stage(M_FF + 2, KT - 2, body=lambda i, b: hidden(0)(i + 1, b))
            stage(M_FF + KT, KT, body=grow)
            with dve.Fori(0, FG - 2) as g:
                stage(M_FF + 2 * KT, KT, outer=g * (2 * KT), body=hidden(g + 1))
                stage(M_FF + 3 * KT, KT, outer=g * (2 * KT), body=grow)
            stage(M_GATE - 2 * KT, KT, body=hidden(FG - 1))
            stage(M_GATE - KT, KT, body=grown(b_hi, b_lo, "norm_ple", 2 * KT, 7 * KT, M_GATE - KT))

            def split_p():
                dve.wait_ge(sg("p_hi_ready"), 1)
                V.tensor_tensor(p_lo[:, :, :], p_t[:, :, :], p_hi[:, :, :].bitcast(F32), ALU.subtract).then_inc(sg("p_split"), 1)
                invert_root(2)

            def ple_unit(n, b):
                dve.wait_ge(sg("ple_hi_ready"), n + 1)
                V.tensor_tensor(pw_lo[:, b, :, :], pw[:, b, :, :], pw_hi[:, b, :, :].bitcast(F32), ALU.subtract).then_inc(sg("ple_split"), 1)

            def gated(i, b):
                n = 2 * i + b
                dve.wait_ge(sg("unit_done"), i * 4 + (2 + Z_ODD + 2 * (M_GATE + b + 1)))
                V.tensor_tensor(ev[:, b, :], acc[b][:, :], rstd[:, :], ALU.mult).then_inc(sg("acc_taken"), 1)
                dve.wait_ge(sg("acc_taken"), 2 * i + (M_GATE + b + 3))
                dve.sem_inc(sg("gate_scaled"), 1)
                dve.wait_ge(sg("gate_ready"), n + 1)
                dve.wait_ge(sg("ple_done"), n + 3)
                V.tensor_tensor(gt[:, b, :], gt[:, b, :], bank[b][:, :], ALU.mult).then_inc(sg("ple_taken"), 1)
                dve.wait_ge(sg("ple_taken"), n + 3)
                V.tensor_tensor(h[:, bass.ds(n, 1), :], h[:, bass.ds(n, 1), :], gt[:, b:b + 1, :], ALU.add).then_inc(sg("h_ready"), 1)

            ple_unit(0, 0)
            next_units(0, M_GATE, early=lambda: mean_square(2), between=split_p)
            gated(0, 0)
            ple_unit(1, 1)
            next_units(0, M_GATE + 1)
            gated(0, 1)
            with dve.Fori(0, KT // 2 - 2) as i:
                for b in range(2):
                    ple_unit(2 * i + (b + 2), b)
                    next_units(i, M_GATE + 2 + b)
                    gated(i + 1, b)
            i = KT // 2 - 1
            ple_unit(2 * i, 0)
            next_units(i, M_GATE)
            gated(i, 0)
            ple_unit(2 * i + 1, 1)
            gated(i, 1)
            dve.wait_ge(sg("h_ready"), 4 * KT)
            invert_rms(3)
            with dve.Fori(0, KT // 4) as i:
                for b in range(4):
                    dve.wait_ge(sg("final_transposed"), 4 * i + b + 1)
                    V.scalar_tensor_tensor(hn[:, b:b + 1, :], h[:, bass.ds(4 * i + b, 1), :], pc("norm_final", 4 * i + b),
                                           rstd[:, None, :], ALU.mult, ALU.mult).then_inc(sg("final_ready"), 1)

        @block.gpsimd
        def _(pool):
            G = nc.gpsimd
            pool.sem_inc(sg("squares_summed"), 2)
            G.memset(prow[:, :, :], 0.0).then_inc(sg("rows_cleared"), 1)

            def sums(n):
                if n:
                    pool.wait_ge(sg("sumsq_spread"), n)
                G.memset(sumsq[:, :], 0.0).then_inc(sg("sumsq_cleared"), 1)
                pool.wait_ge(sg("sumsq_cleared"), n + 1)
                with pool.Fori(0, KT // 2) as i:
                    for b in range(2):
                        pool.wait_ge(sg("squares_ready"), 2 * i + (n * KT + b + 1))
                        G.tensor_tensor(sumsq[:, :], sumsq[:, :], sq[:, b, :], ALU.add).then_inc(sg("squares_summed"), 1)
                        pool.wait_ge(sg("squares_summed"), 2 * i + (n * KT + b + 3))

            sums(0)
            pool.wait_ge(sg("h_ready"), KT)
            for k in range(4):
                pool.dma_start(h_v[:, 4 * k:4 * k + 4, :], h[:, 4 * k:4 * k + 4, :]).then_inc(sg("h_stored"), 16)
            pool.wait_ge(sg("odd_ready"), 1)
            for b, r in enumerate((slice(0, 32), slice(32, 48))):
                pool.dma_start(zo_d[r, :], ev[r, 0, :]).then_inc(sg(f"ev_free{b}"), 16)
            pool.wait_ge(sg("operand_split"), KT)
            pool.wait_ge(sg("h_stored"), 64)
            for t in (kin, rin, vin, xin_wa, xin_g, xin_h):
                G.memset(t[:, 0:1], 0.0).then_inc(sg("first_columns_zero"), 1)
            with pool.Fori(0, Z_TILES // 2) as i:
                for b in range(2):
                    pool.wait_ge(sg("acc_taken"), 2 * i + (b + 3))
                    pool.dma_start(z_d[bass.ds(2 * i + b, 1), :, :].rearrange("a p t -> (a p) t"), ev[:, b, :]).then_inc(sg(f"ev_free{b}"), 16)

            pool.wait_ge(sg("unit_done"), 2 + Z_ODD + 2 * Z_TILES)
            for n, t in enumerate(diagonals):
                if n == N_CLEAR - 2:
                    pool.wait_ge(sg("features_made"), NPAIR)
                G.memset(t, 0.0).then_inc(sg("diagonals_cleared"), 1)
            pool.wait_ge(sg("diagonals_cleared"), N_CLEAR)
            halves = ((slice(0, 64), 0), (slice(64, 128), 1))

            def chunk(j, b):
                def wait(name, g, n, k):
                    pool.wait_ge(sg(name), j * (4 * n) + (2 * (b * n + k) - 1 + g))

                def level(lv):
                    for g in range(2):
                        if lv > 2:
                            wait("pt_done", g, 5, lv - 2)
                        else:
                            wait("products_ready", g, 2, 1)
                        for ph, a in halves:
                            last = G.tensor_tensor(nbd[ph, lv % 2, pairs[g], a, :], gb[ph, pairs[g], 0, :],
                                                   const(C_LVL + lv * C, C, ph)[:, None, :].broadcast_to([64, H, C]), ALU.mult)
                        last.then_inc(sg("n_ready"), 1)

                level(1)
                level(2)
                for g in range(2):
                    wait("products_ready", g, 2, 2)
                    pool.sem_inc(sg("pool_waits_taken"), 1)
                    for ph, a in halves:
                        last = G.tensor_copy(mbd[ph, pairs[g], a, :], gk[ph, pairs[g], 0, :])
                    last.then_inc(sg("m_ready"), 1)
                level(3)
                level(4)
                for g in range(2):
                    wait("transposes_taken", g, 3, 3)
                    pool.sem_inc(sg("pool_waits_taken"), 1)
                    for ph, a in halves:
                        last = G.tensor_copy(vst[ph, pairs[g], :], vt[ph, pairs[g], a * C:(a + 1) * C])
                    last.then_inc(sg("v_stacked"), 1)
                level(5)

            with pool.Fori(0, NC // 2) as j:
                for b in range(2):
                    chunk(j, b)

            for i in range(NPAIR // NB):
                for n in range(NB):
                    k = NB * i + n
                    pool.wait_ge(sg("operand_hi_ready"), KT + 2 * NB * i + max(2 * n, 1))
                    G.tensor_tensor(a_lo[:, NPAIR + k, :], yf[:, k, :], a_hi[:, NPAIR + k, :].bitcast(F32), ALU.subtract).then_inc(sg("operand_split"), 1)
            pool.wait_ge(sg("operand_split"), 2 * KT)

            pool.wait_ge(sg("n_ready"), 10 * NC)
            for n in (1, 2, 3):
                sums(n)


    ctx.close()


_INS = ["x", "p", "norm_mix", "w_in", "mu_shift", "w0", "w2", "a0", "a2", "g2", "k_k", "k_a", "r_k", "gn_w", "gn_b",
        "b_f", "q_norm", "k_norm", "w_out", "norm_mlp", "w_ff1", "w_ff2", "norm_ple", "w_ple_gate", "w_ple_proj",
        "norm_final"]


def kernel(**inputs):
    import concourse.bacc as bacc
    from concourse.bass_utils import run_bass_kernel_spmd

    nc = bacc.Bacc("TRN2", target_bir_lowering=False, num_devices=1)
    arrays, args = {}, []
    for name in _INS + ["consts"]:
        a = constants() if name == "consts" else np.ascontiguousarray(inputs[name])
        arrays[f"in_{name}"] = a
        args.append(nc.dram_tensor(f"in_{name}", a.shape, mybir.dt.from_np(a.dtype), kind="ExternalInput").ap())
    args.append(nc.dram_tensor("out", (1, T, D), F32, kind="ExternalOutput").ap())
    build(nc, *args)
    r = run_bass_kernel_spmd(nc, [arrays], core_ids=[0])
    return r.results[0]["out"]
```
